# Optimizing a Trainium2 kernel written in Bass

```python
import jax, jax.numpy as jnp
from jax import lax
import numpy as np

D_MODEL = 1024
BATCH = 1
SEQ = 512
DEPTH = 1

N_MEM = 256
XATTN_HEADS = 4
XATTN_HEAD_DIM = D_MODEL // XATTN_HEADS
D_FF = 2816
GLA_HEADS = 4
GLA_DK = 64
GLA_DV = 128
GLA_KEY_W = GLA_HEADS * GLA_DK
GLA_VAL_W = GLA_HEADS * GLA_DV
GATE_RANK = 16
GATE_TAU = 16.0
CHUNK = 64
CONV_W = 512
CONV_K = 3
D_MIX = GLA_VAL_W + CONV_W
EPS = 1e-6
IN_SPLITS = (GLA_KEY_W, GLA_KEY_W, GLA_VAL_W, GLA_VAL_W, GATE_RANK, GATE_RANK,
             CONV_W, CONV_W, CONV_W)
D_IN = sum(IN_SPLITS)


def rms_norm(x, g):
    xf = x.astype(jnp.float32)
    y = xf * lax.rsqrt(jnp.mean(xf * xf, axis=-1, keepdims=True) + EPS)
    return (y * g.astype(jnp.float32)).astype(x.dtype)

def swiglu(h, w_gate, w_up, w_down):
    return (jax.nn.silu(h @ w_gate) * (h @ w_up)) @ w_down

def gla_chunked(q, k, v, g):
    b_, h_, s_, dk = q.shape
    dv = v.shape[-1]
    n = s_ // CHUNK
    q = q.reshape(b_, h_, n, CHUNK, dk)
    k = k.reshape(b_, h_, n, CHUNK, dk)
    v = v.reshape(b_, h_, n, CHUNK, dv)
    bcum = jnp.cumsum(g.reshape(b_, h_, n, CHUNK, dk), axis=3)
    b_last = bcum[:, :, :, -1:, :]
    q_in = q * jnp.exp(bcum)
    k_in = k * jnp.exp(-bcum)
    mask = jnp.tril(jnp.ones((CHUNK, CHUNK), dtype=bool))
    att = jnp.einsum('bhncd,bhnmd->bhncm', q_in, k_in)
    att = jnp.where(mask, att, 0.0)
    o_intra = jnp.einsum('bhncm,bhnmv->bhncv', att, v)
    k_st = k * jnp.exp(b_last - bcum)
    d_state = jnp.einsum('bhncd,bhncv->bhndv', k_st, v)
    decay = jnp.exp(b_last[:, :, :, 0, :])

    def step(state, inp):
        dec, ds = inp
        return dec[..., None] * state + ds, state

    init = jnp.zeros((b_, h_, dk, dv), jnp.float32)
    _, states = lax.scan(step, init, (jnp.moveaxis(decay, 2, 0), jnp.moveaxis(d_state, 2, 0)))
    states = jnp.moveaxis(states, 0, 2)
    o_inter = jnp.einsum('bhncd,bhndv->bhncv', q_in, states)
    return (o_intra + o_inter).reshape(b_, h_, s_, dv)

def low_rank_log_gate(z, w2, b2):
    zf = z.astype(jnp.float32) @ w2.astype(jnp.float32) + b2.astype(jnp.float32)
    lg = jax.nn.log_sigmoid(zf) / GATE_TAU
    bsz, s_ = z.shape[0], z.shape[1]
    return lg.reshape(bsz, s_, GLA_HEADS, GLA_DK).transpose(0, 2, 1, 3)

def to_heads(t, nh):
    bsz, s_, w = t.shape
    return t.reshape(bsz, s_, nh, w // nh).transpose(0, 2, 1, 3)

def token_mixing(h, w_in, gf_w, gf_b, gb_w, gb_b, gla_norm, conv_w, conv_b, w_out):
    bsz, s_, _ = h.shape
    proj = h @ w_in
    idx = np.cumsum(IN_SPLITS)[:-1].tolist()
    q, k, v, r, zf, zb, bg, cg, xv = jnp.split(proj, idx, axis=-1)
    qh = to_heads(q, GLA_HEADS).astype(jnp.float32) * (GLA_DK ** -0.5)
    kh = to_heads(k, GLA_HEADS).astype(jnp.float32)
    vh = to_heads(v, GLA_HEADS).astype(jnp.float32)
    g_fwd = low_rank_log_gate(zf, gf_w, gf_b)
    g_bwd = low_rank_log_gate(zb, gb_w, gb_b)
    o_fwd = gla_chunked(qh, kh, vh, g_fwd)
    flip = lambda t: jnp.flip(t, axis=2)
    o_bwd = flip(gla_chunked(flip(qh), flip(kh), flip(vh), flip(g_bwd)))
    o = o_fwd + o_bwd
    o = o * lax.rsqrt(jnp.mean(o * o, axis=-1, keepdims=True) + EPS)
    o = o * gla_norm.astype(jnp.float32).reshape(GLA_HEADS, 1, GLA_DV)
    o = o.transpose(0, 2, 1, 3).reshape(bsz, s_, GLA_VAL_W).astype(h.dtype)
    a_out = o * jax.nn.silu(r)
    u = cg * xv
    u_prev = jnp.pad(u[:, :-1], ((0, 0), (1, 0), (0, 0)))
    u_next = jnp.pad(u[:, 1:], ((0, 0), (0, 1), (0, 0)))
    conv = conv_w[0] * u_prev + conv_w[1] * u + conv_w[2] * u_next + conv_b
    c_out = bg * conv
    return jnp.concatenate([a_out, c_out], axis=-1) @ w_out

def memory_cross_attention(h, m, w_q, w_kv, w_o):
    q = to_heads(h @ w_q, XATTN_HEADS)
    kv = m @ w_kv
    k, v = jnp.split(kv, 2, axis=-1)
    k = to_heads(k, XATTN_HEADS)
    v = to_heads(v, XATTN_HEADS)
    s = jnp.einsum('bhsd,bhmd->bhsm', q.astype(jnp.float32), k.astype(jnp.float32))
    p = jax.nn.softmax(s * (XATTN_HEAD_DIM ** -0.5), axis=-1)
    o = jnp.einsum('bhsm,bhmd->bhsd', p, v.astype(jnp.float32)).astype(h.dtype)
    bsz, _, s_, _ = o.shape
    o = o.transpose(0, 2, 1, 3).reshape(bsz, s_, D_MODEL)
    return o @ w_o

def first_inputs(seed: int = 0) -> dict:
    key = jax.random.key(seed)
    ks = iter(jax.random.split(key, 40))

    def dense(shape, fan_in):
        return jax.random.normal(next(ks), shape, jnp.float32) * (fan_in ** -0.5)

    def gain(shape):
        return 1.0 + 0.02 * jax.random.normal(next(ks), shape, jnp.float32)

    def small(shape, scale=0.02, offset=0.0):
        return offset + scale * jax.random.normal(next(ks), shape, jnp.float32)

    L = DEPTH
    return {
        "x": jax.random.normal(next(ks), (BATCH, SEQ, D_MODEL), jnp.float32),
        "mem": jax.random.normal(next(ks), (BATCH, N_MEM, D_MODEL), jnp.float32),
        "ffn1_norm": gain((L, D_MODEL)),
        "ffn1_w_gate": dense((L, D_MODEL, D_FF), D_MODEL),
        "ffn1_w_up": dense((L, D_MODEL, D_FF), D_MODEL),
        "ffn1_w_down": dense((L, D_FF, D_MODEL), D_FF),
        "mix_norm": gain((L, D_MODEL)),
        "w_in": dense((L, D_MODEL, D_IN), D_MODEL),
        "gate_fwd_w": dense((L, GATE_RANK, GLA_KEY_W), GATE_RANK),
        "gate_fwd_b": small((L, GLA_KEY_W), 0.5, 1.0),
        "gate_bwd_w": dense((L, GATE_RANK, GLA_KEY_W), GATE_RANK),
        "gate_bwd_b": small((L, GLA_KEY_W), 0.5, 1.0),
        "gla_norm": gain((L, GLA_VAL_W)),
        "conv_w": dense((L, CONV_K, CONV_W), CONV_K),
        "conv_b": small((L, CONV_W)),
        "w_out": dense((L, D_MIX, D_MODEL), D_MIX),
        "xattn_norm": gain((L, D_MODEL)),
        "mem_norm": gain((L, D_MODEL)),
        "xattn_w_q": dense((L, D_MODEL, D_MODEL), D_MODEL),
        "xattn_w_kv": dense((L, D_MODEL, 2 * D_MODEL), D_MODEL),
        "xattn_w_o": dense((L, D_MODEL, D_MODEL), D_MODEL),
        "ffn2_norm": gain((L, D_MODEL)),
        "ffn2_w_gate": dense((L, D_MODEL, D_FF), D_MODEL),
        "ffn2_w_up": dense((L, D_MODEL, D_FF), D_MODEL),
        "ffn2_w_down": dense((L, D_FF, D_MODEL), D_FF),
        "final_norm": gain((D_MODEL,)),
    }

def first_block(x, mem, ffn1_norm, ffn1_w_gate, ffn1_w_up, ffn1_w_down, mix_norm, w_in,
              gate_fwd_w, gate_fwd_b, gate_bwd_w, gate_bwd_b, gla_norm, conv_w, conv_b,
              w_out, xattn_norm, mem_norm, xattn_w_q, xattn_w_kv, xattn_w_o,
              ffn2_norm, ffn2_w_gate, ffn2_w_up, ffn2_w_down, final_norm):
    for l in range(DEPTH):
        x = x + 0.5 * swiglu(rms_norm(x, ffn1_norm[l]), ffn1_w_gate[l], ffn1_w_up[l], ffn1_w_down[l])
        x = x + token_mixing(rms_norm(x, mix_norm[l]), w_in[l], gate_fwd_w[l], gate_fwd_b[l],
                             gate_bwd_w[l], gate_bwd_b[l], gla_norm[l], conv_w[l], conv_b[l], w_out[l])
        x = x + memory_cross_attention(rms_norm(x, xattn_norm[l]), rms_norm(mem, mem_norm[l]),
                                       xattn_w_q[l], xattn_w_kv[l], xattn_w_o[l])
        x = x + 0.5 * swiglu(rms_norm(x, ffn2_norm[l]), ffn2_w_gate[l], ffn2_w_up[l], ffn2_w_down[l])
    return rms_norm(x, final_norm)


DEPTH_2 = 2

N_MIXERS = 2
N_META = 16
N_HEADS = 16
QK_NOPE_DIM = 64
QK_ROPE_DIM = 32
QK_HEAD_DIM = QK_NOPE_DIM + QK_ROPE_DIM
V_HEAD_DIM = 64
Q_LORA_RANK = 384
KV_LORA_RANK = 256
ROPE_THETA = 10000.0
Q_BLOCK = 128
POOL_WINDOWS = (2, 4, 8, 16)
N_POOL_GROUPS = len(POOL_WINDOWS)
POOL_GROUP_DIM = D_MODEL // N_POOL_GROUPS
CONV_WIDTH = 3
NORM_EPS = 1e-6
N_MLA_LAYERS = len(range(0, DEPTH_2, N_MIXERS))
N_POOL_LAYERS = DEPTH_2 - N_MLA_LAYERS


def rmsnorm(x, g):
    xf = x.astype(jnp.float32)
    y = xf * lax.rsqrt(jnp.mean(xf * xf, axis=-1, keepdims=True) + NORM_EPS)
    return (y * g.astype(jnp.float32)).astype(x.dtype)

def rope_tables(length):
    inv = 1.0 / (ROPE_THETA ** (jnp.arange(0, QK_ROPE_DIM, 2, dtype=jnp.float32) / QK_ROPE_DIM))
    ang = jnp.arange(length, dtype=jnp.float32)[:, None] * inv[None, :]
    return jnp.cos(ang), jnp.sin(ang)

def apply_rope(x, cos, sin):
    xf = x.astype(jnp.float32)
    x1, x2 = jnp.split(xf, 2, axis=-1)
    c = cos[None, :, None, :]
    s = sin[None, :, None, :]
    return jnp.concatenate([x1 * c - x2 * s, x2 * c + x1 * s], axis=-1).astype(x.dtype)

def mla_mixer(h, w_dqkv, q_norm, w_uq, kv_norm, w_ukv, w_o, cos, sin):
    B, L, _ = h.shape
    a = h @ w_dqkv
    c_q, c_kv, k_rope = jnp.split(a, [Q_LORA_RANK, Q_LORA_RANK + KV_LORA_RANK], axis=-1)
    c_q = rmsnorm(c_q, q_norm)
    c_kv = rmsnorm(c_kv, kv_norm)
    q = (c_q @ w_uq).reshape(B, L, N_HEADS, QK_HEAD_DIM)
    q = jnp.concatenate([q[..., :QK_NOPE_DIM], apply_rope(q[..., QK_NOPE_DIM:], cos, sin)], axis=-1)
    kv = (c_kv @ w_ukv).reshape(B, L, N_HEADS, QK_NOPE_DIM + V_HEAD_DIM)
    k_nope, v = jnp.split(kv, [QK_NOPE_DIM], axis=-1)
    k_rope = apply_rope(k_rope[:, :, None, :], cos, sin)
    k = jnp.concatenate([k_nope, jnp.broadcast_to(k_rope, (B, L, N_HEADS, QK_ROPE_DIM))], axis=-1)
    scale = QK_HEAD_DIM ** -0.5
    outs = []
    for start in range(0, L, Q_BLOCK):
        end = start + Q_BLOCK
        qb = q[:, start:end]
        kb = k[:, :end]
        vb = v[:, :end]
        s = jnp.einsum('bqhd,bkhd->bhqk', qb, kb).astype(jnp.float32) * scale
        mask = jnp.arange(start, end)[:, None] >= jnp.arange(end)[None, :]
        s = jnp.where(mask[None, None], s, -jnp.inf)
        p = jax.nn.softmax(s, axis=-1).astype(vb.dtype)
        outs.append(jnp.einsum('bhqk,bkhd->bqhd', p, vb))
    o = jnp.concatenate(outs, axis=1).reshape(B, L, N_HEADS * V_HEAD_DIM)
    return o @ w_o

def pool_mixer(h, w_group, scale):
    B, L, D = h.shape
    hf = h.astype(jnp.float32).reshape(B, L, N_POOL_GROUPS, POOL_GROUP_DIM)
    csum = jnp.cumsum(hf, axis=1)
    t = jnp.arange(1, L + 1, dtype=jnp.float32)
    means = []
    for g, w in enumerate(POOL_WINDOWS):
        cg = csum[:, :, g, :]
        prev = jnp.pad(cg[:, :L - w], ((0, 0), (w, 0), (0, 0)))
        cnt = jnp.minimum(t, float(w))[None, :, None]
        means.append((cg - prev) / cnt)
    pooled = jnp.stack(means, axis=2)
    mixed = (pooled - hf).astype(h.dtype)
    y = jnp.einsum('blgc,gcd->blgd', mixed, w_group).reshape(B, L, D)
    return y * scale

def conv_ffn(h, w_up, conv_w, conv_b, w_down):
    L = h.shape[1]
    u = h @ w_up
    up = jnp.pad(u, ((0, 0), (CONV_WIDTH - 1, 0), (0, 0)))
    u = conv_b + sum(conv_w[j] * up[:, j:j + L] for j in range(CONV_WIDTH))
    gate, val = jnp.split(u, 2, axis=-1)
    return (jax.nn.silu(gate) * val) @ w_down

def second_inputs(seed: int = 0) -> dict:
    key = jax.random.key(seed)
    ks = jax.random.split(key, 24)
    f32 = jnp.float32

    def nrm(k, shape, fan_in):
        return jax.random.normal(k, shape, f32) * (fan_in ** -0.5)

    def gain(k, shape, s=0.05):
        return 1.0 + s * jax.random.normal(k, shape, f32)

    return {
        "x": jax.random.normal(ks[0], (BATCH, SEQ, D_MODEL), f32),
        "meta_tokens": jax.random.normal(ks[1], (N_META, D_MODEL), f32),
        "norm_mix_pre": gain(ks[2], (DEPTH_2, D_MODEL)),
        "norm_mix_post": gain(ks[3], (DEPTH_2, D_MODEL)),
        "norm_ffn_pre": gain(ks[4], (DEPTH_2, D_MODEL)),
        "norm_ffn_post": gain(ks[5], (DEPTH_2, D_MODEL)),
        "mla_w_dqkv": nrm(ks[6], (N_MLA_LAYERS, D_MODEL, Q_LORA_RANK + KV_LORA_RANK + QK_ROPE_DIM), D_MODEL),
        "mla_q_norm": gain(ks[7], (N_MLA_LAYERS, Q_LORA_RANK)),
        "mla_w_uq": nrm(ks[8], (N_MLA_LAYERS, Q_LORA_RANK, N_HEADS * QK_HEAD_DIM), Q_LORA_RANK),
        "mla_kv_norm": gain(ks[9], (N_MLA_LAYERS, KV_LORA_RANK)),
        "mla_w_ukv": nrm(ks[10], (N_MLA_LAYERS, KV_LORA_RANK, N_HEADS * (QK_NOPE_DIM + V_HEAD_DIM)), KV_LORA_RANK),
        "mla_w_o": nrm(ks[11], (N_MLA_LAYERS, N_HEADS * V_HEAD_DIM, D_MODEL), N_HEADS * V_HEAD_DIM),
        "pool_w_group": nrm(ks[12], (N_POOL_LAYERS, N_POOL_GROUPS, POOL_GROUP_DIM, POOL_GROUP_DIM), POOL_GROUP_DIM),
        "pool_scale": gain(ks[13], (N_POOL_LAYERS, D_MODEL), 0.1),
        "ffn_w_up": nrm(ks[14], (DEPTH_2, D_MODEL, 2 * D_FF), D_MODEL),
        "ffn_conv_w": nrm(ks[15], (DEPTH_2, CONV_WIDTH, 2 * D_FF), CONV_WIDTH),
        "ffn_conv_b": 0.01 * jax.random.normal(ks[16], (DEPTH_2, 2 * D_FF), f32),
        "ffn_w_down": nrm(ks[17], (DEPTH_2, D_FF, D_MODEL), D_FF),
    }

def second_block(x, meta_tokens, norm_mix_pre, norm_mix_post, norm_ffn_pre, norm_ffn_post,
              mla_w_dqkv, mla_q_norm, mla_w_uq, mla_kv_norm, mla_w_ukv, mla_w_o,
              pool_w_group, pool_scale, ffn_w_up, ffn_conv_w, ffn_conv_b, ffn_w_down):
    B, S, D = x.shape
    L = N_META + S
    L_pad = -(-L // Q_BLOCK) * Q_BLOCK
    meta = jnp.broadcast_to(meta_tokens.astype(x.dtype)[None], (B, N_META, D))
    h = jnp.concatenate([meta, x, jnp.zeros((B, L_pad - L, D), x.dtype)], axis=1)
    cos, sin = rope_tables(L_pad)
    for i in range(DEPTH_2):
        j = i // N_MIXERS
        a = rmsnorm(h, norm_mix_pre[i])
        if i % N_MIXERS == 0:
            m = mla_mixer(a, mla_w_dqkv[j], mla_q_norm[j], mla_w_uq[j], mla_kv_norm[j],
                          mla_w_ukv[j], mla_w_o[j], cos, sin)
        else:
            m = pool_mixer(a, pool_w_group[j], pool_scale[j])
        h = h + rmsnorm(m, norm_mix_post[i])
        f = conv_ffn(rmsnorm(h, norm_ffn_pre[i]), ffn_w_up[i], ffn_conv_w[i], ffn_conv_b[i], ffn_w_down[i])
        h = h + rmsnorm(f, norm_ffn_post[i])
    return h[:, N_META:L]


def setup_inputs(seed=0):
    out = dict(first_inputs(seed))
    for name, value in second_inputs(seed + 1).items():
        if name != "x":
            out[name + "_2"] = value
    return out


def reference(
    x, mem, ffn1_norm, ffn1_w_gate, ffn1_w_up, ffn1_w_down, mix_norm, w_in, gate_fwd_w,
    gate_fwd_b, gate_bwd_w, gate_bwd_b, gla_norm, conv_w, conv_b, w_out, xattn_norm, mem_norm,
    xattn_w_q, xattn_w_kv, xattn_w_o, ffn2_norm, ffn2_w_gate, ffn2_w_up, ffn2_w_down,
    final_norm, meta_tokens_2, norm_mix_pre_2, norm_mix_post_2, norm_ffn_pre_2, norm_ffn_post_2,
    mla_w_dqkv_2, mla_q_norm_2, mla_w_uq_2, mla_kv_norm_2, mla_w_ukv_2, mla_w_o_2,
    pool_w_group_2, pool_scale_2, ffn_w_up_2, ffn_conv_w_2, ffn_conv_b_2, ffn_w_down_2,
):
    x = first_block(
        x, mem, ffn1_norm, ffn1_w_gate, ffn1_w_up, ffn1_w_down, mix_norm, w_in, gate_fwd_w,
        gate_fwd_b, gate_bwd_w, gate_bwd_b, gla_norm, conv_w, conv_b, w_out, xattn_norm,
        mem_norm, xattn_w_q, xattn_w_kv, xattn_w_o, ffn2_norm, ffn2_w_gate, ffn2_w_up,
        ffn2_w_down, final_norm,
    )
    return second_block(
        x, meta_tokens_2, norm_mix_pre_2, norm_mix_post_2, norm_ffn_pre_2, norm_ffn_post_2,
        mla_w_dqkv_2, mla_q_norm_2, mla_w_uq_2, mla_kv_norm_2, mla_w_ukv_2, mla_w_o_2,
        pool_w_group_2, pool_scale_2, ffn_w_up_2, ffn_conv_w_2, ffn_conv_b_2, ffn_w_down_2,
    )


_drawn_inputs = setup_inputs


def setup_inputs(seed=0):
    import zlib

    import numpy as np

    out = dict(_drawn_inputs(seed))
    spreads = {}
    factors = {'ffn1_norm': 3.031,
     'gla_norm': 5.481,
     'conv_b': 3.444,
     'xattn_norm': 8.0,
     'mem_norm': 7.861,
     'ffn2_norm': 5.431,
     'ffn_conv_b_2': 5.291}
    for name, (base, spread) in spreads.items():
        noise = np.random.default_rng([zlib.crc32(name.encode()), seed]).standard_normal(out[name].shape)
        drawn = base * np.exp(spread * noise) if base else spread * noise
        out[name] = __import__('jax').numpy.asarray(drawn.astype(out[name].dtype))
    for name, factor in factors.items():
        out[name] = (out[name] * factor).astype(out[name].dtype)
    return out
```

```python
from contextlib import ExitStack

import numpy as np
import concourse.bass as bass
from concourse import mybir

F32 = mybir.dt.float32
F32R = mybir.dt.float32r
U32 = mybir.dt.uint32
ALU = mybir.AluOpType
ACT = mybir.ActivationFunctionType
AX = mybir.AxisListType

P = 128
D = 1024
KD = D // P
S1 = 512
META = 16
S2 = S1 + META
CW = S2 // 2
F = 2816
FT = F // P
PARTS = ((0, 8), (8, 8), (16, 6))
EPS = 1e-6
MEM = 256
XH_HEADS, XHD = 4, 256
GH, GDK, GDV, CHUNK = 4, 64, 128, 64
NCH = S1 // CHUNK
MH, NOPE, ROPE, VD = 16, 64, 32, 64
QL, KVL = 384, 256
MLA_SCALE = float((NOPE + ROPE) ** -0.5)
WINDOWS = (2, 4, 8, 16)
RAW, SPLIT = 4, 2
SLOT = 8 * P
NEG = -float(2 ** 127)

C_ID, C_ONE, C_MF, C_MB, C_NEG, C_NEGM, C_DUP, C_ROPE, C_COR, C_RST = 0, 128, 256, 384, 512, 640, 656, 784, 1312, 1376
C_END = 1888

GROUP_ROWS = (
    (("ffn1_norm", 0, 8), ("mix_norm", 0, 8), ("xattn_norm", 0, 8), ("mem_norm", 0, 8), ("ffn2_norm", 0, 8),
     ("final_norm", None, 8), ("norm_mix_pre_2", 0, 8), ("norm_mix_pre_2", 1, 8), ("norm_mix_post_2", 0, 8),
     ("norm_mix_post_2", 1, 8), ("norm_ffn_pre_2", 0, 8), ("norm_ffn_pre_2", 1, 8), ("norm_ffn_post_2", 0, 8),
     ("norm_ffn_post_2", 1, 8), ("pool_scale_2", 0, 8), ("mla_q_norm_2", 0, 3), ("mla_kv_norm_2", 0, 2)),
    (("gate_fwd_b", 0, 2), ("gate_bwd_b", 0, 2), ("gla_norm", 0, 4), ("conv_w", (0, 0), 4), ("conv_w", (0, 1), 4),
     ("conv_w", (0, 2), 4), ("conv_b", 0, 4)),
    (("ffn_conv_w_2", (0, 0), 44), ("ffn_conv_w_2", (0, 1), 44)),
    (("ffn_conv_w_2", (0, 2), 44), ("ffn_conv_b_2", 0, 44)),
    (("ffn_conv_w_2", (1, 0), 44), ("ffn_conv_w_2", (1, 1), 44)),
    (("ffn_conv_w_2", (1, 2), 44), ("ffn_conv_b_2", 1, 44)),
)


def constant_tile():
    c = np.zeros((P, C_END), np.float32)
    p = np.arange(P)[:, None]
    f = np.arange(P)[None, :]
    c[:, C_ID:C_ID + P] = p == f
    c[:, C_ONE:C_ONE + P] = 1.0
    same = (p // CHUNK) == (f // CHUNK)
    c[:, C_MF:C_MF + P] = same & (p <= f)
    c[:, C_MB:C_MB + P] = same & (p >= f)
    c[:, C_NEG:C_NEG + P] = np.where(f > p, NEG, 0.0)
    c[:, C_NEGM:C_NEGM + META] = np.where(f[:, :META] > p, NEG, 0.0)
    c[:, C_DUP:C_DUP + P] = (p >= NOPE) & (f >= NOPE) & (p % ROPE == f % ROPE)
    half = ROPE // 2
    inv = (1.0 / (np.float32(10000.0) ** (np.arange(0, ROPE, 2, dtype=np.float32) / np.float32(ROPE)))).astype(np.float32)
    ang = inv[:, None] * np.arange(S2, dtype=np.float32)[None, :]
    cos, sin = np.cos(ang).astype(np.float32), np.sin(ang).astype(np.float32)
    c[:NOPE, C_ROPE:C_ROPE + S2] = 1.0
    c[NOPE:NOPE + ROPE, C_ROPE:C_ROPE + S2] = np.concatenate([cos, cos])
    c[NOPE + ROPE:, C_ROPE:C_ROPE + S2] = np.concatenate([-sin, sin])
    for g, w in enumerate(WINDOWS):
        t = np.arange(1, 17, dtype=np.float32)
        c[:, C_COR + 16 * g:C_COR + 16 * (g + 1)] = w / np.minimum(t, w)
    c[:, C_RST:C_RST + S1] = (np.arange(S1) % CHUNK != 0)
    return c


class Signal:

    def __init__(self, sem):
        self.sem = sem
        self.order = {}
        self.done = 0

    def declare(self, *keys):
        for k in keys:
            assert k not in self.order, k
            self.order[k] = len(self.order) + 1

    def at(self, key):
        return self.order[key]

    def inc(self, ins, key):
        self.done += 1
        assert self.order[key] == self.done, (key, self.done)
        ins.then_inc(self.sem, 1)

    def wait(self, eng, key):
        eng.wait_ge(self.sem, self.order[key])


class Unit:

    def __init__(self, kt, cols, src, form=None):
        self.kt, self.cols, self.src, self.form = kt, cols, src, form
        self.raw_cols = cols // P * (NOPE + ROPE) if form == "rotary" else cols


class Loop:

    def __init__(self, count, units):
        assert len(units) == 4
        self.count, self.units = count, units


def build(nc, A, out):
    ctx = ExitStack()
    with ctx:
        program(nc, ctx, A, out)


def program(nc, ctx, A, out):
    def sb(name, shape, dt=F32, scope=ctx):
        return scope.enter_context(nc.sbuf_tensor(name, shape, dt))

    def sem(name):
        return ctx.enter_context(nc.semaphore(name))

    X = sb("X", [P, KD, S2])
    XHI = sb("XHI", [P, KD, S2], F32R)
    XLO = sb("XLO", [P, KD, S2], F32R)
    raw = sb("raw", [P, RAW, SLOT])
    w_hi = sb("w_hi", [P, SPLIT, SLOT], F32R)
    w_lo = sb("w_lo", [P, SPLIT, SLOT], F32R)
    const = sb("const", [P, C_END])
    cols = sb("cols", [P, len(GROUP_ROWS), P])
    acc = sb("acc", [P, S2])
    sq = sb("sq", [P, 2, S2])
    ms = sb("ms", [P, S2 + 8])
    rn = sb("rn", [P, S2 + 8])
    post_t = sb("post_t", [P, 2, S2 + 8])
    rt, sd = post_t[:, 0, :], post_t[:, 1, :]

    ident = const[:, C_ID:C_ID + P]
    ones = const[:, C_ONE:C_ONE + P]

    def column(name, index, tile, n=1):
        for g, group in enumerate(GROUP_ROWS):
            at = 0
            for nm, ix, rows in group:
                if nm == name and ix == index:
                    return cols[:, g, bass.ds(at + tile, n)] if not isinstance(tile, int) else cols[:, g, at + tile:at + tile + n]
                at += rows
        raise KeyError(name)

    start = ExitStack()
    rows = sb("rows", [P, len(GROUP_ROWS), P], scope=start)
    x_in = sb("x_in", [P, S1 // P, D], scope=start)
    meta_in = sb("meta_in", [META, D], scope=start)
    start.close()

    ffn_scope = ExitStack()
    M = sb("M", [P, KD, S2], scope=ffn_scope)
    h_hi = sb("h_hi", [P, 8, S2], F32R, ffn_scope)
    h_lo = sb("h_lo", [P, 8, S2], F32R, ffn_scope)
    g_buf = sb("g_buf", [P, S2 + 2], scope=ffn_scope)
    u_buf = sb("u_buf", [P, S2 + 2], scope=ffn_scope)
    g_conv = sb("g_conv", [P, S2], scope=ffn_scope)
    u_conv = sb("u_conv", [P, S2], scope=ffn_scope)
    g_act = sb("g_act", [P, S2], scope=ffn_scope)
    hid = sb("hid", [P, S2], scope=ffn_scope)
    ffn_scope.close()

    mix = ExitStack()
    q_in = sb("q_in", [P, 4, S1], scope=mix)
    k_in = sb("k_in", [P, 4, S1], scope=mix)
    kst_tok = sb("kst_tok", [P, 4, 4, P], scope=mix)
    v_tok = sb("v_tok", [P, 4, GH * GDV], scope=mix)
    cu = sb("cu", [P, 4, S1 + 2], scope=mix)
    cv = sb("cv", [P, 4, S1], scope=mix)
    r_act = sb("r_act", [P, 4, S1], scope=mix)
    gate_w = sb("gate_w", [32, 512], scope=mix)
    mtmp = sb("mtmp", [P, 2, S1], scope=mix)
    dec = sb("dec", [P, 4, NCH], scope=mix)
    tot = sb("tot", [P, 4, NCH], scope=mix)
    mix_a = ExitStack()
    zz = sb("zz", [32, S1], scope=mix_a)
    t1 = sb("t1", [P, 4, S1], scope=mix_a)
    t2 = sb("t2", [P, 4, S1], scope=mix_a)
    t3 = sb("t3", [P, 4, S1], scope=mix_a)
    qs = sb("qs", [P, 2, S1], scope=mix_a)
    ks = sb("ks", [P, 2, S1], scope=mix_a)
    mix_a.close()
    mix_c = ExitStack()
    state = sb("state", [P, 4, NCH, GDV], scope=mix_c)
    att = sb("att", [P, 2, 2, S1], scope=mix_c)
    o_gla = sb("o_gla", [P, 2, S1], scope=mix_c)
    o_sq = sb("o_sq", [P, 2, S1], scope=mix_c)
    mix_c.close()
    mix.close()

    xat = ExitStack()
    mem_in = sb("mem_in", [P, 2, D], scope=xat)
    m_hi = sb("m_hi", [P, KD, MEM], F32R, xat)
    m_lo = sb("m_lo", [P, KD, MEM], F32R, xat)
    m_acc = sb("m_acc", [P, MEM], scope=xat)
    m_sq = sb("m_sq", [P, 2, MEM], scope=xat)
    m_ms = sb("m_ms", [P, MEM + 2], scope=xat)
    m_sd = sb("m_sd", [P, MEM + 2], scope=xat)
    m_rn = sb("m_rn", [P, MEM + 2], scope=xat)
    m_rt = sb("m_rt", [P, MEM + 2], scope=xat)
    xk = sb("xk", [P, KD, MEM], scope=xat)
    xv = sb("xv", [P, 2, D], scope=xat)
    xq = sb("xq", [P, KD, S1], scope=xat)
    xp = sb("xp", [P, 3, MEM], scope=xat)
    xpt = sb("xpt", [P, 2, 2, S1], scope=xat)
    xst = sb("xst", [P, 16, 4], scope=xat)
    xat.close()

    mla = ExitStack()
    sb("M_place_mla", [P, KD, S2], scope=mla)
    cq = sb("cq", [P, 3, S2], scope=mla)
    cq_hi = sb("cq_hi", [P, 3, S2], F32R, mla)
    cq_lo = sb("cq_lo", [P, 3, S2], F32R, mla)
    ckv_hi = sb("ckv_hi", [P, 2, S2], F32R, mla)
    ckv_lo = sb("ckv_lo", [P, 2, S2], F32R, mla)
    ct = sb("ct", [P, S2], scope=mla)
    r_kv = sb("r_kv", [P, S2 + 8], scope=mla)
    q4 = sb("q4", [P, 4, S2], scope=mla)
    k4 = sb("k4", [P, 4, S2], scope=mla)
    v4 = sb("v4", [P, 2, 5, P], scope=mla)
    pr = sb("pr", [P, 2, 1360], scope=mla)
    pt = sb("pt", [P, 2, 5, P], scope=mla)
    mst = sb("mst", [P, 16, 5, 3], scope=mla)
    mla.close()

    pool_scope = ExitStack()
    sb("M_place_pool", [P, KD, S2], scope=pool_scope)
    pa = sb("pa", [P, KD, S2 + 16], scope=pool_scope)
    pb = sb("pb", [P, 2, S2 + 16], scope=pool_scope)
    pc = sb("pc", [P, 2, S2 + 16], scope=pool_scope)
    mixed = sb("mixed", [P, KD, S2], scope=pool_scope)
    pool_scope.close()

    end = ExitStack()
    sb("M_place_end", [P, KD, S2], scope=end)
    out_tok = sb("out_tok", [P, S1 // P, D], scope=end)
    end.close()

    PS = [ctx.enter_context(nc.psum_tensor(f"PS{i}", [P, 2, 512], F32)) for i in range(4)]

    raw_loaded = [sem(f"raw_loaded{s}") for s in range(RAW)]
    hi_done = sem("hi_done")
    lo_done = sem("lo_done")
    unit_summed = sem("unit_summed")
    unit_read = sem("unit_read")
    x_hi = sem("x_hi")
    x_lo = sem("x_lo")
    sq_done = sem("sq_done")
    acc_done = sem("acc_done")
    norm_sum = sem("norm_sum")
    norm_ms = sem("norm_ms")
    norm_sd = sem("norm_sd")
    silu_done = sem("silu_done")
    hid_prod = sem("hid_prod")
    hid_hi = sem("hid_hi")
    hid_lo = sem("hid_lo")
    conv_tap = sem("conv_tap")
    conv_mid = sem("conv_mid")
    conv_done = sem("conv_done")
    post_scaled = sem("post_scaled")
    post_added = sem("post_added")
    const_in = sem("const_in")
    rows_in = sem("rows_in")
    x_loaded = sem("x_loaded")
    meta_loaded = sem("meta_loaded")
    small_in = sem("small_in")
    out_done = sem("out_done")
    dve_step = sem("dve_step")
    act_step = sem("act_step")
    pool_step = sem("pool_step")
    x_ready = Signal(sem("x_ready"))
    cols_ready = sem("cols_ready")
    turned = Signal(sem("turned"))
    pe_mix = Signal(sem("pe_mix"))
    act_mix = Signal(sem("act_mix"))
    dve_mix = Signal(sem("dve_mix"))
    pe_x = Signal(sem("pe_x"))
    act_x = Signal(sem("act_x"))
    dve_x = Signal(sem("dve_x"))
    pe_m = Signal(sem("pe_m"))
    act_m = Signal(sem("act_m"))
    dve_m = Signal(sem("dve_m"))
    out_ready = sem("out_ready")

    def tiled(w, kt, c0, width):
        return w[0:kt * P, c0:c0 + width].rearrange("(k p) m -> p k m", p=P)

    def by_tile(w, k0, kt):
        return w[k0 * P:(k0 + kt) * P, :].rearrange("(k p) (f m) -> p k f m", p=P, m=P)

    def ffn_units(wg, wu, wd, u_tile0):
        segs = []
        gv, uv = by_tile(wg, 0, KD), by_tile(wu, 0, KD)
        for f0, n in PARTS:
            body = []
            for a in range(2):
                body.append(Unit(KD, P, lambda i, f=f0 + a: gv[:, :, f + 2 * i, :]))
                body.append(Unit(KD, P, lambda i, f=f0 + a + u_tile0: uv[:, :, f + 2 * i, :]))
            segs.append(Loop(n // 2, body))
            dv = by_tile(wd, f0, n)
            segs.append(Loop(2, [Unit(n, P, lambda i, j=j, dv=dv: dv[:, :, j + 4 * i, :]) for j in range(4)]))
        return segs

    def straight(view, kt, width=P, form=None):
        return Unit(kt, width, lambda i, v=view: v, form)

    w_in, w_out = A["w_in"][0], A["w_out"][0]
    O_Q, O_K, O_V, O_R, O_Z = 0, 256, 512, 1024, 1536
    O_BG, O_CG, O_XV = 1568, 2080, 2592
    mix_units = [straight(tiled(w_in, KD, O_Z, P), KD)]
    mix_units += [straight(tiled(w_in, KD, O_Q + P * i, P), KD) for i in range(2)]
    mix_units += [straight(tiled(w_in, KD, O_K + P * i, P), KD) for i in range(2)]
    mix_units += [straight(w_in[2 * P * i:2 * P * (i + 1), O_V:O_V + 512].rearrange("(k p) m -> p k m", p=P), 2, 512)
                  for i in range(4)]
    for o in (O_R, O_CG, O_XV, O_BG):
        mix_units += [straight(tiled(w_in, KD, o + P * i, P), KD) for i in range(4)]
    mix_units += [straight(tiled(w_out, KD, P * i, P), KD) for i in range(KD)]

    w_kv, w_q, w_o = A["xattn_w_kv"][0], A["xattn_w_q"][0], A["xattn_w_o"][0]
    xat_units = [straight(tiled(w_kv, KD, P * i, P), KD) for i in range(KD)]
    for hf in range(2):
        xat_units += [straight(w_kv[2 * P * i:2 * P * (i + 1), D + 512 * hf:D + 512 * (hf + 1)]
                               .rearrange("(k p) m -> p k m", p=P), 2, 512) for i in range(4)]
    xat_units += [straight(tiled(w_q, KD, P * i, P), KD) for i in range(KD)]
    xat_units += [straight(tiled(w_o, KD, P * i, P), KD) for i in range(KD)]

    w_dqkv, w_uq, w_ukv, w_mo = A["mla_w_dqkv_2"][0], A["mla_w_uq_2"][0], A["mla_w_ukv_2"][0], A["mla_w_o_2"][0]
    HW = NOPE + ROPE
    mla_units = [straight(tiled(w_dqkv, KD, P * i, P), KD) for i in range(5)]
    mla_units += [straight(tiled(w_dqkv, KD, QL + KVL - NOPE, HW), KD, P, "rotary")]
    for p in range(MH // 2):
        mla_units += [straight(tiled(w_ukv, 2, 2 * P * p, 2 * P), 2, 2 * P, "kv")]
        mla_units += [straight(tiled(w_uq, 3, 2 * HW * p, 2 * HW), 3, 2 * P, "rotary")]
    mla_units += [straight(tiled(w_mo, KD, P * i, P), KD) for i in range(KD)]

    w_pool = A["pool_w_group_2"][0]
    pool_units = [straight(w_pool[g].rearrange("(k p) m -> p k m", p=P), 2, 2 * P) for g in range(4)]

    w_cu, w_cd = A["ffn_w_up_2"], A["ffn_w_down_2"]
    SEGS = []
    PHASE = {}

    def phase(name, segs):
        PHASE[name] = sum(4 * s.count if isinstance(s, Loop) else 1 for s in SEGS)
        SEGS.extend(segs)

    phase("ffn1", ffn_units(A["ffn1_w_gate"][0], A["ffn1_w_up"][0], A["ffn1_w_down"][0], 0))
    phase("mix", mix_units)
    phase("xat", xat_units)
    phase("ffn2", ffn_units(A["ffn2_w_gate"][0], A["ffn2_w_up"][0], A["ffn2_w_down"][0], 0))
    phase("mla", mla_units)
    phase("cffn0", ffn_units(w_cu[0], w_cu[0], w_cd[0], FT))
    phase("pool", pool_units)
    phase("cffn1", ffn_units(w_cu[1], w_cu[1], w_cd[1], FT))
    FLAT = []
    for s in SEGS:
        if isinstance(s, Loop):
            for i in range(s.count):
                FLAT += s.units
        else:
            FLAT.append(s)
    NUNITS = len(FLAT)

    def raw_view(n, u):
        return raw[:, n % RAW, 0:u.kt * u.raw_cols].rearrange("p (k m) -> p k m", k=u.kt)

    def hi_lo_pieces(n, u, dst):
        s, r = n % SPLIT, n % RAW
        if u.form is None:
            w = u.kt * u.cols
            return [(dst[:, s, 0:w], raw[:, r, 0:w], w_hi[:, s, 0:w])]
        if u.form == "kv":
            v = raw[:, r, 0:u.kt * u.cols].rearrange("p (g t m) -> p g t m", t=2, m=NOPE)
            half = u.kt * u.cols // 2
            cut = [slice(t * half, (t + 1) * half) for t in range(2)]
            return [(dst[:, s, c].rearrange("p (g m) -> p g m", m=NOPE), v[:, :, t, :],
                     w_hi[:, s, c].rearrange("p (g m) -> p g m", m=NOPE)) for t, c in enumerate(cut)]
        g = u.kt * u.cols // P
        d = dst[:, s, 0:g * P].rearrange("p (g m) -> p g m", m=P)
        h = w_hi[:, s, 0:g * P].rearrange("p (g m) -> p g m", m=P)
        v = raw[:, r, 0:g * HW].rearrange("p (g m) -> p g m", m=HW)
        half = ROPE // 2
        cuts = ((0, 0, HW), (HW, NOPE + half, half), (HW + half, NOPE, half))
        return [(d[:, :, a:a + w], v[:, :, b:b + w], h[:, :, a:a + w]) for a, b, w in cuts]

    def later(n, it, add):
        return n + add if isinstance(it, int) and it == 0 else 4 * it + (n + add)

    def sp_unit(sp, n, it, u):
        if n >= RAW or not (isinstance(it, int) and it == 0):
            sp.wait_ge(lo_done, later(n, it, 1 - RAW))
        sp.dma_start(raw_view(n, u), u.src(it)).then_inc(raw_loaded[n % RAW], 16)

    def walk(eng, step):
        n = 0
        for s in SEGS:
            if isinstance(s, Loop):
                for j, u in enumerate(s.units):
                    step(eng, n + j, 0, u)
                if s.count > 1:
                    with eng.Fori(1, s.count) as it:
                        for j, u in enumerate(s.units):
                            step(eng, n + j, it, u)
                n += 4 * s.count
            else:
                step(eng, n, 0, s)
                n += 1
            yield n

    def pool_unit(pool, n, it, u):
        pool.wait_ge(hi_done, later(n, it, 1))
        pieces = hi_lo_pieces(n, u, w_lo)
        for i, (d, r, h) in enumerate(pieces):
            ins = nc.gpsimd.tensor_tensor(d, r, h.bitcast(F32), ALU.subtract)
        ins.then_inc(lo_done, 1)

    def act_hi(act, n, it, u):
        act.wait_ge(raw_loaded[n % RAW], 16 * (n // RAW + 1) if isinstance(it, int) and it == 0
                    else 16 * it + 16 * (n // RAW + 1))
        if n >= SPLIT or not (isinstance(it, int) and it == 0):
            act.wait_ge(unit_summed, later(n, it, 1 - SPLIT))
        for d, r, _ in hi_lo_pieces(n, u, w_hi):
            ins = nc.scalar.activation(d, r, ACT.Copy)
        ins.then_inc(hi_done, 1)

    hi_next = [0]

    def hi_to(act, n):
        while hi_next[0] <= min(n, NUNITS - 1):
            act_hi(act, hi_next[0], 0, FLAT[hi_next[0]])
            hi_next[0] += 1

    def psv(pair, blk):
        return PS[pair][:, 0, :] if blk == 1 else PS[pair][:, :, 0:CW]

    def sv(ap, blk):
        return ap if blk == 1 else ap.rearrange("p (c w) -> p c w", c=2)

    def width(blk):
        return S1 if blk == 1 else S2

    def chunks(blk):
        return ((0, 0, S1),) if blk == 1 else ((0, 0, CW), (1, CW, CW))

    def xt(m, blk):
        return X[:, m, META:S2] if blk == 1 else X[:, m, 0:S2]

    def hi(m, blk):
        return XHI[:, m, 0:width(blk)]

    def lo(m, blk):
        return XLO[:, m, 0:width(blk)]

    def pe_unit(pe, n, it, u, ahi, alo, outs, ready=None, cols0=0, signal=True, wait=True):
        if wait:
            if n >= 4 or not (isinstance(it, int) and it == 0):
                pe.wait_ge(unit_read, later(n, it, -3))
            pe.wait_ge(lo_done, later(n, it, 1))
        s = n % SPLIT
        for k in range(u.kt):
            if ready:
                ready(k)
            c0 = k * u.cols + cols0
            wh, wl = w_hi[:, s, c0:c0 + P], w_lo[:, s, c0:c0 + P]
            for ps, c, w in outs:
                nc.tensor.matmul(ps, wh, ahi(k)[:, c:c + w], start=(k == 0), stop=False)
            for ps, c, w in outs:
                nc.tensor.matmul(ps, wh, alo(k)[:, c:c + w], start=False, stop=False)
            for ps, c, w in outs:
                ins = nc.tensor.matmul(ps, wl, ahi(k)[:, c:c + w], start=False, stop=(k == u.kt - 1))
        if signal:
            ins.then_inc(unit_summed, 1)

    def outs_of(pair, blk):
        return [(PS[pair][:, c, 0:w], c0, w) for c, c0, w in chunks(blk)]

    def pe_norm(pe, s, pair, blk, source=acc, need=None):
        if need is None:
            pe.wait_ge(acc_done, KD * s + KD)
        for ps, c, w in outs_of(pair, blk):
            ins = nc.tensor.matmul(ps, ones, source[:, c:c + w], start=True, stop=True)
        return ins

    def step_link(eng, sm):
        n = [0]

        def link(ins):
            n[0] += 1
            ins.then_inc(sm, 1)
            eng.wait_ge(sm, n[0])
        return link

    block = ctx.enter_context(nc.Block())

    S_FFN1, S_MIX, S_XAT, S_FFN2, S_FIN, S_MLA, S_MLAP, S_CF0, S_CF0P, S_POOL, S_POOLP, S_CF1, S_CF1P = range(13)
    D_FFN1, D_MIX, D_MIXO, D_XAT, D_XATO, D_FFN2, D_MLA, D_CF0, D_POOL, D_CF1 = range(10)

    turned.declare("cols", "meta", *[("x", k) for k in range(KD)], *[("out", t) for t in range(4)])
    x_ready.declare("meta", *[("x", k) for k in range(KD)], *[("fin", k) for k in range(KD)])

    def act_loop(act, count, body):
        body(0)
        if count > 2:
            with act.Fori(1, count - 1) as it:
                body(it)
        if count > 1:
            body(count - 1)

    def run_loop(eng, count, body):
        body(0)
        if count > 1:
            with eng.Fori(1, count) as it:
                body(it)

    def static(it):
        return isinstance(it, int)

    def first(it):
        return isinstance(it, int) and it == 0

    def act_split(act, d, m, j, blk, gain):
        nc.scalar.activation(hi(m, blk), xt(m, blk), ACT.Identity, scale=gain(m)).then_inc(x_hi, 1)

    def act_square(act, s, m, j, src, w):
        if not (static(m) and KD * s + m < 2):
            act.wait_ge(acc_done, m + (KD * s - 1))
        nc.scalar.activation(sq[:, j % 2, 0:w], src, ACT.Square).then_inc(sq_done, 1)

    def dve_split(dve, d, m, blk, gain):
        dve.wait_ge(x_hi, m + (KD * d + 1))
        nc.vector.scalar_tensor_tensor(lo(m, blk), xt(m, blk), gain(m), hi(m, blk).bitcast(F32), ALU.mult,
                                       ALU.subtract).then_inc(x_lo, 1)

    def dve_acc(dve, s, m, j, w):
        dve.wait_ge(sq_done, m + (KD * s + 1))
        if static(m) and m == 0:
            nc.vector.tensor_copy(acc[:, 0:w], sq[:, 0, 0:w]).then_inc(acc_done, 1)
        else:
            dve.wait_ge(acc_done, m + KD * s)
            nc.vector.tensor_tensor(acc[:, 0:w], acc[:, 0:w], sq[:, j % 2, 0:w], ALU.add).then_inc(acc_done, 1)

    def act_sqrt(act, s, w):
        act.wait_ge(norm_ms, s + 1)
        nc.scalar.activation(sd[:, 0:w], ms[:, 0:w], ACT.Sqrt).then_inc(norm_sd, 1)

    def newton(link, r, v, t, s):
        link(nc.vector.reciprocal(r, s))
        link(nc.vector.tensor_tensor(t, r, r, ALU.mult))
        link(nc.vector.scalar_tensor_tensor(t, t, -0.5, v, ALU.mult, ALU.mult))
        link(nc.vector.scalar_tensor_tensor(r, t, 1.5, r, ALU.add, ALU.mult))

    def dve_norm(dve, link, s, pair, blk, rc=0):
        w = width(blk)
        dve.wait_ge(norm_sum, s + 1)
        if rc:
            link(nc.vector.tensor_scalar(ms[:, w:w + rc], PS[pair][:, 1, 0:rc], 1.0 / D, EPS, ALU.mult, ALU.add))
        nc.vector.tensor_scalar(sv(ms[:, 0:w], blk), psv(pair, blk), 1.0 / D, EPS, ALU.mult, ALU.add).then_inc(norm_ms, 1)
        dve.wait_ge(norm_sd, s + 1)
        w += rc
        newton(link, rn[:, 0:w], ms[:, 0:w], rt[:, 0:w], sd[:, 0:w])

    def gain_of(name, index):
        return lambda m: column(name, index, m)

    G_FFN1, G_MIX, G_XAT = gain_of("ffn1_norm", 0), gain_of("mix_norm", 0), gain_of("xattn_norm", 0)
    G_MEM, G_FFN2, G_FIN = gain_of("mem_norm", 0), gain_of("ffn2_norm", 0), gain_of("final_norm", None)
    G_PRE = [gain_of("norm_mix_pre_2", i) for i in range(2)]
    G_POST = [gain_of("norm_mix_post_2", i) for i in range(2)]
    G_FPRE = [gain_of("norm_ffn_pre_2", i) for i in range(2)]
    G_FPOST = [gain_of("norm_ffn_post_2", i) for i in range(2)]

    GROUP_SIZES = [sum(r for _, _, r in group) for group in GROUP_ROWS]

    def act_start(act):
        for g, group in enumerate(GROUP_ROWS):
            at = 0
            for name, index, n in group:
                v = A[name]
                for ix in ((index,) if isinstance(index, int) else index or ()):
                    v = v[ix]
                act.dma_start(rows[at:at + n, g, :], v.rearrange("(f p) -> f p", p=P)).then_inc(rows_in, 16)
                at += n
        act.dma_start(meta_in[:, :], A["meta_tokens_2"]).then_inc(meta_loaded, 16)
        hi_to(act, 1)
        act.wait_ge(cols_ready, len(GROUP_ROWS))
        for k in range(KD):
            x_ready.wait(act, ("x", k))
            act_split(act, D_FFN1, k, k, 1, G_FFN1)
            act_square(act, S_FFN1, k, k, xt(k, 1), S1)

    NDMA = sum(len(g) for g in GROUP_ROWS)

    def pe_start(pe):
        pe.wait_ge(const_in, 16)
        pe.wait_ge(rows_in, 16 * NDMA)
        for g, n in enumerate(GROUP_SIZES):
            ins = nc.tensor.transpose(PS[0][:, g // 4, (g % 4) * P:(g % 4) * P + n], rows[0:n, g, :], ident[0:n, 0:n])
        turned.inc(ins, "cols")
        pe.wait_ge(meta_loaded, 16)
        for k in range(KD):
            ins = nc.tensor.transpose(PS[1][:, 1, k * META:(k + 1) * META], meta_in[:, k * P:(k + 1) * P],
                                      ident[0:META, 0:META])
        turned.inc(ins, "meta")
        pe.wait_ge(x_loaded, 16 * (S1 // P))
        for k in range(KD):
            pair = (k + 2) % 4
            if k == 2:
                pe.wait_ge(cols_ready, len(GROUP_ROWS))
            if k == 3:
                x_ready.wait(pe, "meta")
            if k >= 4:
                x_ready.wait(pe, ("x", k - 4))
            for t in range(S1 // P):
                ins = nc.tensor.transpose(PS[pair][:, 0, t * P:(t + 1) * P], x_in[:, t, k * P:(k + 1) * P], ident)
            turned.inc(ins, ("x", k))
        x_ready.wait(pe, ("x", KD - 1))

    def dve_start(dve):
        turned.wait(dve, "cols")
        for g, n in enumerate(GROUP_SIZES):
            nc.vector.tensor_copy(cols[:, g, 0:n], PS[0][:, g // 4, (g % 4) * P:(g % 4) * P + n]).then_inc(cols_ready, 1)
        dve.wait_ge(cols_ready, len(GROUP_ROWS))
        turned.wait(dve, "meta")
        x_ready.inc(nc.vector.tensor_copy(X[:, :, 0:META], PS[1][:, 1, 0:KD * META].rearrange("p (k t) -> p k t", k=KD)),
                    "meta")
        for k in range(KD):
            turned.wait(dve, ("x", k))
            x_ready.inc(nc.vector.tensor_copy(xt(k, 1), PS[(k + 2) % 4][:, 0, :]), ("x", k))
            if k:
                dve_split(dve, D_FFN1, k - 1, 1, G_FFN1)
                dve_acc(dve, S_FFN1, k - 1, k - 1, S1)
        dve_split(dve, D_FFN1, KD - 1, 1, G_FFN1)
        dve_acc(dve, S_FFN1, KD - 1, KD - 1, S1)

    def pe_ffn(pe, name, blk, inv, s, d):
        n = PHASE[name]
        n0 = n
        for pi, (f0, nt) in enumerate(PARTS):
            def up(it, n=n, pi=pi):
                for j in range(4):
                    ready = None
                    if first(it) and pi == 0 and j == 0:
                        ready = lambda k: pe.wait_ge(x_lo, KD * d + k + 1)
                    if first(it) and pi == 0 and j == 3:
                        pe.wait_ge(norm_ms, s + 1)
                    pe_unit(pe, n + j, it, FLAT[n + j], lambda k: hi(k, blk), lambda k: lo(k, blk),
                            outs_of((n + j) % 4, blk), ready)
                    if first(it) and pi == 0 and j == 0:
                        if n:
                            pe.wait_ge(unit_read, n)
                        pe_norm(pe, s, (n + 3) % 4, blk).then_inc(norm_sum, 1)
            run_loop(pe, nt // 2, up)
            n += 2 * nt

            def down(it, n=n, f0=f0):
                for j in range(4):
                    ready = None
                    if first(it) and j == 0:
                        ready = lambda k: pe.wait_ge(hid_lo, inv * FT + f0 + k + 1)
                    pe_unit(pe, n + j, it, FLAT[n + j], lambda k: h_hi[:, k, 0:width(blk)],
                            lambda k: h_lo[:, k, 0:width(blk)], outs_of((n + j) % 4, blk), ready)
            run_loop(pe, 2, down)
            n += KD

    def act_ffn(act, name, blk, inv, s, after):
        n = PHASE[name]
        w = width(blk)
        cb = (inv - 2) * FT
        for pi, (f0, nt) in enumerate(PARTS):
            count = nt // 2

            def look(it, n, j, count):
                if static(it):
                    if n + j + 2 + 4 * it < NUNITS:
                        act_hi(act, n + j + 2, it, FLAT[n + j + 2 + 4 * it])
                else:
                    act_hi(act, n + j + 2, it, FLAT[n + (j + 2) % 4])

            def up(it, n=n, pi=pi, f0=f0, count=count):
                for a in range(2):
                    g = (inv * FT + f0 + a) + 2 * it
                    look(it, n, 2 * a, count)
                    if first(it) and pi == 0 and a == 0:
                        act_sqrt(act, s, w)
                    act.wait_ge(unit_read, later(n, it, 2 * a + 1))
                    if blk == 2:
                        f = (f0 + a) + 2 * it
                        nc.scalar.activation(g_conv[:, :], g_buf[:, 2:], ACT.Identity, scale=tap(inv - 2, 2, f),
                                             bias=tap(inv - 2, 3, f)).then_inc(conv_tap, 1)
                        act.wait_ge(conv_done, (2 * (cb + f0 + a) + 1) + 4 * it)
                        nc.scalar.activation(g_act[:, 0:w], g_conv[:, 0:w], ACT.Silu).then_inc(silu_done, 1)
                    else:
                        nc.scalar.activation(g_act[:, 0:w], g_buf[:, 0:w], ACT.Silu).then_inc(silu_done, 1)
                    look(it, n, 2 * a + 1, count)
                    if blk == 2:
                        act.wait_ge(unit_read, later(n, it, 2 * a + 2))
                        nc.scalar.activation(u_conv[:, :], u_buf[:, 2:], ACT.Identity, scale=tap(inv - 2, 2, f + FT),
                                             bias=tap(inv - 2, 3, f + FT)).then_inc(conv_tap, 1)
                    act.wait_ge(hid_prod, g + 1)
                    nc.scalar.activation(h_hi[:, a + 2 * it, 0:w], hid[:, 0:w], ACT.Copy).then_inc(hid_hi, 1)
            act_loop(act, count, up)
            n += 2 * nt

            def down(it, n=n, pi=pi):
                for j in range(4):
                    look(it, n, j, 2)
                    if pi == len(PARTS) - 1:
                        act.wait_ge(unit_read, later(n, it, j + 1))
                        after(j + 4 * it, j)
            act_loop(act, 2, down)
            n += KD
        hi_next[0] = n + 2

    def tap(layer, j, f):
        if j < 3:
            return column("ffn_conv_w_2", (layer, j), f)
        return column("ffn_conv_b_2", layer, f)

    def dve_ffn(dve, link, name, blk, inv, s, after):
        n = PHASE[name]
        w = width(blk)
        cb = (inv - 2) * FT
        if blk == 2:
            link(nc.vector.memset(g_buf[:, 0:2], 0.0))
            link(nc.vector.memset(u_buf[:, 0:2], 0.0))
        dve_norm(dve, link, s, (n + 3) % 4, blk)
        r = sv(rn[:, 0:w], blk)
        n_down = None
        for pi, (f0, nt) in enumerate(PARTS):
            def up(it, n=n, f0=f0):
                for a in range(2):
                    g = (inv * FT + f0 + a) + 2 * it
                    f = (f0 + a) + 2 * it
                    for b, (buf, cv_) in enumerate(((g_buf, g_conv), (u_buf, u_conv))):
                        m = n + 2 * a + b
                        dst = buf[:, 2:2 + w] if blk == 2 else buf[:, 0:w]
                        dve.wait_ge(unit_summed, later(m, it, 1))
                        nc.vector.tensor_tensor(sv(dst, blk), psv(m % 4, blk), r, ALU.mult).then_inc(unit_read, 1)
                        if blk == 2:
                            ci = (2 * (cb + f0 + a) + b + 1) + 4 * it
                            ft = f + FT if b else f
                            dve.wait_ge(conv_tap, ci)
                            nc.vector.scalar_tensor_tensor(cv_[:, :], buf[:, 1:1 + w], tap(inv - 2, 1, ft), cv_[:, :],
                                                           ALU.mult, ALU.add).then_inc(conv_mid, 1)
                            dve.wait_ge(conv_mid, ci)
                            nc.vector.scalar_tensor_tensor(cv_[:, :], buf[:, 0:w], tap(inv - 2, 0, ft), cv_[:, :],
                                                           ALU.mult, ALU.add).then_inc(conv_done, 1)
                    up_src = u_conv if blk == 2 else u_buf
                    if blk == 2:
                        dve.wait_ge(conv_done, (2 * (cb + f0 + a) + 2) + 4 * it)
                    else:
                        dve.wait_ge(unit_read, later(n, it, 2 * a + 2))
                    dve.wait_ge(silu_done, g + 1)
                    nc.vector.tensor_tensor(hid[:, 0:w], g_act[:, 0:w], up_src[:, 0:w], ALU.mult).then_inc(hid_prod, 1)
                    dve.wait_ge(hid_hi, g + 1)
                    nc.vector.tensor_tensor(h_lo[:, a + 2 * it, 0:w], hid[:, 0:w], h_hi[:, a + 2 * it, 0:w].bitcast(F32),
                                            ALU.subtract).then_inc(hid_lo, 1)
            run_loop(dve, nt // 2, up)
            n += 2 * nt

            def down(it, n=n, pi=pi, n_down=n_down):
                for j in range(4):
                    m = j + 4 * it
                    dve.wait_ge(unit_summed, later(n, it, j + 1))
                    ps = psv((n + j) % 4, blk)
                    if pi:
                        dve.wait_ge(unit_read, later(n_down, it, j + 1))
                    if blk == 1:
                        nc.vector.scalar_tensor_tensor(xt(m, 1), ps, 0.5, xt(m, 1), ALU.mult, ALU.add).then_inc(unit_read, 1)
                    elif pi == 0:
                        nc.vector.tensor_copy(sv(M[:, m, :], 2), ps).then_inc(unit_read, 1)
                    else:
                        nc.vector.tensor_tensor(sv(M[:, m, :], 2), ps, sv(M[:, m, :], 2), ALU.add).then_inc(unit_read, 1)
                    if pi == len(PARTS) - 1:
                        after(m, j)
            run_loop(dve, 2, down)
            n_down = n
            n += KD

    def pe_post(pe, s, n):
        pe.wait_ge(unit_read, n)
        pe_norm(pe, s, n % 4, 2).then_inc(norm_sum, 1)

    def dve_post(dve, link, i, s, n, gain, s_next=None, d_next=None, g_next=None):
        dve_norm(dve, link, s, n % 4, 2)
        for k in range(KD + 1):
            if k < KD:
                if k >= 2:
                    dve.wait_ge(post_added, KD * i + k - 1)
                nc.vector.scalar_tensor_tensor(post_t[:, k % 2, 0:S2], M[:, k, :], gain(k), rn[:, 0:S2], ALU.mult,
                                               ALU.mult).then_inc(post_scaled, 1)
            if k and s_next is not None:
                if d_next is not None:
                    dve_split(dve, d_next, k - 1, 2, g_next)
                dve_acc(dve, s_next, k - 1, k - 1, S2)

    def pool_post(pool, i):
        for k in range(KD):
            pool.wait_ge(post_scaled, KD * i + k + 1)
            nc.gpsimd.tensor_tensor(X[:, k, :], X[:, k, :], post_t[:, k % 2, 0:S2], ALU.add).then_inc(post_added, 1)

    def act_post(act, i, s, s_next=None, d_next=None, g_next=None):
        act_sqrt(act, s, S2)
        for k in range(KD if s_next is not None else 0):
            act.wait_ge(post_added, KD * i + k + 1)
            if d_next is not None:
                act_split(act, d_next, k, k, 2, g_next)
            act_square(act, s_next, k, k, X[:, k, :], S2)

    def pe_out(pe, need):
        need(pe)
        for t in range(S1 // P):
            for k in range(KD):
                ins = nc.tensor.transpose(PS[t][:, k // 4, (k % 4) * P:(k % 4 + 1) * P],
                                          X[:, k, META + t * P:META + (t + 1) * P], ident)
            turned.inc(ins, ("out", t))

    def dve_out(dve):
        for t in range(S1 // P):
            turned.wait(dve, ("out", t))
            nc.vector.tensor_copy(out_tok[:, t, :].rearrange("p (c w) -> p c w", c=2), PS[t][:, :, :]).then_inc(out_ready, 1)

    pe_mix.declare("lg", *[("kt", i) for i in range(4)], *[("ds", i) for i in range(4)],
                   ("att", 0), ("att", 1), ("o", 0), ("att", 2), ("o", 1), ("att", 3),
                   ("osum", 0), ("o", 2), ("osum", 1), ("o", 3), ("osum", 2), ("osum", 3))
    act_mix.declare("abs", "exp", "ln", "eq", "es", "ek", *[("r", j) for j in range(4)], *[("ktc", i) for i in range(4)],
                    *[("tap", j) for j in range(4)],
                    ("osq", 0), ("osq", 1), ("osd", 0), ("osq", 2), ("osd", 1), ("osq", 3), ("osd", 2), ("osd", 3))
    dve_mix.declare("gz", *[("min", i) for i in range(4)], "scan", "diff", ("qin", 0), ("qin", 1), ("kst", 0), ("kst", 1),
                    ("kin", 0), ("kin", 1), ("state", 0), ("state", 1),
                    ("u", 0), ("u", 1), ("state", 2), ("u", 2), ("u", 3), ("state", 3),
                    *[("c", j) for j in range(4)], "attz",
                    ("att", 0), ("att", 1), ("att", 2), ("att", 3),
                    *[(k, h) for h in range(4) for k in ("oms", "oread", "y")])
    W_OUT = 25
    SIDE = [PS[i][:, 1, :] for i in range(4)]
    MIXO_ORDER = [4, 5, 6, 7, 0, 1, 2, 3]

    def side_of(c):
        at = c // 2
        return SIDE[2 * (c % 2) + at // 2][:, at % 2 * 256:(at % 2 + 1) * 256]

    def pe_mixer(pe):
        n = PHASE["mix"]
        H, L = (lambda k: hi(k, 1)), (lambda k: lo(k, 1))

        def unit(j, ready=None):
            pe_unit(pe, n + j, 0, FLAT[n + j], H, L, outs_of((n + j) % 4, 1), ready)

        unit(0, lambda k: pe.wait_ge(x_lo, KD * D_MIX + k + 1))
        pr_ = (n + 3) % 4
        pe.wait_ge(unit_read, n)
        pe_norm(pe, S_MIX, pr_, 1)
        for t in range(4):
            ins = nc.tensor.matmul(PS[pr_][:, 1, t:t + 1], acc[:, t * P:(t + 1) * P], ones[:, 0:1], start=True, stop=True)
        ins.then_inc(norm_sum, 1)
        unit(1)
        unit(2)
        pe.wait_ge(norm_ms, S_MIX + 1)
        pe.wait_ge(unit_read, n + 1)
        pe.wait_ge(small_in, 32)
        for i in range(4):
            ins = nc.tensor.matmul(SIDE[i], gate_w[:, i * P:(i + 1) * P], zz[:, :], start=True, stop=True)
        pe_mix.inc(ins, "lg")
        unit(3)
        unit(4)
        act_mix.wait(pe, "abs")
        dve_mix.wait(pe, ("min", 3))
        for i in range(4):
            m = n + 5 + i
            pe.wait_ge(lo_done, m + 1)
            s = m % SPLIT
            for kk in range(2):
                k = 2 * i + kk
                wh, wl = w_hi[:, s, kk * 512:(kk + 1) * 512], w_lo[:, s, kk * 512:(kk + 1) * 512]
                for t in range(4):
                    xh, xl = H(k)[:, t * P:(t + 1) * P], L(k)[:, t * P:(t + 1) * P]
                    nc.tensor.matmul(SIDE[t], xh, wh, start=(k == 0), stop=False)
                    nc.tensor.matmul(SIDE[t], xh, wl, start=False, stop=False)
                    ins = nc.tensor.matmul(SIDE[t], xl, wh, start=False, stop=(k == KD - 1))
            ins.then_inc(unit_summed, 1)
        for j in range(4):
            unit(9 + j)
        pe.wait_ge(unit_read, n + 9)
        dve_mix.wait(pe, ("kst", 1))
        for i in range(4):
            for t in range(4):
                ins = nc.tensor.transpose(SIDE[i][:, t * P:(t + 1) * P], t3[:, i, t * P:(t + 1) * P], ident)
            pe_mix.inc(ins, ("kt", i))
        for j in range(4):
            for jj in range(2 if j < 4 else 0):
                unit(13 + 2 * j + jj)
            if j == 0:
                act_mix.wait(pe, ("ktc", 3))
            else:
                dve_mix.wait(pe, ("state", j - 1))
            for c in (range(0, NCH - 1) if j < 2 else range(1, NCH)):
                p0 = CHUNK * (c % 2)
                ins = nc.tensor.matmul(side_of(c), kst_tok[p0:p0 + CHUNK, j, c // 2, :],
                                       v_tok[p0:p0 + CHUNK, c // 2, (j % 2) * 256:(j % 2 + 1) * 256], start=True, stop=True)
            pe_mix.inc(ins, ("ds", j))
        for j in range(4):
            unit(21 + j)
        dve_mix.wait(pe, ("kin", 1))

        def scores(h):
            p0 = GDK * (h % 2)
            if h < 2:
                dve_mix.wait(pe, ("state", 3))
            else:
                dve_mix.wait(pe, ("att", h - 2))
            for d in range(2):
                i = 2 * d + h // 2
                for t in range(4):
                    ins = nc.tensor.matmul(SIDE[2 * (h % 2) + d][:, t * P:(t + 1) * P], k_in[p0:p0 + GDK, i, t * P:(t + 1) * P],
                                           q_in[p0:p0 + GDK, i, t * P:(t + 1) * P], start=True, stop=True)
            pe_mix.inc(ins, ("att", h))

        def output(h):
            p0 = GDK * (h % 2)
            if h == 0:
                pe.wait_ge(unit_read, n + W_OUT)
            dve_mix.wait(pe, ("att", h))
            for t in range(4):
                o = PS[h][:, 0, t * P:(t + 1) * P]
                v = v_tok[:, t, h * GDV:(h + 1) * GDV]
                nc.tensor.matmul(o, v, att[:, h % 2, 0, t * P:(t + 1) * P], start=True, stop=False)
                pieces = [(0, 2 * t), (0, 2 * t + 1), (1, 2 * t), (1, 2 * t + 1)]
                pieces = [(d, c) for d, c in pieces if not (d == 0 and c == 0) and not (d == 1 and c == NCH - 1)]
                for d, c in pieces:
                    i = 2 * d + h // 2
                    nc.tensor.matmul(PS[h][:, 0, c * CHUNK:(c + 1) * CHUNK], state[p0:p0 + GDK, i, c, :],
                                     q_in[p0:p0 + GDK, i, c * CHUNK:(c + 1) * CHUNK], start=False, stop=False)
                ins = nc.tensor.matmul(o, v, att[:, h % 2, 1, t * P:(t + 1) * P], start=False, stop=True)
            pe_mix.inc(ins, ("o", h))

        def output_norm(h):
            act_mix.wait(pe, ("osq", h))
            dve_mix.wait(pe, ("att", 2 if h < 2 else 3))
            pe_mix.inc(nc.tensor.matmul(SIDE[h], ones, osq[h], start=True, stop=True), ("osum", h))

        scores(0)
        scores(1)
        output(0)
        scores(2)
        output(1)
        scores(3)
        output_norm(0)
        output(2)
        output_norm(1)
        output(3)
        output_norm(2)
        output_norm(3)
        for j in range(KD):
            m = n + W_OUT + j
            if j < 4:
                dve_mix.wait(pe, ("oread", m % 4))
            pe_unit_order(pe, m, H, L, 1, lambda at: pe.wait_ge(x_lo, KD * D_MIXO + at + 1) if j == 0 else None)

    def pe_unit_order(pe, n, ahi, alo, blk, ready):
        u = FLAT[n]
        pe.wait_ge(unit_read, n - 3)
        pe.wait_ge(lo_done, n + 1)
        s = n % SPLIT
        for at, k in enumerate(MIXO_ORDER):
            ready(at)
            wh, wl = w_hi[:, s, k * P:(k + 1) * P], w_lo[:, s, k * P:(k + 1) * P]
            for ps, c, w in outs_of(n % 4, blk):
                nc.tensor.matmul(ps, wh, ahi(k)[:, c:c + w], start=(at == 0), stop=False)
                nc.tensor.matmul(ps, wh, alo(k)[:, c:c + w], start=False, stop=False)
                ins = nc.tensor.matmul(ps, wl, ahi(k)[:, c:c + w], start=False, stop=(at == u.kt - 1))
        ins.then_inc(unit_summed, 1)

    osq = [o_sq[:, h % 2, :] for h in range(4)]

    def act_mixer(act):
        n = PHASE["mix"]
        hi_to(act, n + 2)
        dve_mix.wait(act, "gz")
        act.dma_start(gate_w[0:16, 0:256], A["gate_fwd_w"][0]).then_inc(small_in, 16)
        act.dma_start(gate_w[16:32, 256:512], A["gate_bwd_w"][0]).then_inc(small_in, 16)
        act_sqrt(act, S_MIX, S1 + 4)
        hi_to(act, n + 4)
        pe_mix.wait(act, "lg")
        link = step_link(act, act_step)
        gb = [column("gate_fwd_b" if i < 2 else "gate_bwd_b", 0, i % 2) for i in range(4)]
        for i in range(3):
            dve_mix.wait(act, ("min", i))
            link(nc.scalar.activation(t1[:, i, :], SIDE[i], ACT.Abs, bias=gb[i]))
        dve_mix.wait(act, ("min", 3))
        act_mix.inc(nc.scalar.activation(t1[:, 3, :], SIDE[3], ACT.Abs, bias=gb[3]), "abs")
        act_mix.wait(act, "abs")
        act_mix.inc(nc.scalar.activation(t1[:, :, :], t1[:, :, :], ACT.Exp, scale=-1.0), "exp")
        act_mix.wait(act, "exp")
        act_mix.inc(nc.scalar.activation(t1[:, :, :], t1[:, :, :], ACT.Ln, bias=1.0), "ln")
        hi_to(act, n + 5)
        dve_mix.wait(act, "scan")
        act_mix.inc(nc.scalar.activation(t3[:, :, :], t1[:, :, :], ACT.Exp, scale=1.0 / 16), "eq")
        hi_to(act, n + 6)
        dve_mix.wait(act, "diff")
        link(nc.scalar.activation(dec[:, :, :], tot[:, :, :], ACT.Exp, scale=1.0 / 16))
        act_mix.inc(nc.scalar.activation(t2[:, :, :], t2[:, :, :], ACT.Exp, scale=1.0 / 16), "es")
        act_mix.wait(act, "eq")
        act_mix.inc(nc.scalar.activation(t1[:, :, :], t1[:, :, :], ACT.Exp, scale=-1.0 / 16), "ek")
        hi_to(act, n + 10)
        for j in range(4):
            hi_to(act, n + 9 + j + 2)
            act.wait_ge(unit_read, n + 9 + j + 1)
            act_mix.inc(nc.scalar.activation(r_act[:, j, :], mtmp[:, j % 2, :], ACT.Silu), ("r", j))
        for i in range(4):
            pe_mix.wait(act, ("kt", i))
            act_mix.inc(nc.scalar.activation(kst_tok[:, i, :, :], SIDE[i].rearrange("p (t f) -> p t f", t=4), ACT.Copy),
                        ("ktc", i))
        hi_to(act, n + 18)
        for j in range(4):
            hi_to(act, n + 17 + j + 2)
            dve_mix.wait(act, ("u", j))
            act_mix.inc(nc.scalar.activation(cv[:, j, :], cu[:, j, 1:S1 + 1], ACT.Identity,
                                             scale=column("conv_w", (0, 1), j), bias=column("conv_b", 0, j)), ("tap", j))
        for j in range(4):
            hi_to(act, n + 21 + j + 2)
        act.wait_ge(unit_summed, n + W_OUT)
        for j in range(4):
            dve_mix.wait(act, ("c", j))
            nc.scalar.activation(hi(4 + j, 1), cv[:, j, :], ACT.Copy).then_inc(x_hi, 1)

        def square(h):
            pe_mix.wait(act, ("o", h))
            act_mix.inc(nc.scalar.activation(osq[h], PS[h][:, 0, :], ACT.Square), ("osq", h))

        def root(h):
            dve_mix.wait(act, ("oms", h))
            act_mix.inc(nc.scalar.activation(sd[:, 0:S1], ms[:, 0:S1], ACT.Sqrt), ("osd", h))

        def split(h):
            dve_mix.wait(act, ("y", h))
            nc.scalar.activation(hi(h, 1), o_gla[:, h % 2, :], ACT.Copy).then_inc(x_hi, 1)

        square(0)
        square(1)
        root(0)
        split(0)
        square(2)
        root(1)
        split(1)
        square(3)
        root(2)
        split(2)
        root(3)
        split(3)
        act.wait_ge(x_lo, KD * (D_MIXO + 1))
        act.dma_start(mem_in[:, :, :], A["mem"][0].rearrange("(t p) d -> p t d", p=P)).then_inc(x_loaded, 16)
        act_out_units(act, n + W_OUT, S_XAT)

    def act_out_units(act, n, s):
        for m in range(KD):
            hi_to(act, n + m + 2)
            act.wait_ge(unit_read, n + m + 1)
            act_square(act, s, m, m, xt(m, 1), S1)

    def dve_out_units(dve, n, s):
        for m in range(KD):
            dve.wait_ge(unit_summed, n + m + 1)
            nc.vector.tensor_tensor(xt(m, 1), PS[(n + m) % 4][:, 0, :], xt(m, 1), ALU.add).then_inc(unit_read, 1)
            dve_acc(dve, s, m, m, S1)

    def act_split_all(act, d, gain, n):
        act.wait_ge(unit_summed, n)
        for m in range(KD):
            act_split(act, d, m, m, 1, gain)

    def dve_split_all(dve, d, gain):
        for m in range(KD):
            dve_split(dve, d, m, 1, gain)

    def dve_mixer(dve, link):
        n = PHASE["mix"]
        R = rn[:, 0:S1]

        def summed(j):
            dve.wait_ge(unit_summed, n + j + 1)
            return PS[(n + j) % 4][:, 0, :]

        link(nc.vector.memset(cu[:, :, 0:1], 0.0))
        link(nc.vector.memset(cu[:, :, S1 + 1:S1 + 2], 0.0))
        dve.wait_ge(unit_summed, n)
        dve_mix.inc(nc.vector.memset(gate_w[:, :], 0.0), "gz")
        dve_norm(dve, link, S_MIX, (n + 3) % 4, 1, rc=4)
        nc.vector.tensor_tensor(zz[:, :], summed(0)[0:32, :], R[0:32, :], ALU.mult).then_inc(unit_read, 1)
        for t in range(2):
            nc.vector.scalar_tensor_tensor(qs[:, t, :], summed(1 + t), float(GDK ** -0.5), R, ALU.mult,
                                           ALU.mult).then_inc(unit_read, 1)
        pe_mix.wait(dve, "lg")
        for i in range(4):
            dve_mix.inc(nc.vector.tensor_scalar(t2[:, i, :], SIDE[i], column("gate_fwd_b" if i < 2 else "gate_bwd_b", 0, i % 2),
                                                0.0, ALU.add, ALU.min), ("min", i))
        for t in range(2):
            nc.vector.tensor_tensor(ks[:, t, :], summed(3 + t), R, ALU.mult).then_inc(unit_read, 1)
        act_mix.wait(dve, "ln")
        dve_mix.wait(dve, ("min", 3))
        link(nc.vector.tensor_tensor(t2[:, :, :], t2[:, :, :], t1[:, :, :], ALU.subtract))
        reset = const[:, C_RST:C_RST + S1]
        for i in range(4):
            rev = slice(None) if i < 2 else slice(None, None, -1)
            ins = nc.vector.tensor_tensor_scan(t1[:, i, :][:, rev], reset, t2[:, i, :][:, rev], 0.0, ALU.mult, ALU.add)
            if i < 3:
                link(ins)
        dve_mix.inc(ins, "scan")
        dve_mix.wait(dve, "scan")
        link(nc.vector.tensor_copy(tot[:, 0:2, :], t1[:, 0:2, CHUNK - 1::CHUNK]))
        link(nc.vector.tensor_copy(tot[:, 2:4, :], t1[:, 2:4, 0::CHUNK]))
        dve_mix.inc(nc.vector.tensor_tensor(t2[:, :, :].rearrange("p i (c t) -> p (i c) t", t=CHUNK),
                                            tot[:, :, :].rearrange("p i c -> p (i c)").to_broadcast([P, 4 * NCH, CHUNK]),
                                            t1[:, :, :].rearrange("p i (c t) -> p (i c) t", t=CHUNK), ALU.subtract), "diff")
        act_mix.wait(dve, "eq")
        dve.wait_ge(unit_read, n + 5)
        for d in range(2):
            dve_mix.inc(nc.vector.tensor_tensor(q_in[:, 2 * d:2 * d + 2, :], qs[:, :, :], t3[:, 2 * d:2 * d + 2, :], ALU.mult),
                        ("qin", d))
        act_mix.wait(dve, "es")
        dve_mix.wait(dve, ("qin", 1))
        for d in range(2):
            dve_mix.inc(nc.vector.tensor_tensor(t3[:, 2 * d:2 * d + 2, :], ks[:, :, :], t2[:, 2 * d:2 * d + 2, :], ALU.mult),
                        ("kst", d))
        act_mix.wait(dve, "ek")
        for d in range(2):
            dve_mix.inc(nc.vector.tensor_tensor(k_in[:, 2 * d:2 * d + 2, :], ks[:, :, :], t1[:, 2 * d:2 * d + 2, :], ALU.mult),
                        ("kin", d))
        dve.wait_ge(unit_summed, n + 9)
        for t in range(4):
            nc.vector.tensor_scalar(v_tok[:, t, :], SIDE[t], rn[:, S1 + t:S1 + t + 1], None, ALU.mult).then_inc(unit_read, 1)
        for j in range(4):
            if j >= 2:
                act_mix.wait(dve, ("r", j - 2))
            nc.vector.tensor_tensor(mtmp[:, j % 2, :], summed(9 + j), R, ALU.mult).then_inc(unit_read, 1)

        def states(i):
            pe_mix.wait(dve, ("ds", i))
            order = range(0, NCH - 1) if i < 2 else range(NCH - 1, 0, -1)
            step = 1 if i < 2 else -1
            for at, c in enumerate(order):
                for a in range(2):
                    p0 = GDK * a
                    ds = side_of(c)[p0:p0 + GDK, a * GDV:(a + 1) * GDV]
                    to = state[p0:p0 + GDK, i, c + step, :]
                    if at == 0:
                        ins = nc.vector.tensor_copy(to, ds)
                    else:
                        ins = nc.vector.scalar_tensor_tensor(to, state[p0:p0 + GDK, i, c, :], dec[p0:p0 + GDK, i, c:c + 1], ds,
                                                             ALU.mult, ALU.add)
                    if at == NCH - 2 and a == 1:
                        dve_mix.inc(ins, ("state", i))
                    else:
                        link(ins)

        for j in range(4):
            nc.vector.tensor_tensor(cv[:, j, :], summed(13 + j), R, ALU.mult).then_inc(unit_read, 1)
            if j == 1:
                states(0)
        states(1)
        act_mix.wait(dve, ("r", 3))
        for j in range(4):
            if j >= 2:
                dve_mix.wait(dve, ("u", j - 2))
            nc.vector.tensor_tensor(mtmp[:, j % 2, :], summed(17 + j), R, ALU.mult).then_inc(unit_read, 1)
            dve.wait_ge(unit_read, n + 18 + j)
            dve_mix.inc(nc.vector.tensor_tensor(cu[:, j, 1:S1 + 1], mtmp[:, j % 2, :], cv[:, j, :], ALU.mult), ("u", j))
            if j == 1:
                states(2)
        states(3)
        for j in range(4):
            act_mix.wait(dve, ("tap", j))
            link(nc.vector.scalar_tensor_tensor(cv[:, j, :], cu[:, j, 0:S1], column("conv_w", (0, 0), j), cv[:, j, :],
                                                ALU.mult, ALU.add))
            link(nc.vector.scalar_tensor_tensor(cv[:, j, :], cu[:, j, 2:S1 + 2], column("conv_w", (0, 2), j), cv[:, j, :],
                                                ALU.mult, ALU.add))
        for j in range(4):
            if j >= 2:
                dve_mix.wait(dve, ("c", j - 2))
            nc.vector.tensor_tensor(mtmp[:, j % 2, :], summed(21 + j), R, ALU.mult).then_inc(unit_read, 1)
            dve.wait_ge(unit_read, n + 22 + j)
            dve_mix.inc(nc.vector.tensor_tensor(cv[:, j, :], mtmp[:, j % 2, :], cv[:, j, :], ALU.mult), ("c", j))
        pe_mix.wait(dve, ("kt", 3))
        dve_mix.inc(nc.vector.memset(att[:, :, :, :], 0.0), "attz")
        dve_mix.wait(dve, "attz")

        def masked(h):
            pe_mix.wait(dve, ("att", h))
            if h >= 2:
                pe_mix.wait(dve, ("o", h - 2))
            for d in range(2):
                mask = const[:, (C_MF, C_MB)[d]:(C_MF, C_MB)[d] + P].bitcast(U32)
                for t in range(4):
                    ins = nc.vector.copy_predicated(att[:, h % 2, d, t * P:(t + 1) * P], mask,
                                                    SIDE[2 * (h % 2) + d][:, t * P:(t + 1) * P])
                    if not (d == 1 and t == 3):
                        link(ins)
            dve_mix.inc(ins, ("att", h))

        def lower(h):
            src = o_gla[:, h % 2, :] if h < 4 else cv[:, h - 4, :]
            dve.wait_ge(x_hi, KD * D_MIXO + MIXO_ORDER.index(h) + 1)
            nc.vector.tensor_tensor(lo(h, 1), src, hi(h, 1).bitcast(F32), ALU.subtract).then_inc(x_lo, 1)

        def normed(h):
            pe_mix.wait(dve, ("osum", h))
            dve_mix.inc(nc.vector.tensor_scalar(ms[:, 0:S1], SIDE[h], 1.0 / GDV, EPS, ALU.mult, ALU.add), ("oms", h))
            act_mix.wait(dve, ("osd", h))
            newton(link, rn[:, 0:S1], ms[:, 0:S1], rt[:, 0:S1], sd[:, 0:S1])
            if h >= 2:
                dve.wait_ge(x_lo, KD * D_MIXO + MIXO_ORDER.index(h - 2) + 1)
            dve_mix.inc(nc.vector.scalar_tensor_tensor(o_gla[:, h % 2, :], PS[h][:, 0, :], column("gla_norm", 0, h), R,
                                                       ALU.mult, ALU.mult), ("oread", h))
            dve_mix.wait(dve, ("oread", h))
            dve_mix.inc(nc.vector.tensor_tensor(o_gla[:, h % 2, :], o_gla[:, h % 2, :], r_act[:, h, :], ALU.mult), ("y", h))
            lower(h)

        masked(0)
        masked(1)
        for j in range(4):
            lower(4 + j)
        masked(2)
        masked(3)
        for h in range(4):
            normed(h)
        dve_out_units(dve, n + W_OUT, S_XAT)

    pe_x.declare(*[("mt", k) for k in range(KD)], "msum", ("s", 0), ("s", 1),
                 *[x for i in range(16) for x in (([("s", i + 2)] if i < 14 else []) + [("t", i)]
                                                  + ([("pv", i // 4 - 1)] if i % 4 == 0 and i else []))], ("pv", 3))
    act_x.declare(*[(a, k) for k in range(KD) for a in ("mhi", "msq")], "msd", ("p", 0), ("p", 1),
                  *[x for i in range(16) for x in ((("tc", i),) if i >= 14 else (("tc", i), ("p", i + 2)))])
    dve_x.declare(*[(a, k) for k in range(KD) for a in ("mlo", "macc")], "mms", "mrn", ("max", 0),
                  *[x for i in range(16) for x in ((("pn", i),) if i == 15 else (("max", i + 1), ("pn", i)))])
    XS = [PS[0][:, 0, 0:MEM], PS[0][:, 1, 0:MEM], PS[1][:, 0, 0:MEM]]
    XT = PS[1][:, 1, 0:MEM]

    def pe_xat(pe):
        n = PHASE["xat"]
        H, L = (lambda k: hi(k, 1)), (lambda k: lo(k, 1))
        MHI, MLO = (lambda k: m_hi[:, k, :]), (lambda k: m_lo[:, k, :])
        pe.wait_ge(x_loaded, 16 * (S1 // P + 1))
        for k in range(KD):
            if k >= 4:
                act_x.wait(pe, ("msq", k - 4))
                dve_x.wait(pe, ("mlo", k - 4))
            for t in range(2):
                ins = nc.tensor.transpose(SIDE[k % 4][:, t * P:(t + 1) * P], mem_in[:, t, k * P:(k + 1) * P], ident)
            pe_x.inc(ins, ("mt", k))
        for j in range(KD):
            pe_unit(pe, n + j, 0, FLAT[n + j], MHI, MLO, [(PS[(n + j) % 4][:, 0, 0:MEM], 0, MEM)],
                    (lambda k: dve_x.wait(pe, ("mlo", k))) if j == 0 else None)
            if j == 0:
                dve_x.wait(pe, ("macc", KD - 1))
                nc.tensor.matmul(SIDE[3][:, 0:MEM], ones, m_acc[:, :], start=True, stop=True)
                for t in range(2):
                    ins = nc.tensor.matmul(SIDE[3][:, MEM + t:MEM + t + 1], m_acc[:, t * P:(t + 1) * P], ones[:, 0:1],
                                           start=True, stop=True)
                pe_x.inc(ins, "msum")
        dve_x.wait(pe, "mrn")
        for j in range(KD):
            m = n + KD + j
            pe.wait_ge(lo_done, m + 1)
            s, hf = m % SPLIT, j // 4
            for kk in range(2):
                k = 2 * (j % 4) + kk
                wh, wl = w_hi[:, s, kk * 512:(kk + 1) * 512], w_lo[:, s, kk * 512:(kk + 1) * 512]
                for t in range(2):
                    xh, xl = m_hi[:, k, t * P:(t + 1) * P], m_lo[:, k, t * P:(t + 1) * P]
                    nc.tensor.matmul(SIDE[2 * hf + t], xh, wh, start=(k == 0), stop=False)
                    nc.tensor.matmul(SIDE[2 * hf + t], xh, wl, start=False, stop=False)
                    ins = nc.tensor.matmul(SIDE[2 * hf + t], xl, wh, start=False, stop=(k == KD - 1))
            ins.then_inc(unit_summed, 1)
        n += 2 * KD
        pe.wait_ge(unit_read, n)
        pe.wait_ge(acc_done, KD * (S_XAT + 1))
        pe_norm(pe, S_XAT, (n + 3) % 4, 1).then_inc(norm_sum, 1)
        for j in range(KD):
            if j == 3:
                pe.wait_ge(norm_ms, S_XAT + 1)
            pe_unit(pe, n + j, 0, FLAT[n + j], H, L, outs_of((n + j) % 4, 1),
                    (lambda k: pe.wait_ge(x_lo, KD * D_XAT + k + 1)) if j == 0 else None)
        n += KD
        pe.wait_ge(unit_read, n)

        def score(i):
            h, t = i // 4, i % 4
            if i >= 3:
                act_x.wait(pe, ("p", i - 3))
            for kk in range(2):
                ins = nc.tensor.matmul(XS[i % 3], xq[:, 2 * h + kk, t * P:(t + 1) * P], xk[:, 2 * h + kk, :],
                                       start=(kk == 0), stop=(kk == 1))
            pe_x.inc(ins, ("s", i))

        def turn(i):
            dve_x.wait(pe, ("pn", i))
            if i:
                act_x.wait(pe, ("tc", i - 1))
            for mt in range(2):
                ins = nc.tensor.transpose(XT[:, mt * P:(mt + 1) * P], xp[:, i % 3, mt * P:(mt + 1) * P], ident)
            pe_x.inc(ins, ("t", i))

        def values(h):
            act_x.wait(pe, ("tc", 4 * h + 3))
            if h >= 2:
                pe.wait_ge(x_lo, KD * D_XATO + 2 * (h - 2) + 2)
            for dt in range(2):
                for mt in range(2):
                    ins = nc.tensor.matmul(PS[2 + h % 2][:, dt, :], xv[:, mt, h * XHD + dt * P:h * XHD + (dt + 1) * P],
                                           xpt[:, h % 2, mt, :], start=(mt == 0), stop=(mt == 1))
            pe_x.inc(ins, ("pv", h))

        score(0)
        score(1)
        for i in range(16):
            if i + 2 < 16:
                score(i + 2)
            turn(i)
            if i % 4 == 0 and i:
                values(i // 4 - 1)
        values(3)
        pe.wait_ge(x_lo, KD * (D_XATO + 1))
        for j in range(KD):
            pe_unit(pe, n + j, 0, FLAT[n + j], H, L, outs_of((n + j) % 4, 1))

    def act_xat(act):
        n = PHASE["xat"]
        for k in range(KD):
            pe_x.wait(act, ("mt", k))
            act_x.inc(nc.scalar.activation(m_hi[:, k, :], SIDE[k % 4][:, 0:MEM], ACT.Identity, scale=G_MEM(k)), ("mhi", k))
            if k >= 2:
                dve_x.wait(act, ("macc", k - 2))
            act_x.inc(nc.scalar.activation(m_sq[:, k % 2, :], SIDE[k % 4][:, 0:MEM], ACT.Square), ("msq", k))
        hi_to(act, n + 2)
        pe_x.wait(act, "msum")
        dve_x.wait(act, "mms")
        act_x.inc(nc.scalar.activation(m_sd[:, :], m_ms[:, :], ACT.Sqrt), "msd")
        hi_to(act, n + 3)
        act_split_all(act, D_XAT, G_XAT, n)
        for j in range(2, 2 * KD):
            hi_to(act, n + j + 2)
        n += 2 * KD
        act_sqrt(act, S_XAT, S1)
        for j in range(KD):
            hi_to(act, n + j + 2)
        n += KD

        def probs(i):
            dve_x.wait(act, ("max", i))
            if i >= 3:
                pe_x.wait(act, ("t", i - 3))
            act_x.inc(nc.scalar.activation(xp[:, i % 3, :], XS[i % 3], ACT.Exp, bias=xst[:, i, 0:1],
                                           accum_out=xst[:, i, 1:2]), ("p", i))

        def turned_copy(i):
            h, t = i // 4, i % 4
            pe_x.wait(act, ("t", i))
            if h >= 2:
                pe_x.wait(act, ("pv", h - 2))
            act_x.inc(nc.scalar.activation(xpt[:, h % 2, :, t * P:(t + 1) * P], XT.rearrange("p (m q) -> p m q", m=2),
                                           ACT.Copy), ("tc", i))

        def upper(h):
            pe_x.wait(act, ("pv", h))
            for dt in range(2):
                nc.scalar.activation(hi(2 * h + dt, 1), PS[2 + h % 2][:, dt, :], ACT.Copy).then_inc(x_hi, 1)

        probs(0)
        probs(1)
        for i in range(16):
            turned_copy(i)
            if i + 2 < 16:
                probs(i + 2)
            if i % 4 == 1 and i > 4:
                upper(i // 4 - 1)
        upper(3)
        act_out_units(act, n, S_FFN2)
        act_split_all(act, D_FFN2, G_FFN2, n + KD)

    def dve_xat(dve, link):
        n = PHASE["xat"]
        for k in range(KD):
            act_x.wait(dve, ("msq", k))
            dve_x.inc(nc.vector.scalar_tensor_tensor(m_lo[:, k, :], SIDE[k % 4][:, 0:MEM], G_MEM(k), m_hi[:, k, :].bitcast(F32),
                                                     ALU.mult, ALU.subtract), ("mlo", k))
            if k == 0:
                dve_x.inc(nc.vector.tensor_copy(m_acc[:, :], m_sq[:, 0, :]), ("macc", k))
            else:
                dve_x.wait(dve, ("macc", k - 1))
                dve_x.inc(nc.vector.tensor_tensor(m_acc[:, :], m_acc[:, :], m_sq[:, k % 2, :], ALU.add), ("macc", k))
        pe_x.wait(dve, "msum")
        dve_x.inc(nc.vector.tensor_scalar(m_ms[:, :], SIDE[3][:, 0:MEM + 2], 1.0 / D, EPS, ALU.mult, ALU.add), "mms")
        act_x.wait(dve, "msd")
        link(nc.vector.reciprocal(m_rn[:, :], m_sd[:, :]))
        link(nc.vector.tensor_tensor(m_rt[:, :], m_rn[:, :], m_rn[:, :], ALU.mult))
        link(nc.vector.scalar_tensor_tensor(m_rt[:, :], m_rt[:, :], -0.5, m_ms[:, :], ALU.mult, ALU.mult))
        dve_x.inc(nc.vector.scalar_tensor_tensor(m_rn[:, :], m_rt[:, :], 1.5, m_rn[:, :], ALU.add, ALU.mult), "mrn")
        dve_x.wait(dve, "mrn")
        dve_split_all(dve, D_XAT, G_XAT)
        for j in range(KD):
            dve.wait_ge(unit_summed, n + j + 1)
            nc.vector.tensor_tensor(xk[:, j, :], PS[(n + j) % 4][:, 0, 0:MEM], m_rn[:, 0:MEM], ALU.mult).then_inc(unit_read, 1)
        for hf in range(2):
            dve.wait_ge(unit_summed, n + KD + 4 * hf + 4)
            for t in range(2):
                for c in range(2):
                    nc.vector.tensor_scalar(xv[:, t, hf * 512 + c * 256:hf * 512 + (c + 1) * 256],
                                            SIDE[2 * hf + t][:, c * 256:(c + 1) * 256], m_rn[:, MEM + t:MEM + t + 1], None,
                                            ALU.mult).then_inc(unit_read, 1)
        n += 2 * KD
        dve_norm(dve, link, S_XAT, (n + 3) % 4, 1)
        for j in range(KD):
            dve.wait_ge(unit_summed, n + j + 1)
            nc.vector.scalar_tensor_tensor(xq[:, j, :], PS[(n + j) % 4][:, 0, :], float(XHD ** -0.5), rn[:, 0:S1], ALU.mult,
                                           ALU.mult).then_inc(unit_read, 1)
        n += KD

        def maximum(i):
            pe_x.wait(dve, ("s", i))
            dve_x.inc(nc.vector.tensor_reduce(xst[:, i, 0:1], XS[i % 3], AX.X, ALU.max, negate=True), ("max", i))

        def scaled(i):
            act_x.wait(dve, ("p", i))
            link(nc.vector.reciprocal(xst[:, i, 2:3], xst[:, i, 1:2]))
            dve_x.inc(nc.vector.tensor_scalar(xp[:, i % 3, :], xp[:, i % 3, :], xst[:, i, 2:3], None, ALU.mult), ("pn", i))

        def lower(h):
            for dt in range(2):
                dve.wait_ge(x_hi, KD * D_XATO + 2 * h + dt + 1)
                nc.vector.tensor_tensor(lo(2 * h + dt, 1), PS[2 + h % 2][:, dt, :], hi(2 * h + dt, 1).bitcast(F32),
                                        ALU.subtract).then_inc(x_lo, 1)

        maximum(0)
        for i in range(16):
            if i + 1 < 16:
                maximum(i + 1)
            scaled(i)
            if i % 4 == 2 and i > 4:
                lower(i // 4 - 1)
        lower(3)
        dve_out_units(dve, n, S_FFN2)
        dve_split_all(dve, D_FFN2, G_FFN2)

    def pe_fin(pe):
        n = PHASE["ffn2"] + 68
        pe.wait_ge(unit_read, n)
        pe_norm(pe, S_FIN, n % 4, 1).then_inc(norm_sum, 1)

    def act_fin(act):
        act_sqrt(act, S_FIN, S1)
        for k in range(KD):
            x_ready.wait(act, ("fin", k))
            act_split(act, D_MLA, k, k, 2, G_PRE[0])
            act_square(act, S_MLA, k, k, X[:, k, :], S2)

    def dve_fin(dve, link):
        dve_norm(dve, link, S_FIN, (PHASE["ffn2"] + 68) % 4, 1)
        for k in range(KD + 1):
            if k < KD:
                x_ready.inc(nc.vector.scalar_tensor_tensor(xt(k, 1), xt(k, 1), G_FIN(k), rn[:, 0:S1], ALU.mult, ALU.mult),
                            ("fin", k))
            if k:
                dve_split(dve, D_MLA, k - 1, 2, G_PRE[0])
                dve_acc(dve, S_MLA, k - 1, k - 1, S2)

    ITEMS = (4, 3, 0, 2, 1)
    KEYS = {j: META + P * j for j in range(5)}
    QROW = {j: max(META + P * (j - 1), 0) for j in range(5)}
    TOK0 = {j: max(META + P * (j - 1), 0) for j in range(5)}
    OFF = {}
    for j in ITEMS:
        OFF[j] = sum(KEYS[i] for i in ITEMS[:ITEMS.index(j)])
    PLACE = {3: PS[1][:, 0, 0:400], 0: PS[1][:, 0, 400:416], 2: PS[1][:, 1, 0:272], 1: PS[1][:, 1, 272:416]}
    GROUPS = ((4,), (3, 0), (2, 1))

    def group_of(j):
        return [g for g in GROUPS if j in g][0]

    def seq(p):
        return [(2 * p + a, j) for a in range(2) for j in ITEMS]

    def pe_pair_order(p):
        o = [("s", 2 * p, j) for j in ITEMS]
        items = seq(p)
        for x, it in enumerate(items):
            o.append(("t",) + it)
            if x in (0, 2, 4):
                o += [("s", 2 * p + 1, j) for j in GROUPS[x // 2]]
            if x:
                o.append(("pv",) + items[x - 1])
        return o + [("pv",) + items[-1]]

    def act_pair_order(p):
        items = seq(p)
        o = [("p",) + items[0], ("p",) + items[1]]
        for x, it in enumerate(items):
            if x + 2 < len(items):
                o.append(("p",) + items[x + 2])
            o += [("tc0",) + it, ("tc",) + it] if it[1] else [("tc",) + it]
            if x == 6:
                o += [("oh", 2 * p, 0), ("oh", 2 * p, 1)]
        return o + [("oh", 2 * p + 1, 0), ("oh", 2 * p + 1, 1)]

    def dve_pair_order(p):
        items = seq(p)
        o = [("kn", p, 0), ("kn", p, 1), ("v", p), ("q", p), ("max",) + items[0], ("max",) + items[1]]
        for x, it in enumerate(items):
            if x + 2 < len(items):
                o.append(("max",) + items[x + 2])
            o.append(("pn",) + it)
            if x == 7:
                o += [("ol", 2 * p, 0), ("ol", 2 * p, 1)]
        return o + [("ol", 2 * p + 1, 0), ("ol", 2 * p + 1, 1)]

    NP_ = MH // 2
    pe_m.declare("sums", "dup", *[x for p in range(NP_) for x in pe_pair_order(p)])
    act_m.declare(*[(a, t) for t in range(5) for a in ("chi", "csq")], "qsd", "kvsd",
                  *[x for p in range(NP_) for x in act_pair_order(p)])
    dve_m.declare(*[(a, t) for t in range(5) for a in ("clo", "cacc")], "kr", "qms", "ct", "kvms", "rkv", "krope",
                  *[x for p in range(NP_) for x in dve_pair_order(p)])

    def latent(t):
        if t < 3:
            return cq_hi[:, t, :], cq_lo[:, t, :], column("mla_q_norm_2", 0, t), acc, t
        return ckv_hi[:, t - 3, :], ckv_lo[:, t - 3, :], column("mla_kv_norm_2", 0, t - 3), r_kv, t - 3

    def two(ap):
        return ap.rearrange("p (c w) -> p c w", c=2)

    def pe_mla(pe):
        n = PHASE["mla"]
        for j in range(6):
            if j == 3:
                pe.wait_ge(norm_ms, S_MLA + 1)
            pe_unit(pe, n + j, 0, FLAT[n + j], lambda k: hi(k, 2), lambda k: lo(k, 2), outs_of((n + j) % 4, 2),
                    (lambda k: pe.wait_ge(x_lo, KD * D_MLA + k + 1)) if j == 0 else None)
            if j == 0:
                pe.wait_ge(unit_read, n)
                pe_norm(pe, S_MLA, (n + 3) % 4, 2).then_inc(norm_sum, 1)
        n += 6
        pe.wait_ge(unit_read, n)
        dve_m.wait(pe, ("cacc", 4))
        for pair, src in ((0, acc), (1, r_kv)):
            for ps, c, w in outs_of(pair, 2):
                nc.tensor.matmul(ps, ones, src[:, c:c + w], start=True, stop=True)
        for j in range(5):
            ins = nc.tensor.matmul(PS[2][:, 0, j:j + 1], r_kv[:, TOK0[j]:TOK0[j] + P], ones[:, 0:1], start=True, stop=True)
        pe_m.inc(ins, "sums")
        dve_m.wait(pe, "kr")
        for ps, c, w in outs_of(3, 2):
            ins = nc.tensor.matmul(ps, const[NOPE:, C_DUP:C_DUP + P], q4[NOPE:, 1, c:c + w], start=True, stop=True)
        pe_m.inc(ins, "dup")
        dve_m.wait(pe, "ct")
        dve_m.wait(pe, "rkv")
        dve_m.wait(pe, "krope")
        for p in range(NP_):
            pe_pair(pe, p, n + 2 * p)
        n += 2 * NP_
        dve_m.wait(pe, ("ol", MH - 1, 1))
        for j in range(KD):
            pe_unit(pe, n + j, 0, FLAT[n + j], lambda k: hi(k, 2), lambda k: lo(k, 2), outs_of((n + j) % 4, 2))

    def pe_pair(pe, p, n):
        last = 2 * p - 1
        if p:
            for j in ITEMS:
                act_m.wait(pe, ("p", last, j))
        pe.wait_ge(lo_done, n + 1)
        s = n % SPLIT
        wh, wl = w_hi[:, s, 0:4 * P].rearrange("p (g m) -> p g m", m=P), w_lo[:, s, 0:4 * P].rearrange("p (g m) -> p g m", m=P)
        for k in range(2):
            for w, x, st, sp_ in ((wh, ckv_hi, k == 0, False), (wh, ckv_lo, False, False), (wl, ckv_hi, False, k == 1)):
                for ps, c, cw in outs_of(0, 2):
                    nc.tensor.matmul(ps, w[:, k, :], x[:, k, c:c + cw], start=st, stop=sp_)
        for j in range(5):
            dst = PS[1][:, 1, 0:P] if j == 0 else PS[1][:, 0, (j - 1) * P:j * P]
            for k in range(2):
                for w, x, st, sp_ in ((wh, ckv_hi, k == 0, False), (wl, ckv_hi, False, False), (wh, ckv_lo, False, k == 1)):
                    ins = nc.tensor.matmul(dst, x[:, k, TOK0[j]:TOK0[j] + P], w[:, 2 + k, :], start=st, stop=sp_)
        ins.then_inc(unit_summed, 1)
        n += 1
        if p:
            act_m.wait(pe, ("tc", last, ITEMS[-1]))
            dve_m.wait(pe, ("ol", last, 1))
        pe.wait_ge(lo_done, n + 1)
        s = n % SPLIT
        for a in range(2):
            for k in range(3):
                c0 = (2 * k + a) * P
                h, l = w_hi[:, s, c0:c0 + P], w_lo[:, s, c0:c0 + P]
                for w, x, st, sp_ in ((h, cq_hi, k == 0, False), (h, cq_lo, False, False), (l, cq_hi, False, k == 2)):
                    for ps, c, cw in outs_of(2 + a, 2):
                        ins = nc.tensor.matmul(ps, w, x[:, k, c:c + cw], start=st, stop=sp_)
        ins.then_inc(unit_summed, 1)
        for key in (("kn", p, 0), ("kn", p, 1), ("v", p), ("q", p)):
            dve_m.wait(pe, key)
        pe.wait_ge(unit_read, n + 1)

        def score(h, j):
            slot = h % 4
            q = q4[:, slot, QROW[j]:QROW[j] + P]
            if h % 2:
                for i in group_of(j):
                    act_m.wait(pe, ("p", h - 1, i))
            if j == 4:
                for c in range(2):
                    nc.tensor.matmul(PS[0][:, c, 0:CW], q, k4[:, slot, c * CW:(c + 1) * CW], start=True, stop=(c == 0))
                dst, m0 = PS[0][:, 1, CW - P:CW], const[:, C_NEG:C_NEG + P]
            else:
                nc.tensor.matmul(PLACE[j], q, k4[:, slot, 0:KEYS[j]], start=True, stop=False)
                dst = PLACE[j] if j == 0 else PLACE[j][:, KEYS[j] - P:KEYS[j]]
                m0 = const[:, C_NEGM:C_NEGM + META] if j == 0 else const[:, C_NEG:C_NEG + P]
            pe_m.inc(nc.tensor.matmul(dst, ident, m0, start=False, stop=True), ("s", h, j))

        items = seq(p)

        def turn(x):
            h, j = items[x]
            dve_m.wait(pe, ("pn", h, j))
            if x:
                act_m.wait(pe, ("tc",) + items[x - 1])
            for i in range(1, j + 1):
                k0 = OFF[j] + TOK0[i]
                nc.tensor.transpose(PS[2][:, 0, (i - 1) * P:i * P], pr[:, h % 2, k0:k0 + P], ident)
            pe_m.inc(nc.tensor.transpose(PS[2][0:META, 1, 0:P], pr[:, h % 2, OFF[j]:OFF[j] + META], ident), ("t", h, j))

        def values(x):
            h, j = items[x]
            act_m.wait(pe, ("tc", h, j))
            p0 = VD * (h % 2)
            nq = META if j == 0 else P
            dst = PS[3][p0:p0 + VD, 1, 0:P] if j == 4 else PS[3][p0:p0 + VD, 0, TOK0[j]:TOK0[j] + nq]
            for i in range(j + 1):
                kk = META if i == 0 else P
                ins = nc.tensor.matmul(dst, v4[0:kk, p % 2, i, p0:p0 + VD], pt[0:kk, x % 2, i, 0:nq], start=(i == 0),
                                       stop=(i == j))
            pe_m.inc(ins, ("pv", h, j))

        for j in ITEMS:
            score(2 * p, j)
        for x in range(len(items)):
            turn(x)
            if x in (0, 2, 4):
                for j in GROUPS[x // 2]:
                    score(2 * p + 1, j)
            if x:
                values(x - 1)
        values(len(items) - 1)

    def prob(h, j):
        return pr[:, h % 2, OFF[j]:OFF[j] + KEYS[j]]

    def scores_of(j):
        return PS[0][:, :, 0:CW] if j == 4 else PLACE[j]

    def act_mla(act):
        n = PHASE["mla"]
        hi_to(act, n + 2)
        act_sqrt(act, S_MLA, S2)
        for t in range(5):
            hi_to(act, n + t + 2)
            act.wait_ge(unit_read, n + t + 1)
            h, _, g, _, _ = latent(t)
            act_m.inc(nc.scalar.activation(h, cq[:, t % 3, :], ACT.Identity, scale=g), ("chi", t))
            if t >= 2:
                dve_m.wait(act, ("cacc", t - 2))
            act_m.inc(nc.scalar.activation(sq[:, t % 2, 0:S2], cq[:, t % 3, :], ACT.Square), ("csq", t))
        hi_to(act, n + 7)
        dve_m.wait(act, "qms")
        act_m.inc(nc.scalar.activation(sd[:, 0:S2], ms[:, 0:S2], ACT.Sqrt), "qsd")
        dve_m.wait(act, "kvms")
        act_m.inc(nc.scalar.activation(sd[:, 0:S2 + 5], ms[:, 0:S2 + 5], ACT.Sqrt), "kvsd")
        n += 6
        for p in range(NP_):
            hi_to(act, n + 2 * p + 3)
            items = seq(p)

            def probs(x):
                h, j = items[x]
                dve_m.wait(act, ("max", h, group_of(j)[-1]))
                if h >= 2:
                    pe_m.wait(act, ("t", h - 2, j))
                d = two(prob(h, j)) if j == 4 else prob(h, j)
                act_m.inc(nc.scalar.activation(d, scores_of(j), ACT.Exp, bias=mst[:, h, j, 0:1], accum_out=mst[:, h, j, 1:2]),
                          ("p", h, j))

            def turned_copy(x):
                h, j = items[x]
                pe_m.wait(act, ("t", h, j))
                if x >= 2:
                    pe_m.wait(act, ("pv",) + items[x - 2])
                nq = P if j else META
                ins = nc.scalar.activation(pt[0:META, x % 2, 0, 0:nq], PS[2][0:META, 1, 0:nq], ACT.Copy)
                if j:
                    act_m.inc(ins, ("tc0", h, j))
                    ins = nc.scalar.activation(pt[:, x % 2, 1:j + 1, :], PS[2][:, 0, 0:j * P].rearrange("p (i q) -> p i q", q=P),
                                               ACT.Copy)
                act_m.inc(ins, ("tc", h, j))

            def upper(h):
                p0 = VD * (h % 2)
                pe_m.wait(act, ("pv", h, ITEMS[-1]))
                act_m.inc(nc.scalar.activation(XHI[p0:p0 + VD, h // 2, 0:400], PS[3][p0:p0 + VD, 0, 0:400], ACT.Copy), ("oh", h, 0))
                act_m.inc(nc.scalar.activation(XHI[p0:p0 + VD, h // 2, 400:S2], PS[3][p0:p0 + VD, 1, 0:P], ACT.Copy), ("oh", h, 1))

            probs(0)
            probs(1)
            for x in range(len(items)):
                if x + 2 < len(items):
                    probs(x + 2)
                turned_copy(x)
                if x == 6:
                    upper(2 * p)
            upper(2 * p + 1)
        n += 2 * NP_
        for m in range(KD):
            hi_to(act, n + m + 2)
            act.wait_ge(unit_read, n + m + 1)
            act_square(act, S_MLAP, m, m, M[:, m, :], S2)

    def dve_mla(dve, link):
        n = PHASE["mla"]
        dve_norm(dve, link, S_MLA, (n + 3) % 4, 2)
        R = rn[:, 0:S2]
        for t in range(5):
            dve.wait_ge(unit_summed, n + t + 1)
            if t >= 3:
                act_m.wait(dve, ("csq", t - 3))
            nc.vector.tensor_tensor(two(cq[:, t % 3, :]), psv((n + t) % 4, 2), two(R), ALU.mult).then_inc(unit_read, 1)
            h, l, g, a, at = latent(t)
            act_m.wait(dve, ("chi", t))
            dve_m.inc(nc.vector.scalar_tensor_tensor(l, cq[:, t % 3, :], g, h.bitcast(F32), ALU.mult, ALU.subtract), ("clo", t))
            act_m.wait(dve, ("csq", t))
            if at == 0:
                dve_m.inc(nc.vector.tensor_copy(a[:, 0:S2], sq[:, t % 2, 0:S2]), ("cacc", t))
            else:
                dve_m.wait(dve, ("cacc", t - 1))
                dve_m.inc(nc.vector.tensor_tensor(a[:, 0:S2], a[:, 0:S2], sq[:, t % 2, 0:S2], ALU.add), ("cacc", t))
        dve.wait_ge(unit_summed, n + 6)
        rope = const[:, C_ROPE:C_ROPE + S2]
        nc.vector.tensor_tensor(two(q4[:, 0, :]), psv((n + 5) % 4, 2), two(R), ALU.mult).then_inc(unit_read, 1)
        dve.wait_ge(unit_read, n + 6)
        dve_m.inc(nc.vector.tensor_tensor(q4[:, 1, :], q4[:, 0, :], rope, ALU.mult), "kr")
        pe_m.wait(dve, "sums")
        dve_m.inc(nc.vector.tensor_scalar(two(ms[:, 0:S2]), psv(0, 2), 1.0 / QL, EPS, ALU.mult, ALU.add), "qms")
        act_m.wait(dve, "qsd")
        newton(link, rn[:, 0:S2], ms[:, 0:S2], rt[:, 0:S2], sd[:, 0:S2])
        dve_m.inc(nc.vector.scalar_tensor_tensor(ct[:, :], rope, MLA_SCALE, rn[:, 0:S2], ALU.mult, ALU.mult), "ct")
        link(nc.vector.tensor_scalar(two(ms[:, 0:S2]), psv(1, 2), 1.0 / KVL, EPS, ALU.mult, ALU.add))
        dve_m.inc(nc.vector.tensor_scalar(ms[:, S2:S2 + 5], PS[2][:, 0, 0:5], 1.0 / KVL, EPS, ALU.mult, ALU.add), "kvms")
        act_m.wait(dve, "kvsd")
        w = S2 + 5
        link(nc.vector.reciprocal(r_kv[:, 0:w], sd[:, 0:w]))
        link(nc.vector.tensor_tensor(rt[:, 0:w], r_kv[:, 0:w], r_kv[:, 0:w], ALU.mult))
        link(nc.vector.scalar_tensor_tensor(rt[:, 0:w], rt[:, 0:w], -0.5, ms[:, 0:w], ALU.mult, ALU.mult))
        dve_m.inc(nc.vector.scalar_tensor_tensor(r_kv[:, 0:w], rt[:, 0:w], 1.5, r_kv[:, 0:w], ALU.add, ALU.mult), "rkv")
        dve_m.wait(dve, "rkv")
        pe_m.wait(dve, "dup")
        for i in range(4):
            ins = nc.vector.tensor_copy(two(k4[NOPE:, i, :]), PS[3][NOPE:, :, 0:CW])
            if i < 3:
                link(ins)
        dve_m.inc(ins, "krope")
        n += 6
        for p in range(NP_):
            dve_pair(dve, link, p, n + 2 * p)
        n += 2 * NP_
        for m in range(KD):
            dve.wait_ge(unit_summed, n + m + 1)
            nc.vector.tensor_copy(two(M[:, m, :]), psv((n + m) % 4, 2)).then_inc(unit_read, 1)
            dve_acc(dve, S_MLAP, m, m, S2)

    def dve_pair(dve, link, p, n):
        dve.wait_ge(unit_summed, n + 1)
        for a in range(2):
            p0 = NOPE * a
            dve_m.inc(nc.vector.tensor_tensor(two(k4[0:NOPE, (2 * p + a) % 4, :]), PS[0][p0:p0 + NOPE, :, 0:CW],
                                              two(r_kv[p0:p0 + NOPE, 0:S2]), ALU.mult), ("kn", p, a))
        dve_m.inc(nc.vector.tensor_scalar(v4[0:META, p % 2, 0, :], PS[1][0:META, 1, 0:P], r_kv[0:META, S2:S2 + 1], None, ALU.mult),
                  ("v", p))
        nc.vector.tensor_tensor(v4[:, p % 2, 1:5, :], PS[1][:, 0, :].rearrange("p (j f) -> p j f", j=4),
                                r_kv[:, S2 + 1:S2 + 5].to_broadcast([P, 4, P]), ALU.mult).then_inc(unit_read, 1)
        dve.wait_ge(unit_summed, n + 2)
        dve_m.inc(nc.vector.tensor_tensor(two(q4[:, (2 * p) % 4, :]), psv(2, 2), two(ct[:, :]), ALU.mult), ("q", p))
        nc.vector.tensor_tensor(two(q4[:, (2 * p + 1) % 4, :]), psv(3, 2), two(ct[:, :]), ALU.mult).then_inc(unit_read, 1)
        items = seq(p)

        def maximum(x):
            h, j = items[x]
            pe_m.wait(dve, ("s", h, group_of(j)[-1]))
            dve_m.inc(nc.vector.tensor_reduce(mst[:, h, j, 0:1], scores_of(j), AX.XY if j == 4 else AX.X, ALU.max, negate=True),
                      ("max", h, j))

        def scaled(x):
            h, j = items[x]
            act_m.wait(dve, ("p", h, j))
            link(nc.vector.reciprocal(mst[:, h, j, 2:3], mst[:, h, j, 1:2]))
            dve_m.inc(nc.vector.tensor_scalar(prob(h, j), prob(h, j), mst[:, h, j, 2:3], None, ALU.mult), ("pn", h, j))

        def lower(h):
            p0 = VD * (h % 2)
            for i, (c0, c1, src) in enumerate(((0, 400, PS[3][p0:p0 + VD, 0, 0:400]), (400, S2, PS[3][p0:p0 + VD, 1, 0:P]))):
                act_m.wait(dve, ("oh", h, i))
                dve_m.inc(nc.vector.tensor_tensor(XLO[p0:p0 + VD, h // 2, c0:c1], src, XHI[p0:p0 + VD, h // 2, c0:c1].bitcast(F32),
                                                  ALU.subtract), ("ol", h, i))

        maximum(0)
        maximum(1)
        for x in range(len(items)):
            if x + 2 < len(items):
                maximum(x + 2)
            scaled(x)
            if x == 7:
                lower(2 * p)
        lower(2 * p + 1)

    pool_mixed = Signal(sem("pool_mixed"))
    pool_evac = Signal(sem("pool_evac"))
    pool_mixed.declare(*range(4))
    pool_evac.declare(*range(0, KD, 2))

    def pool_out(eng, m):
        if m % 2:
            eng.wait_ge(unit_read, PHASE["pool"] + m // 2 + 1)
        else:
            pool_evac.wait(eng, m)

    def pe_pool(pe):
        n = PHASE["pool"]
        pe.wait_ge(unit_read, n)
        pe_norm(pe, S_POOL, n % 4, 2).then_inc(norm_sum, 1)
        for g in range(4):
            pe.wait_ge(lo_done, n + g + 1)
            s = (n + g) % SPLIT
            for k in range(2):
                pe.wait_ge(x_lo, KD * D_POOL + 2 * g + k + 1)
            for mt in range(2):
                m = 2 * g + mt
                if m >= 4:
                    pool_out(pe, m - 4)
                elif m == 0:
                    pe.wait_ge(norm_ms, S_POOL + 1)
                for k in range(2):
                    c0 = k * 256 + mt * P
                    wh, wl = w_hi[:, s, c0:c0 + P], w_lo[:, s, c0:c0 + P]
                    for w, x, st, sp_ in ((wh, hi, k == 0, False), (wh, lo, False, False), (wl, hi, False, k == 1)):
                        for ps, c, cw in outs_of(m % 4, 2):
                            ins = nc.tensor.matmul(ps, w, x(2 * g + k, 2)[:, c:c + cw], start=st, stop=sp_)
            ins.then_inc(unit_summed, 1)

    def act_pool(act):
        n = PHASE["pool"]
        for g in range(4):
            pool_mixed.wait(act, g)
            for k in range(2):
                nc.scalar.activation(hi(2 * g + k, 2), mixed[:, 2 * g + k, :], ACT.Copy).then_inc(x_hi, 1)
        for g in range(4):
            hi_to(act, n + g + 2)
            for mt in range(2):
                m = 2 * g + mt
                pool_out(act, m)
                act_square(act, S_POOLP, m, m, M[:, m, :], S2)

    def dve_pool(dve, link):
        n = PHASE["pool"]
        link(nc.vector.memset(pa[:, :, 0:16], 0.0))
        dve_norm(dve, link, S_POOL, n % 4, 2)
        for g, win in enumerate(WINDOWS):
            for k in (2 * g, 2 * g + 1):
                link(nc.vector.scalar_tensor_tensor(pa[:, k, 16:], X[:, k, :], G_PRE[1](k), rn[:, 0:S2], ALU.mult, ALU.mult))
            a = pa[:, 2 * g:2 * g + 2, :]
            src, span, turn = a, 1, 0
            while span < win:
                dst = (pb, pc)[turn]
                lo_ = 2 * span - 1
                link(nc.vector.tensor_tensor(dst[:, :, lo_:], src[:, :, lo_:], src[:, :, lo_ - span:S2 + 16 - span], ALU.add))
                src, span, turn = dst, 2 * span, 1 - turn
            cor = const[:, C_COR + 16 * g:C_COR + 16 * (g + 1)]
            for k in range(2):
                link(nc.vector.tensor_tensor(src[:, k, 16:32], src[:, k, 16:32], cor, ALU.mult))
            pool_mixed.inc(nc.vector.scalar_tensor_tensor(mixed[:, 2 * g:2 * g + 2, :], src[:, :, 16:], 1.0 / win, a[:, :, 16:],
                                                          ALU.mult, ALU.subtract), g)
            pool_mixed.wait(dve, g)
            for k in (2 * g, 2 * g + 1):
                dve.wait_ge(x_hi, KD * D_POOL + k + 1)
                nc.vector.tensor_tensor(lo(k, 2), mixed[:, k, :], hi(k, 2).bitcast(F32), ALU.subtract).then_inc(x_lo, 1)
        for g in range(4):
            dve.wait_ge(unit_summed, n + g + 1)
            for mt in range(2):
                m = 2 * g + mt
                ins = nc.vector.tensor_scalar(two(M[:, m, :]), psv(m % 4, 2), column("pool_scale_2", 0, m), None, ALU.mult)
                if mt:
                    ins.then_inc(unit_read, 1)
                else:
                    pool_evac.inc(ins, m)
            for mt in range(2):
                dve_acc(dve, S_POOLP, 2 * g + mt, mt, S2)

    @block.sync
    def _(sp):
        sp.dma_start(const[:, :], A["const"]).then_inc(const_in, 16)
        for t in range(S1 // P):
            sp.dma_start(x_in[:, t, :], A["x"][0, t * P:(t + 1) * P, :]).then_inc(x_loaded, 16)
        for _ in walk(sp, sp_unit):
            pass
        for t in range(S1 // P):
            sp.wait_ge(out_ready, t + 1)
            sp.dma_start(out[0, t * P:(t + 1) * P, :], out_tok[:, t, :]).then_inc(out_done, 16)
        sp.wait_ge(out_done, 16 * (S1 // P))

    @block.gpsimd
    def _(pool):
        after = {PHASE[name] + 1: i for i, name in enumerate(("cffn0", "pool", "cffn1"))}

        def step(pool, n, it, u):
            pool_unit(pool, n, it, u)
            if static(it) and n in after:
                pool_post(pool, after[n])

        for _ in walk(pool, step):
            pass
        pool_post(pool, 3)

    @block.scalar
    def _(act):
        act_start(act)
        act_ffn(act, "ffn1", 1, 0, S_FFN1, lambda m, j: (act_split(act, D_MIX, m, j, 1, G_MIX),
                                                         act_square(act, S_MIX, m, j, xt(m, 1), S1)))
        act_mixer(act)
        act_xat(act)
        act_ffn(act, "ffn2", 1, 1, S_FFN2, lambda m, j: act_square(act, S_FIN, m, j, xt(m, 1), S1))
        act_fin(act)
        act_mla(act)
        act_post(act, 0, S_MLAP, S_CF0, D_CF0, G_FPRE[0])
        act_ffn(act, "cffn0", 2, 2, S_CF0, lambda m, j: act_square(act, S_CF0P, m, j, M[:, m, :], S2))
        act_post(act, 1, S_CF0P, S_POOL)
        act_sqrt(act, S_POOL, S2)
        act_pool(act)
        act_post(act, 2, S_POOLP, S_CF1, D_CF1, G_FPRE[1])
        act_ffn(act, "cffn1", 2, 3, S_CF1, lambda m, j: act_square(act, S_CF1P, m, j, M[:, m, :], S2))
        act_post(act, 3, S_CF1P)

    @block.tensor
    def _(pe):
        pe_start(pe)
        pe_ffn(pe, "ffn1", 1, 0, S_FFN1, D_FFN1)
        done = lambda pe: pe.wait_ge(unit_read, NUNITS)
        pe_mixer(pe)
        pe_xat(pe)
        pe_ffn(pe, "ffn2", 1, 1, S_FFN2, D_FFN2)
        pe_fin(pe)
        done = lambda pe: x_ready.wait(pe, ("fin", KD - 1))
        pe_mla(pe)
        pe_post(pe, S_MLAP, PHASE["mla"] + 30)
        done = lambda pe: pe.wait_ge(post_added, KD)
        pe_ffn(pe, "cffn0", 2, 2, S_CF0, D_CF0)
        pe_post(pe, S_CF0P, PHASE["cffn0"] + 68)
        done = lambda pe: pe.wait_ge(post_added, 2 * KD)
        pe_pool(pe)
        pe_post(pe, S_POOLP, PHASE["pool"] + 4)
        done = lambda pe: pe.wait_ge(post_added, 3 * KD)
        pe_ffn(pe, "cffn1", 2, 3, S_CF1, D_CF1)
        pe_post(pe, S_CF1P, PHASE["cffn1"] + 68)
        done = lambda pe: pe.wait_ge(post_added, 4 * KD)
        pe_out(pe, done)

    @block.vector
    def _(dve):
        link = step_link(dve, dve_step)
        dve_start(dve)
        dve_ffn(dve, link, "ffn1", 1, 0, S_FFN1, lambda m, j: (dve_split(dve, D_MIX, m, 1, G_MIX),
                                                               dve_acc(dve, S_MIX, m, j, S1)))
        dve_mixer(dve, link)
        dve_xat(dve, link)
        dve_ffn(dve, link, "ffn2", 1, 1, S_FFN2, lambda m, j: dve_acc(dve, S_FIN, m, j, S1))
        dve_fin(dve, link)
        dve_mla(dve, link)
        dve_post(dve, link, 0, S_MLAP, PHASE["mla"] + 30, G_POST[0], S_CF0, D_CF0, G_FPRE[0])
        dve_ffn(dve, link, "cffn0", 2, 2, S_CF0, lambda m, j: dve_acc(dve, S_CF0P, m, j, S2))
        dve_post(dve, link, 1, S_CF0P, PHASE["cffn0"] + 68, G_FPOST[0], S_POOL)
        dve_pool(dve, link)
        dve_post(dve, link, 2, S_POOLP, PHASE["pool"] + 4, G_POST[1], S_CF1, D_CF1, G_FPRE[1])
        dve_ffn(dve, link, "cffn1", 2, 3, S_CF1, lambda m, j: dve_acc(dve, S_CF1P, m, j, S2))
        dve_post(dve, link, 3, S_CF1P, PHASE["cffn1"] + 68, G_FPOST[1])
        dve_out(dve)


INPUTS = ("x", "mem", "ffn1_norm", "ffn1_w_gate", "ffn1_w_up", "ffn1_w_down", "mix_norm", "w_in", "gate_fwd_w", "gate_fwd_b",
          "gate_bwd_w", "gate_bwd_b", "gla_norm", "conv_w", "conv_b", "w_out", "xattn_norm", "mem_norm", "xattn_w_q",
          "xattn_w_kv", "xattn_w_o", "ffn2_norm", "ffn2_w_gate", "ffn2_w_up", "ffn2_w_down", "final_norm", "meta_tokens_2",
          "norm_mix_pre_2", "norm_mix_post_2", "norm_ffn_pre_2", "norm_ffn_post_2", "mla_w_dqkv_2", "mla_q_norm_2", "mla_w_uq_2",
          "mla_kv_norm_2", "mla_w_ukv_2", "mla_w_o_2", "pool_w_group_2", "pool_scale_2", "ffn_w_up_2", "ffn_conv_w_2",
          "ffn_conv_b_2", "ffn_w_down_2")


def kernel(**inputs):
    import concourse.bacc as bacc
    from concourse.bass_utils import run_bass_kernel_spmd

    nc = bacc.Bacc("TRN2", target_bir_lowering=False, num_devices=1)
    arrays, views = {}, {}
    for name in INPUTS + ("const",):
        a = constant_tile() if name == "const" else np.ascontiguousarray(inputs[name])
        arrays["in_" + name] = a
        views[name] = nc.dram_tensor("in_" + name, a.shape, mybir.dt.from_np(a.dtype), kind="ExternalInput").ap()
    out = nc.dram_tensor("out_0", (1, S1, D), F32, kind="ExternalOutput").ap()
    build(nc, views, out)
    r = run_bass_kernel_spmd(nc, [arrays], core_ids=[0])
    return r.results[0]["out_0"]
```

```python
from contextlib import ExitStack

import numpy as np
import concourse.bass as bass
from concourse import mybir

F32 = mybir.dt.float32
F32R = mybir.dt.float32r
U32 = mybir.dt.uint32
ALU = mybir.AluOpType
ACT = mybir.ActivationFunctionType
AX = mybir.AxisListType

P = 128
D = 1024
KD = D // P
S1 = 512
META = 16
S2 = S1 + META
NEAR = META - 4
S3 = S2 - NEAR
CW = S2 // 2
F = 2816
FT = F // P
PARTS = ((0, 8), (8, 8), (16, 6))
EPS = 1e-6
MEM = 256
XH_HEADS, XHD = 4, 256
GH, GDK, GDV, CHUNK = 4, 64, 128, 64
NCH = S1 // CHUNK
MH, NOPE, ROPE, VD = 16, 64, 32, 64
QL, KVL = 384, 256
MLA_SCALE = float((NOPE + ROPE) ** -0.5)
WINDOWS = (2, 4, 8, 16)
RAW, SPLIT = 4, 2
SLOT = 8 * P
NEG = -float(2 ** 127)

C_ID, C_ONE, C_MF, C_MB, C_NEG, C_NEGM, C_DUP, C_ROPE, C_COR, C_RST = 0, 128, 256, 384, 512, 640, 656, 784, 1312, 1376
C_END = 1888

GROUP_ROWS = (
    (("ffn1_norm", 0, 8), ("mix_norm", 0, 8), ("xattn_norm", 0, 8), ("mem_norm", 0, 8), ("ffn2_norm", 0, 8),
     ("final_norm", None, 8), ("norm_mix_pre_2", 0, 8), ("norm_mix_pre_2", 1, 8), ("norm_mix_post_2", 0, 8),
     ("norm_mix_post_2", 1, 8), ("norm_ffn_pre_2", 0, 8), ("norm_ffn_pre_2", 1, 8), ("norm_ffn_post_2", 0, 8),
     ("norm_ffn_post_2", 1, 8), ("pool_scale_2", 0, 8), ("mla_q_norm_2", 0, 3), ("mla_kv_norm_2", 0, 2)),
    (("gate_fwd_b", 0, 2), ("gate_bwd_b", 0, 2), ("gla_norm", 0, 4), ("conv_w", (0, 0), 4), ("conv_w", (0, 1), 4),
     ("conv_w", (0, 2), 4), ("conv_b", 0, 4)),
    (("ffn_conv_w_2", (0, 0), 44), ("ffn_conv_w_2", (0, 1), 44)),
    (("ffn_conv_w_2", (0, 2), 44), ("ffn_conv_b_2", 0, 44)),
    (("ffn_conv_w_2", (1, 0), 44), ("ffn_conv_w_2", (1, 1), 44)),
    (("ffn_conv_w_2", (1, 2), 44), ("ffn_conv_b_2", 1, 44)),
)


def constant_tile():
    c = np.zeros((P, C_END), np.float32)
    p = np.arange(P)[:, None]
    f = np.arange(P)[None, :]
    c[:, C_ID:C_ID + P] = p == f
    c[:, C_ONE:C_ONE + P] = 1.0
    same = (p // CHUNK) == (f // CHUNK)
    c[:, C_MF:C_MF + P] = same & (p <= f)
    c[:, C_MB:C_MB + P] = same & (p >= f)
    c[:, C_NEG:C_NEG + P] = np.where(f > p, NEG, 0.0)
    c[:, C_NEGM:C_NEGM + META] = np.where(f[:, :META] > p, NEG, 0.0)
    c[:, C_DUP:C_DUP + P] = (p >= NOPE) & (f >= NOPE) & (p % ROPE == f % ROPE)
    half = ROPE // 2
    inv = (1.0 / (np.float32(10000.0) ** (np.arange(0, ROPE, 2, dtype=np.float32) / np.float32(ROPE)))).astype(np.float32)
    ang = inv[:, None] * np.arange(S2, dtype=np.float32)[None, :]
    cos, sin = np.cos(ang).astype(np.float32), np.sin(ang).astype(np.float32)
    c[:NOPE, C_ROPE:C_ROPE + S2] = 1.0
    c[NOPE:NOPE + ROPE, C_ROPE:C_ROPE + S2] = np.concatenate([cos, cos])
    c[NOPE + ROPE:, C_ROPE:C_ROPE + S2] = np.concatenate([-sin, sin])
    for g, w in enumerate(WINDOWS):
        t = np.arange(1, 17, dtype=np.float32)
        c[:, C_COR + 16 * g:C_COR + 16 * (g + 1)] = w / np.minimum(t, w)
    c[:, C_RST:C_RST + S1] = (np.arange(S1) % CHUNK != 0)
    return c


class Signal:

    def __init__(self, sem):
        self.sem = sem
        self.order = {}
        self.done = 0

    def declare(self, *keys):
        for k in keys:
            assert k not in self.order, k
            self.order[k] = len(self.order) + 1

    def at(self, key):
        return self.order[key]

    def inc(self, ins, key):
        self.done += 1
        assert self.order[key] == self.done, (key, self.done)
        ins.then_inc(self.sem, 1)

    def wait(self, eng, key):
        eng.wait_ge(self.sem, self.order[key])


class Unit:

    def __init__(self, kt, cols, src, form=None):
        self.kt, self.cols, self.src, self.form = kt, cols, src, form
        self.raw_cols = cols // P * (NOPE + ROPE) if form == "rotary" else cols


class Loop:

    def __init__(self, count, units):
        assert len(units) == 4
        self.count, self.units = count, units


def build(nc, A, out):
    ctx = ExitStack()
    with ctx:
        program(nc, ctx, A, out)


def program(nc, ctx, A, out):
    def sb(name, shape, dt=F32, scope=ctx):
        return scope.enter_context(nc.sbuf_tensor(name, shape, dt))

    def sem(name):
        return ctx.enter_context(nc.semaphore(name))

    X = sb("X", [P, KD, S2])
    XHI = sb("XHI", [P, KD, S2], F32R)
    XLO = sb("XLO", [P, KD, S2], F32R)
    raw = sb("raw", [P, RAW, SLOT])
    w_hi = sb("w_hi", [P, SPLIT, SLOT], F32R)
    w_lo = sb("w_lo", [P, SPLIT, SLOT], F32R)
    const = sb("const", [P, C_END])
    cols = sb("cols", [P, len(GROUP_ROWS), P])
    acc = sb("acc", [P, S2])
    sq = sb("sq", [P, 2, S2])
    ms = sb("ms", [P, S2 + 8])
    rn = sb("rn", [P, S2 + 8])
    post_t = sb("post_t", [P, 3, S2 + 8])
    rt, sd = post_t[:, 0, :], post_t[:, 1, :]

    ident = const[:, C_ID:C_ID + P]
    ones = const[:, C_ONE:C_ONE + P]

    def column(name, index, tile, n=1):
        for g, group in enumerate(GROUP_ROWS):
            at = 0
            for nm, ix, rows in group:
                if nm == name and ix == index:
                    return cols[:, g, bass.ds(at + tile, n)] if not isinstance(tile, int) else cols[:, g, at + tile:at + tile + n]
                at += rows
        raise KeyError(name)

    start = ExitStack()
    rows = sb("rows", [P, len(GROUP_ROWS), P], scope=start)
    x_in = sb("x_in", [P, S1 // P, D], scope=start)
    meta_in = sb("meta_in", [META, D], scope=start)
    start.close()

    ffn_scope = ExitStack()
    M = sb("M", [P, KD, S2], scope=ffn_scope)
    h_hi = sb("h_hi", [P, 8, S2], F32R, ffn_scope)
    h_lo = sb("h_lo", [P, 8, S2], F32R, ffn_scope)
    g_buf = sb("g_buf", [P, S2 + 2], scope=ffn_scope)
    u_buf = sb("u_buf", [P, S2 + 2], scope=ffn_scope)
    g_conv = sb("g_conv", [P, S2], scope=ffn_scope)
    u_conv = sb("u_conv", [P, S2], scope=ffn_scope)
    g_act = sb("g_act", [P, S2], scope=ffn_scope)
    hid = sb("hid", [P, S2], scope=ffn_scope)
    ffn_scope.close()

    mix = ExitStack()
    q_in = sb("q_in", [P, 4, S1], scope=mix)
    k_in = sb("k_in", [P, 4, S1], scope=mix)
    kst_tok = sb("kst_tok", [P, 4, 4, P], scope=mix)
    v_tok = sb("v_tok", [P, 4, GH * GDV], scope=mix)
    cu = sb("cu", [P, 4, S1 + 2], scope=mix)
    cv = sb("cv", [P, 4, S1], scope=mix)
    r_act = sb("r_act", [P, 4, S1], scope=mix)
    gate_w = sb("gate_w", [32, 512], scope=mix)
    mtmp = sb("mtmp", [P, 2, S1], scope=mix)
    dec = sb("dec", [P, 4, NCH], scope=mix)
    tot = sb("tot", [P, 4, NCH], scope=mix)
    mix_a = ExitStack()
    zz = sb("zz", [32, S1], scope=mix_a)
    t1 = sb("t1", [P, 4, S1], scope=mix_a)
    t2 = sb("t2", [P, 4, S1], scope=mix_a)
    t3 = sb("t3", [P, 4, S1], scope=mix_a)
    qs = sb("qs", [P, 2, S1], scope=mix_a)
    ks = sb("ks", [P, 2, S1], scope=mix_a)
    mix_a.close()
    mix_c = ExitStack()
    state = sb("state", [P, 4, NCH, GDV], scope=mix_c)
    att = sb("att", [P, 2, 2, S1], scope=mix_c)
    o_gla = sb("o_gla", [P, 2, S1], scope=mix_c)
    o_sq = sb("o_sq", [P, 2, S1], scope=mix_c)
    mix_c.close()
    mix.close()

    xat = ExitStack()
    mem_in = sb("mem_in", [P, 2, D], scope=xat)
    m_hi = sb("m_hi", [P, KD, MEM], F32R, xat)
    m_lo = sb("m_lo", [P, KD, MEM], F32R, xat)
    m_acc = sb("m_acc", [P, MEM], scope=xat)
    m_sq = sb("m_sq", [P, 2, MEM], scope=xat)
    m_ms = sb("m_ms", [P, MEM + 2], scope=xat)
    m_sd = sb("m_sd", [P, MEM + 2], scope=xat)
    m_rn = sb("m_rn", [P, MEM + 2], scope=xat)
    m_rt = sb("m_rt", [P, MEM + 2], scope=xat)
    xk = sb("xk", [P, KD, MEM], scope=xat)
    xv = sb("xv", [P, 2, D], scope=xat)
    xq = sb("xq", [P, KD, S1], scope=xat)
    xp = sb("xp", [P, 3, MEM], scope=xat)
    xpt = sb("xpt", [P, 2, 2, S1], scope=xat)
    xst = sb("xst", [P, 16, 4], scope=xat)
    xat.close()

    mla = ExitStack()
    v4 = sb("v4", [P, 2, 5, 4 * VD], scope=mla)
    sb("M_place_mla", [P, KD * S2 - 2 * 5 * 4 * VD], scope=mla)
    cq = sb("cq", [P, 3, S2], scope=mla)
    cq_hi = sb("cq_hi", [P, 3, S2], F32R, mla)
    cq_lo = sb("cq_lo", [P, 3, S2], F32R, mla)
    ckv_hi = sb("ckv_hi", [P, 2, S2], F32R, mla)
    ckv_lo = sb("ckv_lo", [P, 2, S2], F32R, mla)
    ct = sb("ct", [P, S2], scope=mla)
    r_kv = sb("r_kv", [P, S2 + 8], scope=mla)
    q4 = sb("q4", [P, 4, S2], scope=mla)
    k8 = sb("k8", [P, 8, S2], scope=mla)
    pr = sb("pr", [P, 2, 1360], scope=mla)
    pt = sb("pt", [P, 2, 5, P], scope=mla)
    mask_r = sb("mask_r", [P, 2, P], F32R, mla)
    mst = sb("mst", [P, 16, 5, 3], scope=mla)
    mla.close()

    pool_scope = ExitStack()
    sb("M_place_pool", [P, KD, S2], scope=pool_scope)
    pa = sb("pa", [P, KD, S2 + 16], scope=pool_scope)
    pb = sb("pb", [P, 2, S2 + 16], scope=pool_scope)
    pc = sb("pc", [P, 2, S2 + 16], scope=pool_scope)
    pd = sb("pd", [P, 3, 2, S2 + 16], scope=pool_scope)
    mixed = sb("mixed", [P, KD, S2], scope=pool_scope)
    pool_scope.close()

    end = ExitStack()
    sb("M_place_end", [P, KD, S2], scope=end)
    out_tok = sb("out_tok", [P, S1 // P, D], scope=end)
    sb("h_place_end", [P, 16 * S2 - S1 // P * D], scope=end)
    diag = sb("diag", [P, KD, P], scope=end)
    end.close()

    PS = [ctx.enter_context(nc.psum_tensor(f"PS{i}", [P, 2, 512], F32)) for i in range(4)]

    raw_loaded = [sem(f"raw_loaded{s}") for s in range(RAW)]
    hi_done = sem("hi_done")
    lo_done = sem("lo_done")
    unit_summed = sem("unit_summed")
    unit_read = sem("unit_read")
    x_hi = sem("x_hi")
    x_lo = sem("x_lo")
    sq_done = sem("sq_done")
    acc_done = sem("acc_done")
    norm_sum = sem("norm_sum")
    norm_ms = sem("norm_ms")
    norm_sd = sem("norm_sd")
    silu_done = sem("silu_done")
    hid_prod = sem("hid_prod")
    hid_hi = sem("hid_hi")
    hid_lo = sem("hid_lo")
    conv_tap = sem("conv_tap")
    conv_mid = sem("conv_mid")
    conv_done = sem("conv_done")
    post_scaled = sem("post_scaled")
    post_added = sem("post_added")
    const_in = sem("const_in")
    rows_in = sem("rows_in")
    gain_in = sem("gain_in")
    rest_in = sem("rest_in")
    x_loaded = sem("x_loaded")
    meta_loaded = sem("meta_loaded")
    small_in = sem("small_in")
    out_done = sem("out_done")
    dve_step = sem("dve_step")
    act_step = sem("act_step")
    pool_step = sem("pool_step")
    pool_in = sem("pool_in")
    x_ready = Signal(sem("x_ready"))
    cols_ready = sem("cols_ready")
    turned = Signal(sem("turned"))
    pe_mix = Signal(sem("pe_mix"))
    act_mix = Signal(sem("act_mix"))
    dve_mix = Signal(sem("dve_mix"))
    pe_x = Signal(sem("pe_x"))
    act_x = Signal(sem("act_x"))
    dve_x = Signal(sem("dve_x"))
    pe_m = Signal(sem("pe_m"))
    job_summed = Signal(sem("job_summed"))
    job_read = Signal(sem("job_read"))
    act_m = Signal(sem("act_m"))
    dve_m = Signal(sem("dve_m"))
    act_end = Signal(sem("act_end"))
    dve_end = Signal(sem("dve_end"))
    out_ready = sem("out_ready")

    def tiled(w, kt, c0, width):
        return w[0:kt * P, c0:c0 + width].rearrange("(k p) m -> p k m", p=P)

    def by_tile(w, k0, kt):
        return w[k0 * P:(k0 + kt) * P, :].rearrange("(k p) (f m) -> p k f m", p=P, m=P)

    def ffn_units(wg, wu, wd, u_tile0):
        segs = []
        gv, uv = by_tile(wg, 0, KD), by_tile(wu, 0, KD)
        for f0, n in PARTS:
            body = []
            for a in range(2):
                body.append(Unit(KD, P, lambda i, f=f0 + a: gv[:, :, f + 2 * i, :]))
                body.append(Unit(KD, P, lambda i, f=f0 + a + u_tile0: uv[:, :, f + 2 * i, :]))
            segs.append(Loop(n // 2, body))
            dv = by_tile(wd, f0, n)
            segs.append(Loop(2, [Unit(n, P, lambda i, j=j, dv=dv: dv[:, :, j + 4 * i, :]) for j in range(4)]))
        return segs

    def straight(view, kt, width=P, form=None):
        return Unit(kt, width, lambda i, v=view: v, form)

    w_in, w_out = A["w_in"][0], A["w_out"][0]
    O_Q, O_K, O_V, O_R, O_Z = 0, 256, 512, 1024, 1536
    O_BG, O_CG, O_XV = 1568, 2080, 2592
    mix_units = [straight(tiled(w_in, KD, O_Z, P), KD)]
    mix_units += [straight(tiled(w_in, KD, O_Q + P * i, P), KD) for i in range(2)]
    mix_units += [straight(tiled(w_in, KD, O_K + P * i, P), KD) for i in range(2)]
    mix_units += [straight(w_in[2 * P * i:2 * P * (i + 1), O_V:O_V + 512].rearrange("(k p) m -> p k m", p=P), 2, 512)
                  for i in range(4)]
    for o in (O_R, O_CG, O_XV, O_BG):
        mix_units += [straight(tiled(w_in, KD, o + P * i, P), KD) for i in range(4)]
    mix_units += [straight(tiled(w_out, KD, P * i, P), KD) for i in range(KD)]

    w_kv, w_q, w_o = A["xattn_w_kv"][0], A["xattn_w_q"][0], A["xattn_w_o"][0]
    xat_units = [straight(tiled(w_kv, KD, P * i, P), KD) for i in range(KD)]
    for hf in range(2):
        xat_units += [straight(w_kv[2 * P * i:2 * P * (i + 1), D + 512 * hf:D + 512 * (hf + 1)]
                               .rearrange("(k p) m -> p k m", p=P), 2, 512) for i in range(4)]
    xat_units += [straight(tiled(w_q, KD, P * i, P), KD) for i in range(KD)]
    xat_units += [straight(tiled(w_o, KD, P * i, P), KD) for i in range(KD)]

    w_dqkv, w_uq, w_ukv, w_mo = A["mla_w_dqkv_2"][0], A["mla_w_uq_2"][0], A["mla_w_ukv_2"][0], A["mla_w_o_2"][0]
    HW = NOPE + ROPE
    mla_units = [straight(tiled(w_dqkv, KD, P * i, P), KD) for i in range(5)]
    mla_units += [straight(tiled(w_dqkv, KD, QL + KVL - NOPE, HW), KD, P, "rotary")]
    VH = 4
    for p in range(MH // 2):
        if 2 * p % VH == 0:
            mla_units += [straight(tiled(w_ukv, 2, 2 * NOPE * 2 * p, 2 * NOPE * VH), 2, 2 * NOPE * VH, "kv")]
        mla_units += [straight(tiled(w_uq, 3, 2 * HW * p, 2 * HW), 3, 2 * P, "rotary")]
    mla_units += [straight(tiled(w_mo, KD, P * i, P), KD) for i in range(KD)]

    w_pool = A["pool_w_group_2"][0]
    pool_units = [straight(w_pool[g].rearrange("(k p) m -> p k m", p=P), 2, 2 * P) for g in range(4)]

    w_cu, w_cd = A["ffn_w_up_2"], A["ffn_w_down_2"]
    SEGS = []
    PHASE = {}

    def phase(name, segs):
        PHASE[name] = sum(4 * s.count if isinstance(s, Loop) else 1 for s in SEGS)
        SEGS.extend(segs)

    phase("ffn1", ffn_units(A["ffn1_w_gate"][0], A["ffn1_w_up"][0], A["ffn1_w_down"][0], 0))
    phase("mix", mix_units)
    phase("xat", xat_units)
    phase("ffn2", ffn_units(A["ffn2_w_gate"][0], A["ffn2_w_up"][0], A["ffn2_w_down"][0], 0))
    phase("mla", mla_units)
    phase("cffn0", ffn_units(w_cu[0], w_cu[0], w_cd[0], FT))
    phase("pool", pool_units)
    phase("cffn1", ffn_units(w_cu[1], w_cu[1], w_cd[1], FT))
    FLAT = []
    for s in SEGS:
        if isinstance(s, Loop):
            for i in range(s.count):
                FLAT += s.units
        else:
            FLAT.append(s)
    NUNITS = len(FLAT)

    def raw_view(n, u):
        return raw[:, n % RAW, 0:u.kt * u.raw_cols].rearrange("p (k m) -> p k m", k=u.kt)

    def hi_lo_pieces(n, u, dst):
        s, r = n % SPLIT, n % RAW
        if u.form == "kv":
            v = raw[:, r, 0:u.kt * u.cols].rearrange("p (g t m) -> p g t m", t=2, m=NOPE)
            half = u.kt * u.cols // 2
            cut = [slice(t * half, (t + 1) * half) for t in range(2)]
            return [(dst[:, s, c].rearrange("p (g m) -> p g m", m=NOPE), v[:, :, t, :],
                     w_hi[:, s, c].rearrange("p (g m) -> p g m", m=NOPE)) for t, c in enumerate(cut)]
        if u.form is None:
            w = u.kt * u.cols
            return [(dst[:, s, 0:w], raw[:, r, 0:w], w_hi[:, s, 0:w])]
        g = u.kt * u.cols // P
        d = dst[:, s, 0:g * P].rearrange("p (g m) -> p g m", m=P)
        h = w_hi[:, s, 0:g * P].rearrange("p (g m) -> p g m", m=P)
        v = raw[:, r, 0:g * HW].rearrange("p (g m) -> p g m", m=HW)
        half = ROPE // 2
        cuts = ((0, 0, HW), (HW, NOPE + half, half), (HW + half, NOPE, half))
        return [(d[:, :, a:a + w], v[:, :, b:b + w], h[:, :, a:a + w]) for a, b, w in cuts]

    def later(n, it, add):
        return n + add if isinstance(it, int) and it == 0 else 4 * it + (n + add)

    def sp_unit(sp, n, it, u):
        if n >= RAW or not (isinstance(it, int) and it == 0):
            sp.wait_ge(lo_done, later(n, it, 1 - RAW))
        sp.dma_start(raw_view(n, u), u.src(it)).then_inc(raw_loaded[n % RAW], 16)

    def walk(eng, step):
        n = 0
        for s in SEGS:
            if isinstance(s, Loop):
                for j, u in enumerate(s.units):
                    step(eng, n + j, 0, u)
                if s.count > 1:
                    with eng.Fori(1, s.count) as it:
                        for j, u in enumerate(s.units):
                            step(eng, n + j, it, u)
                n += 4 * s.count
            else:
                step(eng, n, 0, s)
                n += 1
            yield n

    def pool_unit(pool, n, it, u):
        pool.wait_ge(hi_done, later(n, it, 1))
        pieces = hi_lo_pieces(n, u, w_lo)
        for i, (d, r, h) in enumerate(pieces):
            ins = nc.gpsimd.tensor_tensor(d, r, h.bitcast(F32), ALU.subtract)
        ins.then_inc(lo_done, 1)

    def act_hi(act, n, it, u):
        act.wait_ge(raw_loaded[n % RAW], 16 * (n // RAW + 1) if isinstance(it, int) and it == 0
                    else 16 * it + 16 * (n // RAW + 1))
        if n >= SPLIT or not (isinstance(it, int) and it == 0):
            act.wait_ge(unit_summed, later(n, it, 1 - SPLIT))
        for d, r, _ in hi_lo_pieces(n, u, w_hi):
            ins = nc.scalar.activation(d, r, ACT.Copy)
        ins.then_inc(hi_done, 1)

    hi_next = [0]

    def hi_to(act, n):
        while hi_next[0] <= min(n, NUNITS - 1):
            act_hi(act, hi_next[0], 0, FLAT[hi_next[0]])
            hi_next[0] += 1

    def psv(pair, blk):
        return PS[pair][:, 0, :] if blk == 1 else PS[pair][:, :, 0:width(blk) // 2]

    def sv(ap, blk):
        return ap if blk == 1 else ap.rearrange("p (c w) -> p c w", c=2)

    def width(blk):
        return (S1, S2, S3)[blk - 1]

    def chunks(blk):
        w = width(blk)
        return ((0, 0, w),) if blk == 1 else ((0, 0, w // 2), (1, w // 2, w // 2))

    def xt(m, blk):
        return X[:, m, S2 - width(blk):S2]

    def hi(m, blk):
        return XHI[:, m, 0:width(blk)]

    def lo(m, blk):
        return XLO[:, m, 0:width(blk)]

    def pe_unit(pe, n, it, u, ahi, alo, outs, ready=None, cols0=0, signal=True, wait=True, ks=None):
        if wait:
            if n >= 4 or not (isinstance(it, int) and it == 0):
                pe.wait_ge(unit_read, later(n, it, -3))
            pe.wait_ge(lo_done, later(n, it, 1))
        s = n % SPLIT
        for k in ks or range(u.kt):
            if ready:
                ready(k)
            c0 = k * u.cols + cols0
            wh, wl = w_hi[:, s, c0:c0 + P], w_lo[:, s, c0:c0 + P]
            for ps, c, w in outs:
                nc.tensor.matmul(ps, wh, ahi(k)[:, c:c + w], start=(k == 0), stop=False)
            for ps, c, w in outs:
                nc.tensor.matmul(ps, wh, alo(k)[:, c:c + w], start=False, stop=False)
            for ps, c, w in outs:
                ins = nc.tensor.matmul(ps, wl, ahi(k)[:, c:c + w], start=False, stop=(k == u.kt - 1))
        if signal:
            ins.then_inc(unit_summed, 1)

    def outs_of(pair, blk):
        return [(PS[pair][:, c, 0:w], c0, w) for c, c0, w in chunks(blk)]

    def pe_norm(pe, s, pair, blk):
        pe.wait_ge(acc_done, KD * s + KD)
        for ps, c, w in outs_of(pair, blk):
            ins = nc.tensor.matmul(ps, ones, acc[:, c:c + w], start=True, stop=True)
        return ins

    def pe_square(pe, s, pair, blk, k):
        pe.wait_ge(sq_done, KD * s + k + 1)
        for ps, c, w in outs_of(pair, blk):
            ins = nc.tensor.matmul(ps, ones, sq[:, k % 2, c:c + w], start=(k == 0), stop=(k == KD - 1))
        ins.then_inc(acc_done, 1)

    def pe_first_unit(pe, n, s, d, blk, free):
        pair = (n + 3) % 4
        if free:
            pe.wait_ge(unit_read, free)

        def ready(k):
            if k:
                pe_square(pe, s, pair, blk, k - 1)
            pe.wait_ge(x_lo, KD * d + k + 1)

        pe_unit(pe, n, 0, FLAT[n], lambda k: hi(k, blk), lambda k: lo(k, blk), outs_of(n % 4, blk), ready)
        pe_square(pe, s, pair, blk, KD - 1)

    def step_link(eng, sm):
        n = [0]

        def link(ins):
            n[0] += 1
            ins.then_inc(sm, 1)
            eng.wait_ge(sm, n[0])
        return link

    block = ctx.enter_context(nc.Block())

    S_FFN1, S_MIX, S_XAT, S_FFN2, S_FIN, S_MLA, S_MLAP, S_CF0, S_CF0P, S_POOL, S_POOLP, S_CF1, S_CF1P = range(13)
    PE_SUMMED = (S_FFN1, S_MLA, S_CF0, S_POOL, S_POOLP, S_CF1)
    D_FFN1, D_MIX, D_MIXO, D_XAT, D_XATO, D_FFN2, D_MLA, D_CF0, D_POOL, D_CF1 = range(10)

    OUT_ORDER = (1, 2, 3, 0)

    turned.declare("gain", "meta", *[("x", k) for k in range(KD)], "cols",
                   ("x_out", 0), ("x_out", 1), ("x_out", 2), "sums", ("x_out", 3), *[("m_out", t) for t in OUT_ORDER])
    act_end.declare(*[("diag", m) for m in range(KD)], ("x_out", 0), "root")
    dve_end.declare(("x_out", 1), "ms", ("x_out", 2), ("x_out", 3))
    x_ready.declare("meta", *[("x", k) for k in range(KD)], *[("fin", k) for k in range(KD)])

    def act_loop(act, count, body):
        body(0)
        if count > 2:
            with act.Fori(1, count - 1) as it:
                body(it)
        if count > 1:
            body(count - 1)

    def run_loop(eng, count, body):
        body(0)
        if count > 1:
            with eng.Fori(1, count) as it:
                body(it)

    def static(it):
        return isinstance(it, int)

    def first(it):
        return isinstance(it, int) and it == 0

    def act_split(act, d, m, j, blk, gain):
        nc.scalar.activation(hi(m, blk), xt(m, blk), ACT.Identity, scale=gain(m)).then_inc(x_hi, 1)

    def act_square(act, s, m, j, src, w):
        if not (static(m) and KD * s + m < 2):
            act.wait_ge(acc_done, m + (KD * s - 1))
        nc.scalar.activation(sq[:, j % 2, 0:w], src, ACT.Square).then_inc(sq_done, 1)

    def dve_split(dve, d, m, blk, gain):
        dve.wait_ge(x_hi, m + (KD * d + 1))
        nc.vector.scalar_tensor_tensor(lo(m, blk), xt(m, blk), gain(m), hi(m, blk).bitcast(F32), ALU.mult,
                                       ALU.subtract).then_inc(x_lo, 1)

    def dve_acc(dve, s, m, j, w):
        dve.wait_ge(sq_done, m + (KD * s + 1))
        if static(m) and m == 0:
            nc.vector.tensor_copy(acc[:, 0:w], sq[:, 0, 0:w]).then_inc(acc_done, 1)
        else:
            dve.wait_ge(acc_done, m + KD * s)
            nc.vector.tensor_tensor(acc[:, 0:w], acc[:, 0:w], sq[:, j % 2, 0:w], ALU.add).then_inc(acc_done, 1)

    def act_sqrt(act, s, w):
        act.wait_ge(norm_ms, s + 1)
        act_rsqrt(act, sd[:, 0:w], ms[:, 0:w]).then_inc(norm_sd, 1)

    act_steps = [0]

    def act_link(act, ins):
        act_steps[0] += 1
        ins.then_inc(act_step, 1)
        act.wait_ge(act_step, act_steps[0])

    def act_rsqrt(act, dst, v):
        act_link(act, nc.scalar.activation(dst, v, ACT.Ln))
        return nc.scalar.activation(dst, dst, ACT.Exp, scale=-0.5)

    def newton(link, r, v, t, s, last=None):
        link(nc.vector.tensor_tensor(t, s, s, ALU.mult))
        link(nc.vector.scalar_tensor_tensor(t, t, -0.5, v, ALU.mult, ALU.mult))
        (last or link)(nc.vector.scalar_tensor_tensor(r, t, 1.5, s, ALU.add, ALU.mult))

    def dve_norm(dve, link, s, pair, blk, rc=0):
        w = width(blk)
        if s in PE_SUMMED:
            dve.wait_ge(acc_done, KD * (s + 1))
        else:
            dve.wait_ge(norm_sum, len([x for x in range(s + 1) if x not in PE_SUMMED]))
        if rc:
            link(nc.vector.tensor_scalar(ms[:, w:w + rc], PS[pair][:, 1, 0:rc], 1.0 / D, EPS, ALU.mult, ALU.add))
        nc.vector.tensor_scalar(sv(ms[:, 0:w], blk), psv(pair, blk), 1.0 / D, EPS, ALU.mult, ALU.add).then_inc(norm_ms, 1)
        dve.wait_ge(norm_sd, s + 1)
        w += rc
        newton(link, rn[:, 0:w], ms[:, 0:w], rt[:, 0:w], sd[:, 0:w])

    def gain_of(name, index):
        return lambda m: column(name, index, m)

    G_FFN1, G_MIX, G_XAT = gain_of("ffn1_norm", 0), gain_of("mix_norm", 0), gain_of("xattn_norm", 0)
    G_MEM, G_FFN2, G_FIN = gain_of("mem_norm", 0), gain_of("ffn2_norm", 0), gain_of("final_norm", None)
    G_PRE = [gain_of("norm_mix_pre_2", i) for i in range(2)]
    G_POST = [gain_of("norm_mix_post_2", i) for i in range(2)]
    G_FPRE = [gain_of("norm_ffn_pre_2", i) for i in range(2)]
    G_FPOST = [gain_of("norm_ffn_post_2", i) for i in range(2)]

    GROUP_SIZES = [sum(r for _, _, r in group) for group in GROUP_ROWS]

    def row_loads():
        loads = []
        for g, group in enumerate(GROUP_ROWS):
            at = 0
            for name, index, n in group:
                v = A[name]
                for ix in ((index,) if isinstance(index, int) else index or ()):
                    v = v[ix]
                loads.append((rows[at:at + n, g, :], v.rearrange("(f p) -> f p", p=P)))
                at += n
        return loads

    ROW_LOADS = row_loads()
    ACT_ROWS = 10

    def act_start(act):
        act.dma_start(*ROW_LOADS[0]).then_inc(gain_in, 16)
        act.dma_start(meta_in[:, :], A["meta_tokens_2"]).then_inc(meta_loaded, 16)
        for to, v in ROW_LOADS[1:ACT_ROWS]:
            act.dma_start(to, v).then_inc(rows_in, 16)
        hi_to(act, 1)
        act.wait_ge(cols_ready, 1)
        for k in range(KD):
            x_ready.wait(act, ("x", k))
            act_split(act, D_FFN1, k, k, 1, G_FFN1)
            act_square(act, S_FFN1, k, k, xt(k, 1), S1)

    def pe_start(pe):
        pe.wait_ge(const_in, 16)
        pe.wait_ge(gain_in, 16)
        turned.inc(nc.tensor.transpose(PS[0][:, 1, 0:KD], rows[0:KD, 0, :], ident[0:KD, 0:KD]), "gain")
        pe.wait_ge(meta_loaded, 16)
        for k in range(KD):
            ins = nc.tensor.transpose(PS[1][:, 1, k * META:(k + 1) * META], meta_in[:, k * P:(k + 1) * P],
                                      ident[0:META, 0:META])
        turned.inc(ins, "meta")
        pe.wait_ge(x_loaded, 16 * (S1 // P))
        for k in range(KD):
            if k >= 4:
                x_ready.wait(pe, ("x", k - 4))
            for t in range(S1 // P):
                ins = nc.tensor.transpose(PS[(k + 2) % 4][:, 0, t * P:(t + 1) * P], x_in[:, t, k * P:(k + 1) * P], ident)
            turned.inc(ins, ("x", k))
        x_ready.wait(pe, ("x", KD - 1))

    def pe_rows(pe):
        pe.wait_ge(rest_in, 16)
        pe.wait_ge(rows_in, 16 * (len(ROW_LOADS) - 1))
        for g, n in enumerate(GROUP_SIZES):
            ins = nc.tensor.transpose(PS[g // 4][:, 1, (g % 4) * P:(g % 4) * P + n], rows[0:n, g, :], ident[0:n, 0:n])
        turned.inc(ins, "cols")

    def dve_rows(dve):
        turned.wait(dve, "cols")
        for g, n in enumerate(GROUP_SIZES):
            n0 = 0 if g else KD
            ins = nc.vector.tensor_copy(cols[:, g, n0:n], PS[g // 4][:, 1, (g % 4) * P + n0:(g % 4) * P + n])
        ins.then_inc(cols_ready, 1)

    def dve_start(dve):
        turned.wait(dve, "gain")
        nc.vector.tensor_copy(cols[:, 0, 0:KD], PS[0][:, 1, 0:KD]).then_inc(cols_ready, 1)
        dve.wait_ge(cols_ready, 1)
        turned.wait(dve, "meta")
        x_ready.inc(nc.vector.tensor_copy(X[:, :, 0:META], PS[1][:, 1, 0:KD * META].rearrange("p (k t) -> p k t", k=KD)),
                    "meta")
        for k in range(KD):
            turned.wait(dve, ("x", k))
            x_ready.inc(nc.vector.tensor_copy(xt(k, 1), PS[(k + 2) % 4][:, 0, :]), ("x", k))
        for k in range(KD):
            dve_split(dve, D_FFN1, k, 1, G_FFN1)

    EARLY = 3

    def pe_ffn(pe, name, blk, inv, s, d):
        n = PHASE[name]
        for pi, (f0, nt) in enumerate(PARTS):
            def up(it, n=n, pi=pi):
                for j in range(4):
                    begin = first(it) and pi == 0
                    if begin and j == 0 and s in PE_SUMMED:
                        pe_first_unit(pe, n, s, d, blk, n)
                        continue
                    ready = None
                    if begin and j == 0:
                        ready = lambda k: pe.wait_ge(x_lo, KD * d + k + 1)
                    if begin and j == 3:
                        pe.wait_ge(norm_ms, s + 1)
                    pe_unit(pe, n + j, it, FLAT[n + j], lambda k: hi(k, blk), lambda k: lo(k, blk),
                            outs_of((n + j) % 4, blk), ready)
                    if begin and j == 0:
                        if n:
                            pe.wait_ge(unit_read, n)
                        pe_norm(pe, s, (n + 3) % 4, blk).then_inc(norm_sum, 1)
                if first(it) and pi == 0 and n == 0:
                    pe_rows(pe)
            run_loop(pe, nt // 2, up)
            n += 2 * nt

            def down(it, n=n, f0=f0, nt=nt):
                steps = [(j, 0, nt) for j in range(4)]
                if first(it) and blk > 1:
                    steps[0:2] = [(0, 0, nt - 1), (1, 0, EARLY), (0, nt - 1, nt), (1, EARLY, nt)]
                for j, k0, k1 in steps:
                    ready = None
                    if first(it) and j == 0:
                        ready = lambda k: pe.wait_ge(hid_lo, inv * FT + f0 + k + 1)
                    pe_unit(pe, n + j, it, FLAT[n + j], lambda k: h_hi[:, k, 0:width(blk)],
                            lambda k: h_lo[:, k, 0:width(blk)], outs_of((n + j) % 4, blk), ready,
                            signal=k1 == nt, wait=k0 == 0, ks=range(k0, k1))
            run_loop(pe, 2, down)
            n += KD

    def act_ffn(act, name, blk, inv, s, after):
        n = PHASE[name]
        w = width(blk)
        cb = (inv - 2) * FT
        for pi, (f0, nt) in enumerate(PARTS):
            count = nt // 2

            def look(it, n, j, count):
                if static(it):
                    if n + j + 2 + 4 * it < NUNITS:
                        act_hi(act, n + j + 2, it, FLAT[n + j + 2 + 4 * it])
                else:
                    act_hi(act, n + j + 2, it, FLAT[n + (j + 2) % 4])

            def up(it, n=n, pi=pi, f0=f0, count=count):
                for a in range(2):
                    g = (inv * FT + f0 + a) + 2 * it
                    soon = blk > 1 and first(it) and pi == 0 and a == 0
                    look(it, n, 2 * a, count)
                    if first(it) and pi == 0 and a == 0:
                        act_sqrt(act, s, w)
                    act.wait_ge(unit_read, later(n, it, 2 * a + 1))
                    if blk > 1:
                        f = (f0 + a) + 2 * it
                        nc.scalar.activation(g_conv[:, 0:w], g_buf[:, 2:2 + w], ACT.Identity, scale=tap(inv - 2, 2, f),
                                             bias=tap(inv - 2, 3, f)).then_inc(conv_tap, 1)
                        if soon:
                            look(it, n, 2 * a + 1, count)
                        act.wait_ge(conv_done, (2 * (cb + f0 + a) + 1) + 4 * it)
                        nc.scalar.activation(g_act[:, 0:w], g_conv[:, 0:w], ACT.Silu).then_inc(silu_done, 1)
                    else:
                        nc.scalar.activation(g_act[:, 0:w], g_buf[:, 0:w], ACT.Silu).then_inc(silu_done, 1)
                    if not soon:
                        look(it, n, 2 * a + 1, count)
                    if blk > 1:
                        act.wait_ge(unit_read, later(n, it, 2 * a + 2))
                        nc.scalar.activation(u_conv[:, 0:w], u_buf[:, 2:2 + w], ACT.Identity, scale=tap(inv - 2, 2, f + FT),
                                             bias=tap(inv - 2, 3, f + FT)).then_inc(conv_tap, 1)
                    act.wait_ge(hid_prod, g + 1)
                    nc.scalar.activation(h_hi[:, a + 2 * it, 0:w], hid[:, 0:w], ACT.Copy).then_inc(hid_hi, 1)
            act_loop(act, count, up)
            n += 2 * nt

            def down(it, n=n, pi=pi):
                for j in range(4):
                    look(it, n, j, 2)
                    if pi == len(PARTS) - 1:
                        act.wait_ge(unit_read, later(n, it, j + 1))
                        after(j + 4 * it, j)
            act_loop(act, 2, down)
            n += KD
        hi_next[0] = n + 2

    def tap(layer, j, f):
        if j < 3:
            return column("ffn_conv_w_2", (layer, j), f)
        return column("ffn_conv_b_2", layer, f)

    def dve_ffn(dve, link, name, blk, inv, s, after):
        n = PHASE[name]
        w = width(blk)
        cb = (inv - 2) * FT
        if blk > 1:
            link(nc.vector.memset(g_buf[:, 0:2], 0.0))
            link(nc.vector.memset(u_buf[:, 0:2], 0.0))
        dve_norm(dve, link, s, (n + 3) % 4, blk)
        r = sv(rn[:, 0:w], blk)
        n_down = None
        for pi, (f0, nt) in enumerate(PARTS):
            def up(it, n=n, f0=f0):
                for a in range(2):
                    g = (inv * FT + f0 + a) + 2 * it
                    f = (f0 + a) + 2 * it
                    for b, (buf, cv_) in enumerate(((g_buf, g_conv), (u_buf, u_conv))):
                        m = n + 2 * a + b
                        dst = buf[:, 2:2 + w] if blk > 1 else buf[:, 0:w]
                        dve.wait_ge(unit_summed, later(m, it, 1))
                        nc.vector.tensor_tensor(sv(dst, blk), psv(m % 4, blk), r, ALU.mult).then_inc(unit_read, 1)
                        if blk > 1:
                            ci = (2 * (cb + f0 + a) + b + 1) + 4 * it
                            ft = f + FT if b else f
                            dve.wait_ge(conv_tap, ci)
                            nc.vector.scalar_tensor_tensor(cv_[:, 0:w], buf[:, 1:1 + w], tap(inv - 2, 1, ft), cv_[:, 0:w],
                                                           ALU.mult, ALU.add).then_inc(conv_mid, 1)
                            dve.wait_ge(conv_mid, ci)
                            nc.vector.scalar_tensor_tensor(cv_[:, 0:w], buf[:, 0:w], tap(inv - 2, 0, ft), cv_[:, 0:w],
                                                           ALU.mult, ALU.add).then_inc(conv_done, 1)
                    up_src = u_conv if blk > 1 else u_buf
                    if blk > 1:
                        dve.wait_ge(conv_done, (2 * (cb + f0 + a) + 2) + 4 * it)
                    else:
                        dve.wait_ge(unit_read, later(n, it, 2 * a + 2))
                    dve.wait_ge(silu_done, g + 1)
                    nc.vector.tensor_tensor(hid[:, 0:w], g_act[:, 0:w], up_src[:, 0:w], ALU.mult).then_inc(hid_prod, 1)
                    dve.wait_ge(hid_hi, g + 1)
                    nc.vector.tensor_tensor(h_lo[:, a + 2 * it, 0:w], hid[:, 0:w], h_hi[:, a + 2 * it, 0:w].bitcast(F32),
                                            ALU.subtract).then_inc(hid_lo, 1)
                if first(it) and n == 0:
                    dve_rows(dve)
            run_loop(dve, nt // 2, up)
            n += 2 * nt

            def down(it, n=n, pi=pi, n_down=n_down):
                for j in range(4):
                    m = j + 4 * it
                    dve.wait_ge(unit_summed, later(n, it, j + 1))
                    ps = psv((n + j) % 4, blk)
                    if pi:
                        dve.wait_ge(unit_read, later(n_down, it, j + 1))
                    if blk == 1:
                        nc.vector.scalar_tensor_tensor(xt(m, 1), ps, 0.5, xt(m, 1), ALU.mult, ALU.add).then_inc(unit_read, 1)
                    elif pi == 0:
                        nc.vector.tensor_copy(sv(M[:, m, 0:w], blk), ps).then_inc(unit_read, 1)
                    else:
                        nc.vector.tensor_tensor(sv(M[:, m, 0:w], blk), ps, sv(M[:, m, 0:w], blk), ALU.add).then_inc(unit_read, 1)
                    if pi == len(PARTS) - 1:
                        after(m, j)
            run_loop(dve, 2, down)
            n_down = n
            n += KD

    def pe_post(pe, s, n):
        pe.wait_ge(unit_read, n)
        pe_norm(pe, s, n % 4, 2).then_inc(norm_sum, 1)

    def dve_post(dve, link, i, s, n, gain, d_next=None, g_next=None, blk_next=2):
        dve_norm(dve, link, s, n % 4, 2)
        for k in range(KD + 2):
            if k < KD:
                if k >= 3:
                    dve.wait_ge(post_added, KD * i + k - 2)
                nc.vector.scalar_tensor_tensor(post_t[:, k % 3, 0:S2], M[:, k, :], gain(k), rn[:, 0:S2], ALU.mult,
                                               ALU.mult).then_inc(post_scaled, 1)
            if k >= 2 and d_next is not None:
                dve_split(dve, d_next, k - 2, blk_next, g_next)

    def pool_post(pool, i):
        for k in range(KD):
            pool.wait_ge(post_scaled, KD * i + k + 1)
            nc.gpsimd.tensor_tensor(X[:, k, :], X[:, k, :], post_t[:, k % 3, 0:S2], ALU.add).then_inc(post_added, 1)

    def act_post(act, i, s, s_next, d_next=None, g_next=None, blk_next=2):
        act_sqrt(act, s, S2)
        for k in range(KD):
            act.wait_ge(post_added, KD * i + k + 1)
            if d_next is not None:
                act_split(act, d_next, k, k, blk_next, g_next)
            act_square(act, s_next, k, k, xt(k, blk_next), width(blk_next))

    def pe_out(pe, s, n):
        def turn_x(t):
            for k in range(KD):
                ins = nc.tensor.transpose(PS[pair_of(t)][:, k // 4, (k % 4) * P:(k % 4 + 1) * P],
                                          X[:, k, META + t * P:META + (t + 1) * P], ident)
            turned.inc(ins, ("x_out", t))

        pe.wait_ge(post_added, 3 * KD)
        pe.wait_ge(unit_read, n - 1)
        for t in range(3):
            turn_x(t)
        act_end.wait(pe, ("x_out", 0))
        pe.wait_ge(acc_done, KD * s + KD)
        for t in range(S1 // P):
            ins = nc.tensor.matmul(PS[0][:, 0, t:t + 1], acc[:, TOK_END[t]:TOK_END[t] + P], ones[:, 0:1],
                                   start=True, stop=True)
        turned.inc(ins, "sums")
        pe.wait_ge(unit_read, n)
        turn_x(3)
        act_end.wait(pe, ("diag", KD - 1))
        for t in OUT_ORDER:
            if t:
                dve_end.wait(pe, ("x_out", t))
            else:
                dve_end.wait(pe, "ms")
            for k in range(KD):
                ins = nc.tensor.matmul(PS[pair_of(t)][:, k // 4, (k % 4) * P:(k % 4 + 1) * P],
                                       M[:, k, TOK_END[t]:TOK_END[t] + P], diag[:, k, :], start=True, stop=True)
            turned.inc(ins, ("m_out", t))

    TOK_END = [META - NEAR + t * P for t in range(S1 // P)]

    def pair_of(t):
        return (0, 1, 3, 2)[t]

    def act_diag(act, m, gain):
        act_end.inc(nc.scalar.activation(diag[:, m, :], ident, ACT.Identity, scale=gain(m)), ("diag", m))

    def by_half(ap):
        return ap.rearrange("p (c w) -> p c w", c=2)

    def act_out(act):
        turned.wait(act, ("x_out", 0))
        act_end.inc(nc.scalar.activation(by_half(out_tok[:, 0, :]), PS[pair_of(0)][:, :, :], ACT.Copy), ("x_out", 0))
        dve_end.wait(act, "ms")
        act_end.inc(act_rsqrt(act, sd[:, 0:S1 // P], ms[:, 0:S1 // P]), "root")

    def dve_out(dve, link):
        nt = S1 // P
        for t in (1, 2, 3):
            turned.wait(dve, ("x_out", t))
            dve_end.inc(nc.vector.tensor_copy(by_half(out_tok[:, t, :]), PS[pair_of(t)][:, :, :]), ("x_out", t))
            if t == 1:
                turned.wait(dve, "sums")
                dve_end.inc(nc.vector.tensor_scalar(ms[:, 0:nt], PS[0][:, 0, 0:nt], 1.0 / D, EPS, ALU.mult, ALU.add), "ms")
        act_end.wait(dve, "root")
        newton(link, rn[:, 0:nt], ms[:, 0:nt], rt[:, 0:nt], sd[:, 0:nt])
        dve_end.wait(dve, ("x_out", 3))
        for t in OUT_ORDER:
            turned.wait(dve, ("m_out", t))
            nc.vector.scalar_tensor_tensor(by_half(out_tok[:, t, :]), PS[pair_of(t)][:, :, :], rn[:, t:t + 1],
                                           by_half(out_tok[:, t, :]), ALU.mult, ALU.add).then_inc(out_ready, 1)

    pe_mix.declare("lg", *[("kt", i) for i in range(4)], *[("ds", i) for i in range(4)],
                   ("att", 0), ("att", 1), ("o", 0), ("att", 2), ("o", 1), ("att", 3),
                   ("osum", 0), ("o", 2), ("osum", 1), ("o", 3), ("osum", 2), ("osum", 3))
    act_mix.declare("abs", "exp", "ln", "eq", "es", "ek", *[("r", j) for j in range(4)], *[("ktc", i) for i in range(4)],
                    *[("tap", j) for j in range(4)],
                    ("osq", 0), ("osq", 1), ("osd", 0), ("osq", 2), ("osd", 1), ("osq", 3), ("osd", 2), ("osd", 3))
    dve_mix.declare("gz", *[("min", i) for i in range(4)], "scan", "diff", ("qin", 0), ("qin", 1), ("kst", 0), ("kst", 1),
                    ("kin", 0), ("kin", 1), ("state", 0), ("state", 1),
                    ("u", 0), ("u", 1), ("state", 2), ("u", 2), ("u", 3), ("state", 3),
                    "attz", ("att", 0), ("att", 1), ("c", 0), ("c", 1), ("att", 2), ("c", 2), ("att", 3),
                    ("oms", 0), ("oread", 0), ("y", 0), ("c", 3), ("oms", 1), ("oms", 2), ("oread", 1), ("y", 1), ("oms", 3),
                    ("oread", 2), ("y", 2), ("oread", 3), ("y", 3))
    W_OUT = 25
    SIDE = [PS[i][:, 1, :] for i in range(4)]
    MIXO_ORDER = [4, 5, 6, 7, 0, 1, 2, 3]

    def side_of(c):
        at = c // 2
        return SIDE[2 * (c % 2) + at // 2][:, at % 2 * 256:(at % 2 + 1) * 256]

    def pe_mixer(pe):
        n = PHASE["mix"]
        H, L = (lambda k: hi(k, 1)), (lambda k: lo(k, 1))

        def unit(j, ready=None):
            pe_unit(pe, n + j, 0, FLAT[n + j], H, L, outs_of((n + j) % 4, 1), ready)

        unit(0, lambda k: pe.wait_ge(x_lo, KD * D_MIX + k + 1))
        pr_ = (n + 3) % 4
        pe.wait_ge(unit_read, n)
        pe_norm(pe, S_MIX, pr_, 1)
        for t in range(4):
            ins = nc.tensor.matmul(PS[pr_][:, 1, t:t + 1], acc[:, t * P:(t + 1) * P], ones[:, 0:1], start=True, stop=True)
        ins.then_inc(norm_sum, 1)
        unit(1)
        unit(2)
        pe.wait_ge(norm_ms, S_MIX + 1)
        pe.wait_ge(unit_read, n + 1)
        pe.wait_ge(small_in, 32)
        for i in range(4):
            ins = nc.tensor.matmul(SIDE[i], gate_w[:, i * P:(i + 1) * P], zz[:, :], start=True, stop=True)
        pe_mix.inc(ins, "lg")
        unit(3)
        unit(4)
        act_mix.wait(pe, "abs")
        dve_mix.wait(pe, ("min", 3))
        for i in range(4):
            m = n + 5 + i
            pe.wait_ge(lo_done, m + 1)
            s = m % SPLIT
            for kk in range(2):
                k = 2 * i + kk
                wh, wl = w_hi[:, s, kk * 512:(kk + 1) * 512], w_lo[:, s, kk * 512:(kk + 1) * 512]
                for t in range(4):
                    xh, xl = H(k)[:, t * P:(t + 1) * P], L(k)[:, t * P:(t + 1) * P]
                    nc.tensor.matmul(SIDE[t], xh, wh, start=(k == 0), stop=False)
                    nc.tensor.matmul(SIDE[t], xh, wl, start=False, stop=False)
                    ins = nc.tensor.matmul(SIDE[t], xl, wh, start=False, stop=(k == KD - 1))
            ins.then_inc(unit_summed, 1)
        for j in range(4):
            unit(9 + j)
        pe.wait_ge(unit_read, n + 9)
        dve_mix.wait(pe, ("kst", 1))
        for i in range(4):
            for t in range(4):
                ins = nc.tensor.transpose(SIDE[i][:, t * P:(t + 1) * P], t3[:, i, t * P:(t + 1) * P], ident)
            pe_mix.inc(ins, ("kt", i))
        for j in range(4):
            for jj in range(2 if j < 4 else 0):
                unit(13 + 2 * j + jj)
            if j == 0:
                act_mix.wait(pe, ("ktc", 3))
            else:
                dve_mix.wait(pe, ("state", j - 1))
            for c in (range(0, NCH - 1) if j < 2 else range(1, NCH)):
                p0 = CHUNK * (c % 2)
                ins = nc.tensor.matmul(side_of(c), kst_tok[p0:p0 + CHUNK, j, c // 2, :],
                                       v_tok[p0:p0 + CHUNK, c // 2, (j % 2) * 256:(j % 2 + 1) * 256], start=True, stop=True)
            pe_mix.inc(ins, ("ds", j))
        dve_mix.wait(pe, ("kin", 1))

        def scores(h):
            p0 = GDK * (h % 2)
            if h < 2:
                dve_mix.wait(pe, ("state", 3))
            else:
                dve_mix.wait(pe, ("att", h - 2))
            for d in range(2):
                i = 2 * d + h // 2
                for t in range(4):
                    ins = nc.tensor.matmul(SIDE[2 * (h % 2) + d][:, t * P:(t + 1) * P], k_in[p0:p0 + GDK, i, t * P:(t + 1) * P],
                                           q_in[p0:p0 + GDK, i, t * P:(t + 1) * P], start=True, stop=True)
            pe_mix.inc(ins, ("att", h))

        def output(h):
            p0 = GDK * (h % 2)
            pe.wait_ge(unit_read, n + 22 + h)
            dve_mix.wait(pe, ("att", h))
            bank = PS[(n + 21 + h) % 4][:, 0, :]
            for t in range(4):
                o = bank[:, t * P:(t + 1) * P]
                v = v_tok[:, t, h * GDV:(h + 1) * GDV]
                nc.tensor.matmul(o, v, att[:, h % 2, 0, t * P:(t + 1) * P], start=True, stop=False)
                pieces = [(0, 2 * t), (0, 2 * t + 1), (1, 2 * t), (1, 2 * t + 1)]
                pieces = [(d, c) for d, c in pieces if not (d == 0 and c == 0) and not (d == 1 and c == NCH - 1)]
                for d, c in pieces:
                    i = 2 * d + h // 2
                    nc.tensor.matmul(bank[:, c * CHUNK:(c + 1) * CHUNK], state[p0:p0 + GDK, i, c, :],
                                     q_in[p0:p0 + GDK, i, c * CHUNK:(c + 1) * CHUNK], start=False, stop=False)
                ins = nc.tensor.matmul(o, v, att[:, h % 2, 1, t * P:(t + 1) * P], start=False, stop=True)
            pe_mix.inc(ins, ("o", h))

        def output_norm(h):
            act_mix.wait(pe, ("osq", h))
            dve_mix.wait(pe, ("att", 2 if h < 2 else 3))
            pe_mix.inc(nc.tensor.matmul(SIDE[h], ones, osq[h], start=True, stop=True), ("osum", h))

        scores(0)
        scores(1)
        unit(21)
        unit(22)
        output(0)
        scores(2)
        unit(23)
        output(1)
        scores(3)
        output_norm(0)
        unit(24)
        output(2)
        output_norm(1)
        output(3)
        output_norm(2)
        output_norm(3)
        for j in range(KD):
            m = n + W_OUT + j
            if j < 4:
                dve_mix.wait(pe, ("oread", j))
            pe_unit_order(pe, m, H, L, 1, lambda at: pe.wait_ge(x_lo, KD * D_MIXO + at + 1) if j == 0 else None)

    def pe_unit_order(pe, n, ahi, alo, blk, ready):
        u = FLAT[n]
        pe.wait_ge(unit_read, n - 3)
        pe.wait_ge(lo_done, n + 1)
        s = n % SPLIT
        for at, k in enumerate(MIXO_ORDER):
            ready(at)
            wh, wl = w_hi[:, s, k * P:(k + 1) * P], w_lo[:, s, k * P:(k + 1) * P]
            for ps, c, w in outs_of(n % 4, blk):
                nc.tensor.matmul(ps, wh, ahi(k)[:, c:c + w], start=(at == 0), stop=False)
                nc.tensor.matmul(ps, wh, alo(k)[:, c:c + w], start=False, stop=False)
                ins = nc.tensor.matmul(ps, wl, ahi(k)[:, c:c + w], start=False, stop=(at == u.kt - 1))
        ins.then_inc(unit_summed, 1)

    osq = [o_sq[:, h % 2, :] for h in range(4)]
    OMS = [ms[:, 0:S1], ms[:, 0:S1], att[:, 0, 0, :], att[:, 1, 0, :]]
    OSD = [sd[:, 0:S1], sd[:, 0:S1], att[:, 0, 1, :], att[:, 1, 1, :]]

    def act_mixer(act):
        n = PHASE["mix"]
        hi_to(act, n + 2)
        dve_mix.wait(act, "gz")
        act.dma_start(gate_w[0:16, 0:256], A["gate_fwd_w"][0]).then_inc(small_in, 16)
        act.dma_start(gate_w[16:32, 256:512], A["gate_bwd_w"][0]).then_inc(small_in, 16)
        act_sqrt(act, S_MIX, S1 + 4)
        hi_to(act, n + 4)
        pe_mix.wait(act, "lg")
        link = lambda ins: act_link(act, ins)
        gb = [column("gate_fwd_b" if i < 2 else "gate_bwd_b", 0, i % 2) for i in range(4)]
        for i in range(3):
            dve_mix.wait(act, ("min", i))
            link(nc.scalar.activation(t1[:, i, :], SIDE[i], ACT.Abs, bias=gb[i]))
        dve_mix.wait(act, ("min", 3))
        act_mix.inc(nc.scalar.activation(t1[:, 3, :], SIDE[3], ACT.Abs, bias=gb[3]), "abs")
        act_mix.wait(act, "abs")
        act_mix.inc(nc.scalar.activation(t1[:, :, :], t1[:, :, :], ACT.Exp, scale=-1.0), "exp")
        act_mix.wait(act, "exp")
        act_mix.inc(nc.scalar.activation(t1[:, :, :], t1[:, :, :], ACT.Ln, bias=1.0), "ln")
        hi_to(act, n + 6)
        dve_mix.wait(act, "scan")
        act_mix.inc(nc.scalar.activation(t3[:, :, :], t1[:, :, :], ACT.Exp, scale=1.0 / 16), "eq")
        hi_to(act, n + 7)
        dve_mix.wait(act, "diff")
        link(nc.scalar.activation(dec[:, :, :], tot[:, :, :], ACT.Exp, scale=1.0 / 16))
        act_mix.inc(nc.scalar.activation(t2[:, :, :], t2[:, :, :], ACT.Exp, scale=1.0 / 16), "es")
        act_mix.wait(act, "eq")
        act_mix.inc(nc.scalar.activation(t1[:, :, :], t1[:, :, :], ACT.Exp, scale=-1.0 / 16), "ek")
        hi_to(act, n + 10)
        for j in range(4):
            hi_to(act, n + 9 + j + 2)
            act.wait_ge(unit_read, n + 9 + j + 1)
            act_mix.inc(nc.scalar.activation(r_act[:, j, :], mtmp[:, j % 2, :], ACT.Silu), ("r", j))
        for i in range(4):
            pe_mix.wait(act, ("kt", i))
            act_mix.inc(nc.scalar.activation(kst_tok[:, i, :, :], SIDE[i].rearrange("p (t f) -> p t f", t=4), ACT.Copy),
                        ("ktc", i))
        hi_to(act, n + 18)
        for j in range(4):
            hi_to(act, n + 17 + j + 2)
            dve_mix.wait(act, ("u", j))
            act_mix.inc(nc.scalar.activation(cv[:, j, :], cu[:, j, 1:S1 + 1], ACT.Identity,
                                             scale=column("conv_w", (0, 1), j), bias=column("conv_b", 0, j)), ("tap", j))
        hi_to(act, n + 23)

        def square(h):
            pe_mix.wait(act, ("o", h))
            act_mix.inc(nc.scalar.activation(osq[h], PS[(n + 21 + h) % 4][:, 0, :], ACT.Square), ("osq", h))

        def root(h):
            dve_mix.wait(act, ("oms", h))
            act_mix.inc(act_rsqrt(act, OSD[h], OMS[h]), ("osd", h))

        def split(h):
            dve_mix.wait(act, ("y", h))
            nc.scalar.activation(hi(h, 1), o_gla[:, h % 2, :], ACT.Copy).then_inc(x_hi, 1)

        hi_to(act, n + 24)
        square(0)
        hi_to(act, n + 25)
        square(1)
        root(0)
        hi_to(act, n + 26)
        square(2)
        act.wait_ge(unit_summed, n + W_OUT)
        for j in range(4):
            dve_mix.wait(act, ("c", j))
            nc.scalar.activation(hi(4 + j, 1), cv[:, j, :], ACT.Copy).then_inc(x_hi, 1)
        split(0)
        root(1)
        square(3)
        root(2)
        split(1)
        root(3)
        split(2)
        split(3)
        act.wait_ge(x_lo, KD * (D_MIXO + 1))
        act.dma_start(mem_in[:, :, :], A["mem"][0].rearrange("(t p) d -> p t d", p=P)).then_inc(x_loaded, 16)
        act_out_units(act, n + W_OUT, S_XAT)

    def act_out_units(act, n, s):
        for m in range(KD):
            hi_to(act, n + m + 2)
            act.wait_ge(unit_read, n + m + 1)
            act_square(act, s, m, m, xt(m, 1), S1)

    def dve_out_units(dve, n, s):
        for m in range(KD):
            dve.wait_ge(unit_summed, n + m + 1)
            nc.vector.tensor_tensor(xt(m, 1), PS[(n + m) % 4][:, 0, :], xt(m, 1), ALU.add).then_inc(unit_read, 1)
            dve_acc(dve, s, m, m, S1)

    def act_split_all(act, d, gain, n):
        act.wait_ge(unit_summed, n)
        for m in range(KD):
            act_split(act, d, m, m, 1, gain)

    def dve_split_all(dve, d, gain):
        for m in range(KD):
            dve_split(dve, d, m, 1, gain)

    def dve_mixer(dve, link):
        n = PHASE["mix"]
        R = rn[:, 0:S1]

        def summed(j):
            dve.wait_ge(unit_summed, n + j + 1)
            return PS[(n + j) % 4][:, 0, :]

        link(nc.vector.memset(cu[:, :, 0:1], 0.0))
        link(nc.vector.memset(cu[:, :, S1 + 1:S1 + 2], 0.0))
        dve.wait_ge(unit_summed, n)
        dve_mix.inc(nc.vector.memset(gate_w[:, :], 0.0), "gz")
        dve_norm(dve, link, S_MIX, (n + 3) % 4, 1, rc=4)
        nc.vector.tensor_tensor(zz[:, :], summed(0)[0:32, :], R[0:32, :], ALU.mult).then_inc(unit_read, 1)
        for t in range(2):
            nc.vector.scalar_tensor_tensor(qs[:, t, :], summed(1 + t), float(GDK ** -0.5), R, ALU.mult,
                                           ALU.mult).then_inc(unit_read, 1)
        pe_mix.wait(dve, "lg")
        for i in range(4):
            dve_mix.inc(nc.vector.tensor_scalar(t2[:, i, :], SIDE[i], column("gate_fwd_b" if i < 2 else "gate_bwd_b", 0, i % 2),
                                                0.0, ALU.add, ALU.min), ("min", i))
        for t in range(2):
            nc.vector.tensor_tensor(ks[:, t, :], summed(3 + t), R, ALU.mult).then_inc(unit_read, 1)
        act_mix.wait(dve, "ln")
        dve_mix.wait(dve, ("min", 3))
        link(nc.vector.tensor_tensor(t2[:, :, :], t2[:, :, :], t1[:, :, :], ALU.subtract))
        reset = const[:, C_RST:C_RST + S1]
        for i in range(4):
            rev = slice(None) if i < 2 else slice(None, None, -1)
            ins = nc.vector.tensor_tensor_scan(t1[:, i, :][:, rev], reset, t2[:, i, :][:, rev], 0.0, ALU.mult, ALU.add)
            if i < 3:
                link(ins)
        dve_mix.inc(ins, "scan")
        dve_mix.wait(dve, "scan")
        link(nc.vector.tensor_copy(tot[:, 0:2, :], t1[:, 0:2, CHUNK - 1::CHUNK]))
        link(nc.vector.tensor_copy(tot[:, 2:4, :], t1[:, 2:4, 0::CHUNK]))
        dve_mix.inc(nc.vector.tensor_tensor(t2[:, :, :].rearrange("p i (c t) -> p (i c) t", t=CHUNK),
                                            tot[:, :, :].rearrange("p i c -> p (i c)").to_broadcast([P, 4 * NCH, CHUNK]),
                                            t1[:, :, :].rearrange("p i (c t) -> p (i c) t", t=CHUNK), ALU.subtract), "diff")
        act_mix.wait(dve, "eq")
        dve.wait_ge(unit_read, n + 5)
        for d in range(2):
            dve_mix.inc(nc.vector.tensor_tensor(q_in[:, 2 * d:2 * d + 2, :], qs[:, :, :], t3[:, 2 * d:2 * d + 2, :], ALU.mult),
                        ("qin", d))
        act_mix.wait(dve, "es")
        dve_mix.wait(dve, ("qin", 1))
        for d in range(2):
            dve_mix.inc(nc.vector.tensor_tensor(t3[:, 2 * d:2 * d + 2, :], ks[:, :, :], t2[:, 2 * d:2 * d + 2, :], ALU.mult),
                        ("kst", d))
        act_mix.wait(dve, "ek")
        for d in range(2):
            dve_mix.inc(nc.vector.tensor_tensor(k_in[:, 2 * d:2 * d + 2, :], ks[:, :, :], t1[:, 2 * d:2 * d + 2, :], ALU.mult),
                        ("kin", d))
        dve.wait_ge(unit_summed, n + 9)
        for t in range(4):
            nc.vector.tensor_scalar(v_tok[:, t, :], SIDE[t], rn[:, S1 + t:S1 + t + 1], None, ALU.mult).then_inc(unit_read, 1)
        for j in range(4):
            if j >= 2:
                act_mix.wait(dve, ("r", j - 2))
            nc.vector.tensor_tensor(mtmp[:, j % 2, :], summed(9 + j), R, ALU.mult).then_inc(unit_read, 1)

        def states(i):
            pe_mix.wait(dve, ("ds", i))
            order = range(0, NCH - 1) if i < 2 else range(NCH - 1, 0, -1)
            step = 1 if i < 2 else -1
            for at, c in enumerate(order):
                for a in range(2):
                    p0 = GDK * a
                    ds = side_of(c)[p0:p0 + GDK, a * GDV:(a + 1) * GDV]
                    to = state[p0:p0 + GDK, i, c + step, :]
                    if at == 0:
                        ins = nc.vector.tensor_copy(to, ds)
                    else:
                        ins = nc.vector.scalar_tensor_tensor(to, state[p0:p0 + GDK, i, c, :], dec[p0:p0 + GDK, i, c:c + 1], ds,
                                                             ALU.mult, ALU.add)
                    if at == NCH - 2 and a == 1:
                        dve_mix.inc(ins, ("state", i))
                    else:
                        link(ins)

        for j in range(4):
            nc.vector.tensor_tensor(cv[:, j, :], summed(13 + j), R, ALU.mult).then_inc(unit_read, 1)
            if j == 1:
                states(0)
        states(1)
        act_mix.wait(dve, ("r", 3))
        for j in range(4):
            if j >= 2:
                dve_mix.wait(dve, ("u", j - 2))
            nc.vector.tensor_tensor(mtmp[:, j % 2, :], summed(17 + j), R, ALU.mult).then_inc(unit_read, 1)
            dve.wait_ge(unit_read, n + 18 + j)
            dve_mix.inc(nc.vector.tensor_tensor(cu[:, j, 1:S1 + 1], mtmp[:, j % 2, :], cv[:, j, :], ALU.mult), ("u", j))
            if j == 1:
                states(2)
        states(3)
        for j in range(4):
            act_mix.wait(dve, ("tap", j))
            link(nc.vector.scalar_tensor_tensor(cv[:, j, :], cu[:, j, 0:S1], column("conv_w", (0, 0), j), cv[:, j, :],
                                                ALU.mult, ALU.add))
            link(nc.vector.scalar_tensor_tensor(cv[:, j, :], cu[:, j, 2:S1 + 2], column("conv_w", (0, 2), j), cv[:, j, :],
                                                ALU.mult, ALU.add))
        def convolved(j):
            if j >= 2:
                dve_mix.wait(dve, ("c", j - 2))
            nc.vector.tensor_tensor(mtmp[:, j % 2, :], summed(21 + j), R, ALU.mult).then_inc(unit_read, 1)
            dve.wait_ge(unit_read, n + 22 + j)
            dve_mix.inc(nc.vector.tensor_tensor(cv[:, j, :], mtmp[:, j % 2, :], cv[:, j, :], ALU.mult), ("c", j))

        pe_mix.wait(dve, ("kt", 3))
        dve_mix.inc(nc.vector.memset(att[:, :, :, :], 0.0), "attz")
        dve_mix.wait(dve, "attz")

        def masked(h):
            pe_mix.wait(dve, ("att", h))
            if h >= 2:
                pe_mix.wait(dve, ("o", h - 2))
            for d in range(2):
                mask = const[:, (C_MF, C_MB)[d]:(C_MF, C_MB)[d] + P].bitcast(U32)
                for t in range(4):
                    ins = nc.vector.copy_predicated(att[:, h % 2, d, t * P:(t + 1) * P], mask,
                                                    SIDE[2 * (h % 2) + d][:, t * P:(t + 1) * P])
                    if not (d == 1 and t == 3):
                        link(ins)
            dve_mix.inc(ins, ("att", h))

        def lower(h):
            src = o_gla[:, h % 2, :] if h < 4 else cv[:, h - 4, :]
            dve.wait_ge(x_hi, KD * D_MIXO + MIXO_ORDER.index(h) + 1)
            nc.vector.tensor_tensor(lo(h, 1), src, hi(h, 1).bitcast(F32), ALU.subtract).then_inc(x_lo, 1)

        def mean(h):
            pe_mix.wait(dve, ("osum", h))
            dve_mix.inc(nc.vector.tensor_scalar(OMS[h], SIDE[h], 1.0 / GDV, EPS, ALU.mult, ALU.add), ("oms", h))

        def normed(h):
            act_mix.wait(dve, ("osd", h))
            newton(link, OSD[h], OMS[h], rt[:, 0:S1], OSD[h])
            if h >= 2:
                dve.wait_ge(x_lo, KD * D_MIXO + MIXO_ORDER.index(h - 2) + 1)
            dve_mix.inc(nc.vector.scalar_tensor_tensor(o_gla[:, h % 2, :], PS[(n + 21 + h) % 4][:, 0, :],
                                                       column("gla_norm", 0, h), OSD[h], ALU.mult, ALU.mult), ("oread", h))
            dve_mix.wait(dve, ("oread", h))
            dve_mix.inc(nc.vector.tensor_tensor(o_gla[:, h % 2, :], o_gla[:, h % 2, :], r_act[:, h, :], ALU.mult), ("y", h))

        masked(0)
        masked(1)
        convolved(0)
        convolved(1)
        masked(2)
        convolved(2)
        masked(3)
        mean(0)
        normed(0)
        convolved(3)
        for j in range(4):
            lower(4 + j)
        lower(0)
        mean(1)
        mean(2)
        normed(1)
        mean(3)
        normed(2)
        lower(1)
        normed(3)
        lower(2)
        lower(3)
        dve_out_units(dve, n + W_OUT, S_XAT)

    pe_x.declare(*[("mt", k) for k in range(KD)], "msum", ("s", 0), ("s", 1),
                 *[x for i in range(16) for x in (([("s", i + 2)] if i < 14 else []) + [("t", i)]
                                                  + ([("pv", i // 4 - 1)] if i % 4 == 0 and i else []))], ("pv", 3))
    act_x.declare(*[(a, k) for k in range(KD) for a in ("mhi", "msq")], "msd", ("p", 0), ("p", 1),
                  *[x for i in range(16) for x in ((("tc", i),) if i >= 14 else (("tc", i), ("p", i + 2)))])
    dve_x.declare(*[(a, k) for k in range(KD) for a in ("mlo", "macc")], "mms", "mrn", ("max", 0),
                  *[x for i in range(16) for x in ((("pn", i),) if i == 15 else (("max", i + 1), ("pn", i)))])
    XS = [PS[0][:, 0, 0:MEM], PS[0][:, 1, 0:MEM], PS[1][:, 0, 0:MEM]]
    XT = PS[1][:, 1, 0:MEM]

    def pe_xat(pe):
        n = PHASE["xat"]
        H, L = (lambda k: hi(k, 1)), (lambda k: lo(k, 1))
        MHI, MLO = (lambda k: m_hi[:, k, :]), (lambda k: m_lo[:, k, :])
        pe.wait_ge(x_loaded, 16 * (S1 // P + 1))
        for k in range(KD):
            if k >= 4:
                act_x.wait(pe, ("msq", k - 4))
                dve_x.wait(pe, ("mlo", k - 4))
            for t in range(2):
                ins = nc.tensor.transpose(SIDE[k % 4][:, t * P:(t + 1) * P], mem_in[:, t, k * P:(k + 1) * P], ident)
            pe_x.inc(ins, ("mt", k))
        for j in range(KD):
            pe_unit(pe, n + j, 0, FLAT[n + j], MHI, MLO, [(PS[(n + j) % 4][:, 0, 0:MEM], 0, MEM)],
                    (lambda k: dve_x.wait(pe, ("mlo", k))) if j == 0 else None)
            if j == 0:
                dve_x.wait(pe, ("macc", KD - 1))
                nc.tensor.matmul(SIDE[3][:, 0:MEM], ones, m_acc[:, :], start=True, stop=True)
                for t in range(2):
                    ins = nc.tensor.matmul(SIDE[3][:, MEM + t:MEM + t + 1], m_acc[:, t * P:(t + 1) * P], ones[:, 0:1],
                                           start=True, stop=True)
                pe_x.inc(ins, "msum")
        dve_x.wait(pe, "mrn")
        for j in range(KD):
            m = n + KD + j
            pe.wait_ge(lo_done, m + 1)
            s, hf = m % SPLIT, j // 4
            for kk in range(2):
                k = 2 * (j % 4) + kk
                wh, wl = w_hi[:, s, kk * 512:(kk + 1) * 512], w_lo[:, s, kk * 512:(kk + 1) * 512]
                for t in range(2):
                    xh, xl = m_hi[:, k, t * P:(t + 1) * P], m_lo[:, k, t * P:(t + 1) * P]
                    nc.tensor.matmul(SIDE[2 * hf + t], xh, wh, start=(k == 0), stop=False)
                    nc.tensor.matmul(SIDE[2 * hf + t], xh, wl, start=False, stop=False)
                    ins = nc.tensor.matmul(SIDE[2 * hf + t], xl, wh, start=False, stop=(k == KD - 1))
            ins.then_inc(unit_summed, 1)
        n += 2 * KD
        pe.wait_ge(unit_read, n)
        pe.wait_ge(acc_done, KD * (S_XAT + 1))
        pe_norm(pe, S_XAT, (n + 3) % 4, 1).then_inc(norm_sum, 1)
        for j in range(KD):
            if j == 3:
                pe.wait_ge(norm_ms, S_XAT + 1)
            pe_unit(pe, n + j, 0, FLAT[n + j], H, L, outs_of((n + j) % 4, 1),
                    (lambda k: pe.wait_ge(x_lo, KD * D_XAT + k + 1)) if j == 0 else None)
        n += KD
        pe.wait_ge(unit_read, n)

        def score(i):
            h, t = i // 4, i % 4
            if i >= 3:
                act_x.wait(pe, ("p", i - 3))
            for kk in range(2):
                ins = nc.tensor.matmul(XS[i % 3], xq[:, 2 * h + kk, t * P:(t + 1) * P], xk[:, 2 * h + kk, :],
                                       start=(kk == 0), stop=(kk == 1))
            pe_x.inc(ins, ("s", i))

        def turn(i):
            dve_x.wait(pe, ("pn", i))
            if i:
                act_x.wait(pe, ("tc", i - 1))
            for mt in range(2):
                ins = nc.tensor.transpose(XT[:, mt * P:(mt + 1) * P], xp[:, i % 3, mt * P:(mt + 1) * P], ident)
            pe_x.inc(ins, ("t", i))

        def values(h):
            act_x.wait(pe, ("tc", 4 * h + 3))
            if h >= 2:
                pe.wait_ge(x_lo, KD * D_XATO + 2 * (h - 2) + 2)
            for dt in range(2):
                for mt in range(2):
                    ins = nc.tensor.matmul(PS[2 + h % 2][:, dt, :], xv[:, mt, h * XHD + dt * P:h * XHD + (dt + 1) * P],
                                           xpt[:, h % 2, mt, :], start=(mt == 0), stop=(mt == 1))
            pe_x.inc(ins, ("pv", h))

        score(0)
        score(1)
        for i in range(16):
            if i + 2 < 16:
                score(i + 2)
            turn(i)
            if i % 4 == 0 and i:
                values(i // 4 - 1)
        values(3)
        pe.wait_ge(x_lo, KD * (D_XATO + 1))
        for j in range(KD):
            pe_unit(pe, n + j, 0, FLAT[n + j], H, L, outs_of((n + j) % 4, 1))

    def act_xat(act):
        n = PHASE["xat"]
        for k in range(KD):
            pe_x.wait(act, ("mt", k))
            act_x.inc(nc.scalar.activation(m_hi[:, k, :], SIDE[k % 4][:, 0:MEM], ACT.Identity, scale=G_MEM(k)), ("mhi", k))
            if k >= 2:
                dve_x.wait(act, ("macc", k - 2))
            act_x.inc(nc.scalar.activation(m_sq[:, k % 2, :], SIDE[k % 4][:, 0:MEM], ACT.Square), ("msq", k))
        hi_to(act, n + 2)
        pe_x.wait(act, "msum")
        dve_x.wait(act, "mms")
        act_x.inc(act_rsqrt(act, m_sd[:, :], m_ms[:, :]), "msd")
        hi_to(act, n + 3)
        act_split_all(act, D_XAT, G_XAT, n)
        for j in range(2, 2 * KD):
            hi_to(act, n + j + 2)
        n += 2 * KD
        act_sqrt(act, S_XAT, S1)
        for j in range(KD):
            hi_to(act, n + j + 2)
        n += KD

        def probs(i):
            dve_x.wait(act, ("max", i))
            if i >= 3:
                pe_x.wait(act, ("t", i - 3))
            act_x.inc(nc.scalar.activation(xp[:, i % 3, :], XS[i % 3], ACT.Exp, bias=xst[:, i, 0:1],
                                           accum_out=xst[:, i, 1:2]), ("p", i))

        def turned_copy(i):
            h, t = i // 4, i % 4
            pe_x.wait(act, ("t", i))
            if h >= 2:
                pe_x.wait(act, ("pv", h - 2))
            act_x.inc(nc.scalar.activation(xpt[:, h % 2, :, t * P:(t + 1) * P], XT.rearrange("p (m q) -> p m q", m=2),
                                           ACT.Copy), ("tc", i))

        def upper(h):
            pe_x.wait(act, ("pv", h))
            for dt in range(2):
                nc.scalar.activation(hi(2 * h + dt, 1), PS[2 + h % 2][:, dt, :], ACT.Copy).then_inc(x_hi, 1)

        probs(0)
        probs(1)
        for i in range(16):
            turned_copy(i)
            if i + 2 < 16:
                probs(i + 2)
            if i % 4 == 1 and i > 4:
                upper(i // 4 - 1)
        upper(3)
        act_out_units(act, n, S_FFN2)
        act_split_all(act, D_FFN2, G_FFN2, n + KD)

    def dve_xat(dve, link):
        n = PHASE["xat"]
        for k in range(KD):
            act_x.wait(dve, ("msq", k))
            dve_x.inc(nc.vector.scalar_tensor_tensor(m_lo[:, k, :], SIDE[k % 4][:, 0:MEM], G_MEM(k), m_hi[:, k, :].bitcast(F32),
                                                     ALU.mult, ALU.subtract), ("mlo", k))
            if k == 0:
                dve_x.inc(nc.vector.tensor_copy(m_acc[:, :], m_sq[:, 0, :]), ("macc", k))
            else:
                dve_x.wait(dve, ("macc", k - 1))
                dve_x.inc(nc.vector.tensor_tensor(m_acc[:, :], m_acc[:, :], m_sq[:, k % 2, :], ALU.add), ("macc", k))
        pe_x.wait(dve, "msum")
        dve_x.inc(nc.vector.tensor_scalar(m_ms[:, :], SIDE[3][:, 0:MEM + 2], 1.0 / D, EPS, ALU.mult, ALU.add), "mms")
        act_x.wait(dve, "msd")
        newton(link, m_rn[:, :], m_ms[:, :], m_rt[:, :], m_sd[:, :], lambda ins: dve_x.inc(ins, "mrn"))
        dve_x.wait(dve, "mrn")
        dve_split_all(dve, D_XAT, G_XAT)
        for j in range(KD):
            dve.wait_ge(unit_summed, n + j + 1)
            nc.vector.tensor_tensor(xk[:, j, :], PS[(n + j) % 4][:, 0, 0:MEM], m_rn[:, 0:MEM], ALU.mult).then_inc(unit_read, 1)
        for hf in range(2):
            dve.wait_ge(unit_summed, n + KD + 4 * hf + 4)
            for t in range(2):
                for c in range(2):
                    nc.vector.tensor_scalar(xv[:, t, hf * 512 + c * 256:hf * 512 + (c + 1) * 256],
                                            SIDE[2 * hf + t][:, c * 256:(c + 1) * 256], m_rn[:, MEM + t:MEM + t + 1], None,
                                            ALU.mult).then_inc(unit_read, 1)
        n += 2 * KD
        dve_norm(dve, link, S_XAT, (n + 3) % 4, 1)
        for j in range(KD):
            dve.wait_ge(unit_summed, n + j + 1)
            nc.vector.scalar_tensor_tensor(xq[:, j, :], PS[(n + j) % 4][:, 0, :], float(XHD ** -0.5), rn[:, 0:S1], ALU.mult,
                                           ALU.mult).then_inc(unit_read, 1)
        n += KD

        def maximum(i):
            pe_x.wait(dve, ("s", i))
            dve_x.inc(nc.vector.tensor_reduce(xst[:, i, 0:1], XS[i % 3], AX.X, ALU.max, negate=True), ("max", i))

        def scaled(i):
            act_x.wait(dve, ("p", i))
            link(nc.vector.reciprocal(xst[:, i, 2:3], xst[:, i, 1:2]))
            dve_x.inc(nc.vector.tensor_scalar(xp[:, i % 3, :], xp[:, i % 3, :], xst[:, i, 2:3], None, ALU.mult), ("pn", i))

        def lower(h):
            for dt in range(2):
                dve.wait_ge(x_hi, KD * D_XATO + 2 * h + dt + 1)
                nc.vector.tensor_tensor(lo(2 * h + dt, 1), PS[2 + h % 2][:, dt, :], hi(2 * h + dt, 1).bitcast(F32),
                                        ALU.subtract).then_inc(x_lo, 1)

        maximum(0)
        for i in range(16):
            if i + 1 < 16:
                maximum(i + 1)
            scaled(i)
            if i % 4 == 2 and i > 4:
                lower(i // 4 - 1)
        lower(3)
        dve_out_units(dve, n, S_FFN2)
        dve_split_all(dve, D_FFN2, G_FFN2)

    def pe_fin(pe):
        n = PHASE["ffn2"] + 68
        pe.wait_ge(unit_read, n)
        pe_norm(pe, S_FIN, n % 4, 1).then_inc(norm_sum, 1)

    def act_fin(act):
        act_sqrt(act, S_FIN, S1)
        for k in range(KD):
            x_ready.wait(act, ("fin", k))
            act_split(act, D_MLA, k, k, 2, G_PRE[0])
            act_square(act, S_MLA, k, k, X[:, k, :], S2)

    def dve_fin(dve, link):
        dve_norm(dve, link, S_FIN, (PHASE["ffn2"] + 68) % 4, 1)
        for k in range(KD + 1):
            if k < KD:
                x_ready.inc(nc.vector.scalar_tensor_tensor(xt(k, 1), xt(k, 1), G_FIN(k), rn[:, 0:S1], ALU.mult, ALU.mult),
                            ("fin", k))
            if k:
                dve_split(dve, D_MLA, k - 1, 2, G_PRE[0])

    ITEMS = (4, 2, 1, 3, 0)
    KEYS = {j: META + P * j for j in range(5)}
    QROW = {j: max(META + P * (j - 1), 0) for j in range(5)}
    TOK0 = {j: max(META + P * (j - 1), 0) for j in range(5)}
    OFF = {}
    for j in ITEMS:
        OFF[j] = sum(KEYS[i] for i in ITEMS[:ITEMS.index(j)])
    WIDE = PS[0][:, :, :].rearrange("p b c -> p (b c)")
    PLACE = {4: WIDE[:, 0:528], 2: WIDE[:, 528:800], 1: WIDE[:, 800:944], 3: PS[1][:, 0, 0:400], 0: PS[1][:, 0, 400:416]}
    GROUPS = ((4, 2, 1), (3, 0))
    SEQ = [(h, j) for h in range(MH) for j in ITEMS]
    NI = len(ITEMS)

    def group_of(j):
        return [g for g in GROUPS if j in g][0]

    class Job:
        def __init__(self, unit, kind, at, last):
            self.unit, self.kind, self.at, self.last = unit, kind, at, last

    def kv_jobs(t):
        at = [("k", (a, c)) for a in range(2) for c in range(2)] + [("v", (0, 1)), ("v", (2, 3)), ("v", (4,))]
        return [Job(3 * t, kind, (t,) + x if kind == "k" else (t, x), i == len(at) - 1) for i, (kind, x) in enumerate(at)]

    def q_jobs(p):
        return [Job(3 * (p // 2) + 1 + p % 2, "q", (p, a, c), a == 1 and c == 1) for a in range(2) for c in range(2)]

    FIRST_JOBS = kv_jobs(0) + q_jobs(0)
    JOB_AT = {}
    for t in range(MH // 4):
        beside = q_jobs(2 * t + 1) + (kv_jobs(t + 1) + q_jobs(2 * t + 2) if t + 1 < MH // 4 else [])
        for i, job in enumerate(beside):
            JOB_AT[4 * NI * t + i] = job
    JOBS = FIRST_JOBS + [JOB_AT[x] for x in sorted(JOB_AT)]
    job_summed.declare(*[(j.kind, j.at) for j in JOBS if not j.last])
    job_read.declare(*[(j.kind, j.at) for j in JOBS if not j.last])
    JOB_BANKS = [PS[1][:, 1, :], PS[2][:, 0, :], PS[2][:, 1, :], PS[0][:, 0, :], PS[0][:, 1, :], PS[1][:, 0, :], PS[3][:, 0, :],
                 PS[3][:, 1, :]]
    KEY_BANK = 6

    def job_bank(job):
        at = JOBS.index(job)
        return JOB_BANKS[at % len(JOB_BANKS)] if at < len(FIRST_JOBS) else JOB_BANKS[0]

    def job_wait(eng, job, n, signal, unit_signal):
        if job.last:
            eng.wait_ge(unit_signal, n + job.unit + 1)
        else:
            signal.wait(eng, (job.kind, job.at))

    def pe_mla_order():
        o = [("s", 0, j) for j in ITEMS]
        for x, (h, j) in enumerate(SEQ):
            o.append(("t", h, j))
            if h + 1 < MH and j == 1:
                o += [("s", h + 1, i) for i in GROUPS[0]]
            if h + 1 < MH and j == 0:
                o += [("s", h + 1, i) for i in GROUPS[1]]
            if x:
                o.append(("pv",) + SEQ[x - 1])
        return o + [("pv",) + SEQ[-1]]

    PROBS_AT = {4: (), 2: ((0, 3), (0, 0)), 1: (), 3: ((1, 4),), 0: ((1, 2), (1, 1))}

    def act_mla_order():
        o = [("p", 0, j) for j in GROUPS[0]]
        for x, (h, j) in enumerate(SEQ):
            o += [("tc0", h, j), ("tc", h, j)] if j else [("tc", h, j)]
            o += [("p", h + d, i) for d, i in PROBS_AT[j] if h + d < MH]
            if h and j == 2:
                o += [("oh", h - 1, 0), ("oh", h - 1, 1)]
        return o + [("oh", MH - 1, 0), ("oh", MH - 1, 1)]

    def maxima_at(h, j):
        if j == 4:
            return [(h, i) for i in GROUPS[1]]
        if j == 3 and h + 1 < MH:
            return [(h + 1, i) for i in GROUPS[0]]
        return []

    def dve_mla_order():
        o = [("max", 0, j) for j in GROUPS[0]]
        for x, (h, j) in enumerate(SEQ):
            o.append(("pn", h, j))
            o += [("max",) + it for it in maxima_at(h, j)]
            if h and j == 1:
                o += [("ol", h - 1, 0), ("ol", h - 1, 1)]
        return o + [("ol", MH - 1, 0), ("ol", MH - 1, 1)]

    pe_m.declare("sums", "dup", *pe_mla_order())
    act_m.declare(*[(a, t) for t in range(5) for a in ("chi", "csq")], "qsd", "kvsd", "krope", *act_mla_order())
    dve_m.declare(*[(a, t) for t in range(5) for a in ("clo", "cacc")], "kr", "qms", "kvms", "krope", "ct", "rkv", "masks",
                  *dve_mla_order())

    def latent(t):
        if t < 3:
            return cq_hi[:, t, :], cq_lo[:, t, :], column("mla_q_norm_2", 0, t), acc, t
        return ckv_hi[:, t - 3, :], ckv_lo[:, t - 3, :], column("mla_kv_norm_2", 0, t - 3), r_kv, t - 3

    def two(ap):
        return ap.rearrange("p (c w) -> p c w", c=2)

    flat_cq = cq[:, :, :].rearrange("p t w -> p (t w)")
    kv_ms, kv_sd = flat_cq[:, 0:S2 + 5], flat_cq[:, S2 + 6:2 * S2 + 11]

    def pe_mla(pe):
        n = PHASE["mla"]
        pe_first_unit(pe, n, S_MLA, D_MLA, 2, n)
        for j in range(1, 6):
            if j == 3:
                pe.wait_ge(norm_ms, S_MLA + 1)
            pe_unit(pe, n + j, 0, FLAT[n + j], lambda k: hi(k, 2), lambda k: lo(k, 2), outs_of((n + j) % 4, 2))
        n += 6
        pe.wait_ge(unit_read, n)
        dve_m.wait(pe, ("cacc", 4))
        for pair, src in ((0, acc), (1, r_kv)):
            for ps, c, w in outs_of(pair, 2):
                nc.tensor.matmul(ps, ones, src[:, c:c + w], start=True, stop=True)
        for j in range(5):
            ins = nc.tensor.matmul(PS[2][:, 0, j:j + 1], r_kv[:, TOK0[j]:TOK0[j] + P], ones[:, 0:1], start=True, stop=True)
        pe_m.inc(ins, "sums")
        dve_m.wait(pe, "kr")
        for ps, c, w in outs_of(3, 2):
            ins = nc.tensor.matmul(ps, const[NOPE:, C_DUP:C_DUP + P], q4[NOPE:, 1, c:c + w], start=True, stop=True)
        pe_m.inc(ins, "dup")
        dve_m.wait(pe, "kvms")
        for i, job in enumerate(FIRST_JOBS):
            if i == KEY_BANK:
                dve_m.wait(pe, "krope")
                act_m.wait(pe, "krope")
            pe_job(pe, n, job)
        dve_m.wait(pe, "masks")
        for j in ITEMS:
            pe_score(pe, n, 0, j)
        for x, (h, j) in enumerate(SEQ):
            pe_turn(pe, x)
            if h + 1 < MH and j == GROUPS[0][-1]:
                for i in GROUPS[0]:
                    pe_score(pe, n, h + 1, i)
            if h + 1 < MH and j == GROUPS[1][-1]:
                for i in GROUPS[1]:
                    pe_score(pe, n, h + 1, i)
            if x:
                pe_values(pe, x - 1)
            if x in JOB_AT:
                pe_job(pe, n, JOB_AT[x])
        pe_values(pe, len(SEQ) - 1)
        n += 3 * MH // 4
        dve_m.wait(pe, ("ol", MH - 1, 1))
        for j in range(KD):
            pe_unit(pe, n + j, 0, FLAT[n + j], lambda k: hi(k, 2), lambda k: lo(k, 2), outs_of((n + j) % 4, 2))

    def pe_job(pe, n, job):
        at = JOBS.index(job)
        before = at - (len(JOB_BANKS) if at < len(FIRST_JOBS) else 1)
        if before >= 0:
            job_wait(pe, JOBS[before], n, job_read, unit_read)
        m = n + job.unit
        pe.wait_ge(lo_done, m + 1)
        s, bank = m % SPLIT, job_bank(job)
        if job.kind == "v":
            for i, j in enumerate(job.at[1]):
                for k in range(2):
                    c0 = (2 + k) * 2 * P
                    wh, wl = w_hi[:, s, c0:c0 + 2 * P], w_lo[:, s, c0:c0 + 2 * P]
                    for w, x, st, sp_ in ((wh, ckv_hi, k == 0, False), (wl, ckv_hi, False, False), (wh, ckv_lo, False, k == 1)):
                        ins = nc.tensor.matmul(bank[:, i * 256:(i + 1) * 256], x[:, k, TOK0[j]:TOK0[j] + P], w, start=st, stop=sp_)
        else:
            _, a, c = job.at
            x_hi_, x_lo_, kt = (cq_hi, cq_lo, 3) if job.kind == "q" else (ckv_hi, ckv_lo, 2)
            for k in range(kt):
                c0 = (2 * k + a) * P
                wh, wl = w_hi[:, s, c0:c0 + P], w_lo[:, s, c0:c0 + P]
                for w, x, st, sp_ in ((wh, x_hi_, k == 0, False), (wh, x_lo_, False, False), (wl, x_hi_, False, k == kt - 1)):
                    ins = nc.tensor.matmul(bank[:, 0:CW], w, x[:, k, c * CW:(c + 1) * CW], start=st, stop=sp_)
        if job.last:
            ins.then_inc(unit_summed, 1)
        else:
            job_summed.inc(ins, (job.kind, job.at))

    def pe_score(pe, n, h, j):
        q, k = q4[:, h % 4, QROW[j]:QROW[j] + P], k8[:, h % 8, 0:KEYS[j]]
        if j == GROUPS[0][0]:
            pe.wait_ge(unit_read, n + q_jobs(h // 2)[0].unit + 1)
        if h:
            for i in group_of(j):
                act_m.wait(pe, ("p", h - 1, i))
        dst, m0, m1 = PLACE[j], mask_r[:, 0, :], mask_r[:, 1, :]
        if j == 4:
            nc.tensor.matmul(dst[:, 0:512], q, k[:, 0:512], start=True, stop=False)
            nc.tensor.matmul(dst[:, 512:], q, k[:, 512:], start=True, stop=False)
            edge = 512 - (KEYS[4] - P)
            nc.tensor.matmul(dst[:, 512 - edge:512], m0, m1[:, 0:edge], start=False, stop=True)
            ins = nc.tensor.matmul(dst[:, 512:], m0, m1[:, edge:], start=False, stop=True)
        else:
            nc.tensor.matmul(dst, q, k, start=True, stop=False)
            w = min(P, KEYS[j])
            ins = nc.tensor.matmul(dst[:, KEYS[j] - w:], m0, m1[:, 0:w], start=False, stop=True)
        pe_m.inc(ins, ("s", h, j))

    def pe_turn(pe, x):
        h, j = SEQ[x]
        dve_m.wait(pe, ("pn", h, j))
        if x:
            act_m.wait(pe, ("tc",) + SEQ[x - 1])
        for i in range(1, j + 1):
            k0 = OFF[j] + TOK0[i]
            nc.tensor.transpose(PS[2][:, 0, (i - 1) * P:i * P], pr[:, h % 2, k0:k0 + P], ident)
        pe_m.inc(nc.tensor.transpose(PS[2][0:META, 1, 0:P], pr[:, h % 2, OFF[j]:OFF[j] + META], ident), ("t", h, j))

    def pe_values(pe, x):
        h, j = SEQ[x]
        if j == ITEMS[0] and h >= 2:
            dve_m.wait(pe, ("ol", h - 2, 1))
        act_m.wait(pe, ("tc", h, j))
        p0 = VD * (h % 2)
        nq = META if j == 0 else P
        dst = PS[3][p0:p0 + VD, 1, 0:P] if j == 4 else PS[3][p0:p0 + VD, 0, TOK0[j]:TOK0[j] + nq]
        for i in range(j + 1):
            kk = META if i == 0 else P
            ins = nc.tensor.matmul(dst, v4[0:kk, h // 4 % 2, i, h % 4 * VD:(h % 4 + 1) * VD], pt[0:kk, x % 2, i, 0:nq],
                                   start=(i == 0), stop=(i == j))
        pe_m.inc(ins, ("pv", h, j))

    def prob(h, j):
        return pr[:, h % 2, OFF[j]:OFF[j] + KEYS[j]]

    HI_AT = {6: 4, 13: 5, 17: 6}

    def act_mla(act):
        n = PHASE["mla"]
        hi_to(act, n + 2)
        act_sqrt(act, S_MLA, S2)
        for t in range(5):
            hi_to(act, n + t + 2)
            act.wait_ge(unit_read, n + t + 1)
            h, _, g, _, _ = latent(t)
            act_m.inc(nc.scalar.activation(h, cq[:, t % 3, :], ACT.Identity, scale=g), ("chi", t))
            if t >= 2:
                dve_m.wait(act, ("cacc", t - 2))
            act_m.inc(nc.scalar.activation(sq[:, t % 2, 0:S2], cq[:, t % 3, :], ACT.Square), ("csq", t))
        hi_to(act, n + 7)
        dve_m.wait(act, "qms")
        act_m.inc(act_rsqrt(act, sd[:, 0:S2], ms[:, 0:S2]), "qsd")
        dve_m.wait(act, "kvms")
        act_m.inc(act_rsqrt(act, kv_sd, kv_ms), "kvsd")
        n += 6
        hi_to(act, n + 1)
        dve_m.wait(act, "krope")
        for i in range(4, 8):
            ins = nc.scalar.activation(two(k8[NOPE:, i, :]), PS[3][NOPE:, :, 0:CW], ACT.Copy)
        act_m.inc(ins, "krope")
        hi_to(act, n + 3)

        def probs(h, j):
            dve_m.wait(act, ("max", h, group_of(j)[-1]))
            if h >= 2:
                pe_m.wait(act, ("t", h - 2, j))
            act_m.inc(nc.scalar.activation(prob(h, j), PLACE[j], ACT.Exp, bias=mst[:, h, j, 0:1], accum_out=mst[:, h, j, 1:2]),
                      ("p", h, j))

        def turned_copy(x):
            h, j = SEQ[x]
            pe_m.wait(act, ("t", h, j))
            if x >= 2:
                pe_m.wait(act, ("pv",) + SEQ[x - 2])
            nq = P if j else META
            ins = nc.scalar.activation(pt[0:META, x % 2, 0, 0:nq], PS[2][0:META, 1, 0:nq], ACT.Copy)
            if j:
                act_m.inc(ins, ("tc0", h, j))
                ins = nc.scalar.activation(pt[:, x % 2, 1:j + 1, :], PS[2][:, 0, 0:j * P].rearrange("p (i q) -> p i q", q=P),
                                           ACT.Copy)
            act_m.inc(ins, ("tc", h, j))

        def upper(h):
            p0 = VD * (h % 2)
            pe_m.wait(act, ("pv", h, ITEMS[-1]))
            act_m.inc(nc.scalar.activation(XHI[p0:p0 + VD, h // 2, 0:400], PS[3][p0:p0 + VD, 0, 0:400], ACT.Copy), ("oh", h, 0))
            act_m.inc(nc.scalar.activation(XHI[p0:p0 + VD, h // 2, 400:S2], PS[3][p0:p0 + VD, 1, 0:P], ACT.Copy), ("oh", h, 1))

        for j in GROUPS[0]:
            probs(0, j)
        for x, (h, j) in enumerate(SEQ):
            t, i = x // (4 * NI), x % (4 * NI)
            if i in HI_AT:
                hi_to(act, n + min(3 * t + HI_AT[i], 3 * MH // 4 + 1))
            turned_copy(x)
            for d, jj in PROBS_AT[j]:
                if h + d < MH:
                    probs(h + d, jj)
            if h and j == 2:
                upper(h - 1)
        upper(MH - 1)
        n += 3 * MH // 4
        for m in range(KD):
            hi_to(act, n + m + 2)
            act.wait_ge(unit_read, n + m + 1)
            act_square(act, S_MLAP, m, m, M[:, m, :], S2)

    def dve_mla(dve, link):
        n = PHASE["mla"]
        dve_norm(dve, link, S_MLA, (n + 3) % 4, 2)
        R = rn[:, 0:S2]
        for t in range(5):
            dve.wait_ge(unit_summed, n + t + 1)
            if t >= 3:
                act_m.wait(dve, ("csq", t - 3))
            nc.vector.tensor_tensor(two(cq[:, t % 3, :]), psv((n + t) % 4, 2), two(R), ALU.mult).then_inc(unit_read, 1)
            h, l, g, a, at = latent(t)
            act_m.wait(dve, ("chi", t))
            dve_m.inc(nc.vector.scalar_tensor_tensor(l, cq[:, t % 3, :], g, h.bitcast(F32), ALU.mult, ALU.subtract), ("clo", t))
            act_m.wait(dve, ("csq", t))
            if at == 0:
                dve_m.inc(nc.vector.tensor_copy(a[:, 0:S2], sq[:, t % 2, 0:S2]), ("cacc", t))
            else:
                dve_m.wait(dve, ("cacc", t - 1))
                dve_m.inc(nc.vector.tensor_tensor(a[:, 0:S2], a[:, 0:S2], sq[:, t % 2, 0:S2], ALU.add), ("cacc", t))
        dve.wait_ge(unit_summed, n + 6)
        rope = const[:, C_ROPE:C_ROPE + S2]
        nc.vector.tensor_tensor(two(q4[:, 0, :]), psv((n + 5) % 4, 2), two(R), ALU.mult).then_inc(unit_read, 1)
        dve.wait_ge(unit_read, n + 6)
        dve_m.inc(nc.vector.tensor_tensor(q4[:, 1, :], q4[:, 0, :], rope, ALU.mult), "kr")
        pe_m.wait(dve, "sums")
        dve_m.inc(nc.vector.tensor_scalar(two(ms[:, 0:S2]), psv(0, 2), 1.0 / QL, EPS, ALU.mult, ALU.add), "qms")
        link(nc.vector.tensor_scalar(two(kv_ms[:, 0:S2]), psv(1, 2), 1.0 / KVL, EPS, ALU.mult, ALU.add))
        dve_m.inc(nc.vector.tensor_scalar(kv_ms[:, S2:S2 + 5], PS[2][:, 0, 0:5], 1.0 / KVL, EPS, ALU.mult, ALU.add), "kvms")
        pe_m.wait(dve, "dup")
        for i in range(4):
            ins = nc.vector.tensor_copy(two(k8[NOPE:, i, :]), PS[3][NOPE:, :, 0:CW])
            if i < 3:
                link(ins)
        dve_m.inc(ins, "krope")
        act_m.wait(dve, "qsd")
        newton(link, rn[:, 0:S2], ms[:, 0:S2], rt[:, 0:S2], sd[:, 0:S2])
        dve_m.inc(nc.vector.scalar_tensor_tensor(ct[:, :], rope, MLA_SCALE, rn[:, 0:S2], ALU.mult, ALU.mult), "ct")
        act_m.wait(dve, "kvsd")
        w = S2 + 5
        newton(link, r_kv[:, 0:w], kv_ms, rt[:, 0:w], kv_sd, lambda ins: dve_m.inc(ins, "rkv"))
        dve_m.wait(dve, "rkv")
        link(nc.vector.tensor_copy(mask_r[:, 0, :], ident))
        dve_m.inc(nc.vector.tensor_copy(mask_r[:, 1, :], const[:, C_NEG:C_NEG + P]), "masks")
        n += 6
        for job in FIRST_JOBS:
            dve_job(dve, n, job)

        def maximum(h, j):
            pe_m.wait(dve, ("s", h, group_of(j)[-1]))
            dve_m.inc(nc.vector.tensor_reduce(mst[:, h, j, 0:1], PLACE[j], AX.X, ALU.max, negate=True), ("max", h, j))

        def scaled(h, j):
            act_m.wait(dve, ("p", h, j))
            link(nc.vector.reciprocal(mst[:, h, j, 2:3], mst[:, h, j, 1:2]))
            dve_m.inc(nc.vector.tensor_scalar(prob(h, j), prob(h, j), mst[:, h, j, 2:3], None, ALU.mult), ("pn", h, j))

        def lower(h):
            p0 = VD * (h % 2)
            for i, (c0, c1, src) in enumerate(((0, 400, PS[3][p0:p0 + VD, 0, 0:400]), (400, S2, PS[3][p0:p0 + VD, 1, 0:P]))):
                act_m.wait(dve, ("oh", h, i))
                dve_m.inc(nc.vector.tensor_tensor(XLO[p0:p0 + VD, h // 2, c0:c1], src, XHI[p0:p0 + VD, h // 2, c0:c1].bitcast(F32),
                                                  ALU.subtract), ("ol", h, i))

        for j in GROUPS[0]:
            maximum(0, j)
        for x, (h, j) in enumerate(SEQ):
            scaled(h, j)
            for it in maxima_at(h, j):
                maximum(*it)
            if x - 1 in JOB_AT:
                dve_job(dve, n, JOB_AT[x - 1])
            if h and j == 1:
                lower(h - 1)
        lower(MH - 1)
        n += 3 * MH // 4
        for m in range(KD):
            dve.wait_ge(unit_summed, n + m + 1)
            nc.vector.tensor_copy(two(M[:, m, :]), psv((n + m) % 4, 2)).then_inc(unit_read, 1)
            dve_acc(dve, S_MLAP, m, m, S2)

    def dve_job(dve, n, job):
        job_wait(dve, job, n, job_summed, unit_summed)
        bank, r = job_bank(job), []
        if job.kind == "q":
            p, a, c = job.at
            cols_ = slice(c * CW, (c + 1) * CW)
            r.append(nc.vector.tensor_tensor(q4[:, (2 * p + a) % 4, cols_], bank[:, 0:CW], ct[:, cols_], ALU.mult))
        elif job.kind == "k":
            t, a, c = job.at
            cols_ = slice(c * CW, (c + 1) * CW)
            for i in range(2):
                p0 = NOPE * i
                r.append(nc.vector.tensor_tensor(k8[0:NOPE, (4 * t + 2 * a + i) % 8, cols_], bank[p0:p0 + NOPE, 0:CW],
                                                 r_kv[p0:p0 + NOPE, cols_], ALU.mult))
        else:
            t, tiles = job.at
            for i, j in enumerate(tiles):
                rows_ = META if j == 0 else P
                r.append(nc.vector.tensor_scalar(v4[0:rows_, t % 2, j, :], bank[0:rows_, i * 256:(i + 1) * 256],
                                                 r_kv[0:rows_, S2 + j:S2 + j + 1], None, ALU.mult))
        if job.last:
            r[-1].then_inc(unit_read, 1)
        else:
            job_read.inc(r[-1], (job.kind, job.at))

    pool_mixed = Signal(sem("pool_mixed"))
    pool_evac = Signal(sem("pool_evac"))
    pool_mixed.declare(*range(4))
    pool_evac.declare(*range(0, KD, 2))

    def pool_out(eng, m):
        if m % 2:
            eng.wait_ge(unit_read, PHASE["pool"] + m // 2 + 1)
        else:
            pool_evac.wait(eng, m)

    SUMS = 3

    def pe_pool(pe):
        n = PHASE["pool"]
        pe.wait_ge(unit_read, n)
        for k in range(KD):
            pe_square(pe, S_POOL, SUMS, 2, k)
        for g in range(4):
            pe.wait_ge(lo_done, n + g + 1)
            s = (n + g) % SPLIT
            for k in range(2):
                pe.wait_ge(x_lo, KD * D_POOL + 2 * g + k + 1)
            for mt in range(2):
                m = 2 * g + mt
                if m >= 3:
                    pool_out(pe, m - 3)
                for k in range(2):
                    c0 = k * 256 + mt * P
                    wh, wl = w_hi[:, s, c0:c0 + P], w_lo[:, s, c0:c0 + P]
                    for w, x, st, sp_ in ((wh, hi, k == 0, False), (wh, lo, False, False), (wl, hi, False, k == 1)):
                        for ps, c, cw in outs_of(m % 3, 2):
                            ins = nc.tensor.matmul(ps, w, x(2 * g + k, 2)[:, c:c + cw], start=st, stop=sp_)
            ins.then_inc(unit_summed, 1)
            if g == 1:
                pe.wait_ge(norm_ms, S_POOL + 1)
            if g:
                for m in (2 * g - 2, 2 * g - 1):
                    pe_square(pe, S_POOLP, SUMS, 2, m)
        for m in (KD - 2, KD - 1):
            pe_square(pe, S_POOLP, SUMS, 2, m)

    def act_pool(act):
        n = PHASE["pool"]

        def evacuate(g):
            act.wait_ge(unit_summed, n + g + 1)
            for m in (2 * g, 2 * g + 1):
                ins = nc.scalar.activation(two(M[:, m, :]), psv(m % 3, 2), ACT.Identity, scale=column("pool_scale_2", 0, m))
                if m % 2:
                    ins.then_inc(unit_read, 1)
                else:
                    pool_evac.inc(ins, m)

        def squares(g):
            evacuate(g)
            for m in (2 * g, 2 * g + 1):
                pool_out(act, m)
                act_square(act, S_POOLP, m, m, M[:, m, :], S2)

        for g in range(4):
            pool_mixed.wait(act, g)
            for k in range(2):
                nc.scalar.activation(hi(2 * g + k, 2), mixed[:, 2 * g + k, :], ACT.Copy).then_inc(x_hi, 1)
            if g:
                squares(g - 1)
                hi_to(act, n + g + 1)
        squares(3)
        hi_to(act, n + 5)

    def window_sums(add, a, dst, win):
        src, span, turn = a, 1, 0
        while span < win:
            to, lo_ = dst[turn], 2 * span - 1
            add(to[:, :, lo_:], src[:, :, lo_:], src[:, :, lo_ - span:S2 + 16 - span])
            src, span, turn = to, 2 * span, 1 - turn
        return src

    POOL_GROUPS = (2, 3)
    WIDE_TO = {2: (pd[:, 2, :, :], pd[:, 0, :, :]), 3: (pd[:, 0, :, :], pd[:, 1, :, :])}
    WIDE_SUM = {2: pd[:, 2, :, :], 3: pd[:, 1, :, :]}

    def group_in(g):
        return pa[:, 2 * g:2 * g + 2, :]

    def pool_windows(pool):
        steps = [0]

        def add(to, a, b):
            if steps[0]:
                pool.wait_ge(pool_step, steps[0])
            steps[0] += 1
            nc.gpsimd.tensor_tensor(to, a, b, ALU.add).then_inc(pool_step, 1)

        for i, g in enumerate(POOL_GROUPS):
            pool.wait_ge(pool_in, i + 1)
            window_sums(add, group_in(g), WIDE_TO[g], WINDOWS[g])

    def dve_pool(dve, link):
        n = PHASE["pool"]
        link(nc.vector.memset(pa[:, :, 0:16], 0.0))
        dve_norm(dve, link, S_POOL, SUMS, 2)

        def normed(k):
            return nc.vector.scalar_tensor_tensor(pa[:, k, 16:], X[:, k, :], G_PRE[1](k), rn[:, 0:S2], ALU.mult, ALU.mult)

        def split(g):
            for k in (2 * g, 2 * g + 1):
                dve.wait_ge(x_hi, KD * D_POOL + k + 1)
                nc.vector.tensor_tensor(lo(k, 2), mixed[:, k, :], hi(k, 2).bitcast(F32), ALU.subtract).then_inc(x_lo, 1)

        for g in POOL_GROUPS:
            link(normed(2 * g))
            normed(2 * g + 1).then_inc(pool_in, 1)
        sums = 0
        for g, win in enumerate(WINDOWS):
            if g in POOL_GROUPS:
                sums += win.bit_length() - 1
                if g == 3:
                    split(2)
                dve.wait_ge(pool_step, sums)
                src = WIDE_SUM[g]
            else:
                link(normed(2 * g))
                link(normed(2 * g + 1))
                if g:
                    split(g - 1)
                src = window_sums(lambda to, a, b: link(nc.vector.tensor_tensor(to, a, b, ALU.add)), group_in(g), (pb, pc), win)
            cor = const[:, C_COR + 16 * g:C_COR + 16 * (g + 1)]
            for k in range(2):
                link(nc.vector.tensor_tensor(src[:, k, 16:32], src[:, k, 16:32], cor, ALU.mult))
            pool_mixed.inc(nc.vector.scalar_tensor_tensor(mixed[:, 2 * g:2 * g + 2, :], src[:, :, 16:], 1.0 / win,
                                                          group_in(g)[:, :, 16:], ALU.mult, ALU.subtract), g)
            pool_mixed.wait(dve, g)
            if g == 2:
                split(1)
        split(3)

    @block.sync
    def _(sp):
        front = C_ONE + P
        sp.dma_start(const[:, 0:front], A["const"][:, 0:front]).then_inc(const_in, 16)
        for t in range(S1 // P):
            sp.dma_start(x_in[:, t, :], A["x"][0, t * P:(t + 1) * P, :]).then_inc(x_loaded, 16)

        def step(sp, n, it, u):
            sp_unit(sp, n, it, u)
            if static(it) and n == RAW - 1:
                for to, v in ROW_LOADS[ACT_ROWS:]:
                    sp.dma_start(to, v).then_inc(rows_in, 16)
                sp.dma_start(const[:, front:], A["const"][:, front:]).then_inc(rest_in, 16)

        for _ in walk(sp, step):
            pass
        for i, t in enumerate(OUT_ORDER):
            sp.wait_ge(out_ready, i + 1)
            sp.dma_start(out[0, t * P:(t + 1) * P, :], out_tok[:, t, :]).then_inc(out_done, 16)
        sp.wait_ge(out_done, 16 * (S1 // P))

    @block.gpsimd
    def _(pool):
        after = {PHASE[name] + 1: i for i, name in enumerate(("cffn0", "pool", "cffn1"))}

        def step(pool, n, it, u):
            pool_unit(pool, n, it, u)
            if static(it) and n in after:
                pool_post(pool, after[n])
                if n == PHASE["pool"] + 1:
                    pool_windows(pool)

        for _ in walk(pool, step):
            pass

    @block.scalar
    def _(act):
        act_start(act)
        act_ffn(act, "ffn1", 1, 0, S_FFN1, lambda m, j: (act_split(act, D_MIX, m, j, 1, G_MIX),
                                                         act_square(act, S_MIX, m, j, xt(m, 1), S1)))
        act_mixer(act)
        act_xat(act)
        act_ffn(act, "ffn2", 1, 1, S_FFN2, lambda m, j: act_square(act, S_FIN, m, j, xt(m, 1), S1))
        act_fin(act)
        act_mla(act)
        act_post(act, 0, S_MLAP, S_CF0, D_CF0, G_FPRE[0])
        act_ffn(act, "cffn0", 2, 2, S_CF0, lambda m, j: act_square(act, S_CF0P, m, j, M[:, m, :], S2))
        act_post(act, 1, S_CF0P, S_POOL)
        act_sqrt(act, S_POOL, S2)
        act_pool(act)
        act_post(act, 2, S_POOLP, S_CF1, D_CF1, G_FPRE[1], 3)
        act_ffn(act, "cffn1", 3, 3, S_CF1, lambda m, j: (act_square(act, S_CF1P, m, j, M[:, m, 0:S3], S3),
                                                            act_diag(act, m, G_FPOST[1])))
        act_out(act)

    @block.tensor
    def _(pe):
        pe_start(pe)
        pe_ffn(pe, "ffn1", 1, 0, S_FFN1, D_FFN1)
        pe_mixer(pe)
        pe_xat(pe)
        pe_ffn(pe, "ffn2", 1, 1, S_FFN2, D_FFN2)
        pe_fin(pe)
        pe_mla(pe)
        pe_post(pe, S_MLAP, PHASE["mla"] + 26)
        pe_ffn(pe, "cffn0", 2, 2, S_CF0, D_CF0)
        pe_post(pe, S_CF0P, PHASE["cffn0"] + 68)
        pe_pool(pe)
        pe_ffn(pe, "cffn1", 3, 3, S_CF1, D_CF1)
        pe_out(pe, S_CF1P, PHASE["cffn1"] + 68)

    @block.vector
    def _(dve):
        link = step_link(dve, dve_step)
        dve_start(dve)
        dve_ffn(dve, link, "ffn1", 1, 0, S_FFN1, lambda m, j: (dve_split(dve, D_MIX, m, 1, G_MIX),
                                                               dve_acc(dve, S_MIX, m, j, S1)))
        dve_mixer(dve, link)
        dve_xat(dve, link)
        dve_ffn(dve, link, "ffn2", 1, 1, S_FFN2, lambda m, j: dve_acc(dve, S_FIN, m, j, S1))
        dve_fin(dve, link)
        dve_mla(dve, link)
        dve_post(dve, link, 0, S_MLAP, PHASE["mla"] + 26, G_POST[0], D_CF0, G_FPRE[0])
        dve_ffn(dve, link, "cffn0", 2, 2, S_CF0, lambda m, j: dve_acc(dve, S_CF0P, m, j, S2))
        dve_post(dve, link, 1, S_CF0P, PHASE["cffn0"] + 68, G_FPOST[0])
        dve_pool(dve, link)
        dve_post(dve, link, 2, S_POOLP, 3, G_POST[1], D_CF1, G_FPRE[1], 3)
        dve_ffn(dve, link, "cffn1", 3, 3, S_CF1, lambda m, j: dve_acc(dve, S_CF1P, m, j, S3))
        dve_out(dve, link)


INPUTS = ("x", "mem", "ffn1_norm", "ffn1_w_gate", "ffn1_w_up", "ffn1_w_down", "mix_norm", "w_in", "gate_fwd_w", "gate_fwd_b",
          "gate_bwd_w", "gate_bwd_b", "gla_norm", "conv_w", "conv_b", "w_out", "xattn_norm", "mem_norm", "xattn_w_q",
          "xattn_w_kv", "xattn_w_o", "ffn2_norm", "ffn2_w_gate", "ffn2_w_up", "ffn2_w_down", "final_norm", "meta_tokens_2",
          "norm_mix_pre_2", "norm_mix_post_2", "norm_ffn_pre_2", "norm_ffn_post_2", "mla_w_dqkv_2", "mla_q_norm_2", "mla_w_uq_2",
          "mla_kv_norm_2", "mla_w_ukv_2", "mla_w_o_2", "pool_w_group_2", "pool_scale_2", "ffn_w_up_2", "ffn_conv_w_2",
          "ffn_conv_b_2", "ffn_w_down_2")


def kernel(**inputs):
    import concourse.bacc as bacc
    from concourse.bass_utils import run_bass_kernel_spmd

    nc = bacc.Bacc("TRN2", target_bir_lowering=False, num_devices=1)
    arrays, views = {}, {}
    for name in INPUTS + ("const",):
        a = constant_tile() if name == "const" else np.ascontiguousarray(inputs[name])
        arrays["in_" + name] = a
        views[name] = nc.dram_tensor("in_" + name, a.shape, mybir.dt.from_np(a.dtype), kind="ExternalInput").ap()
    out = nc.dram_tensor("out_0", (1, S1, D), F32, kind="ExternalOutput").ap()
    build(nc, views, out)
    r = run_bass_kernel_spmd(nc, [arrays], core_ids=[0])
    return r.results[0]["out_0"]
```
